# Optimizing a Trainium2 kernel written in Bass

```python
import math
import jax, jax.numpy as jnp
from jax import lax
import numpy as np
import jax
import jax.numpy as jnp

D_MODEL = 1024
BATCH = 1
SEQ = 512
DEPTH = 1

HEAD_DIM = 64
N_DIFF_HEADS = 4
DIFF_V_DIM = 2 * HEAD_DIM
N_SB_HEADS = 8
DIFF_QK_WIDTH = N_DIFF_HEADS * 2 * HEAD_DIM
DIFF_V_WIDTH = N_DIFF_HEADS * DIFF_V_DIM
SB_WIDTH = N_SB_HEADS * HEAD_DIM
MIX_WIDTH = DIFF_V_WIDTH + SB_WIDTH
QKV_WIDTH = 2 * DIFF_QK_WIDTH + DIFF_V_WIDTH + 3 * SB_WIDTH
QKV_SPLITS = (DIFF_QK_WIDTH, 2 * DIFF_QK_WIDTH, 2 * DIFF_QK_WIDTH + DIFF_V_WIDTH,
              2 * DIFF_QK_WIDTH + DIFF_V_WIDTH + SB_WIDTH,
              2 * DIFF_QK_WIDTH + DIFF_V_WIDTH + 2 * SB_WIDTH)
D_FF = 2816
CONV_WIDTH = 3
N_BUCKETS = 32
MAX_DISTANCE = 128
Q_BLOCK = 128
RMS_EPS = 1e-6


def _rmsnorm(x, g):
    xf = x.astype(jnp.float32)
    y = xf * lax.rsqrt(jnp.mean(xf * xf, axis=-1, keepdims=True) + RMS_EPS)
    return (y * g.astype(jnp.float32)).astype(x.dtype)

def _lambda_init(layer):
    return 0.8 - 0.6 * math.exp(-0.3 * layer)

def _relative_bucket(rel):
    n = jnp.maximum(rel, 0)
    max_exact = N_BUCKETS // 2
    nf = jnp.maximum(n, 1).astype(jnp.float32)
    large = max_exact + (jnp.log(nf / max_exact) / math.log(MAX_DISTANCE / max_exact)
                         * (N_BUCKETS - max_exact)).astype(jnp.int32)
    large = jnp.minimum(large, N_BUCKETS - 1)
    return jnp.where(n < max_exact, n, large)

def _diff_attention(q, k, v, lam, rel_bias):
    B, H, _, S, d = q.shape
    nb = S // Q_BLOCK
    qb = q.reshape(B, H, 2, nb, Q_BLOCK, d).transpose(3, 0, 1, 2, 4, 5)
    starts = jnp.arange(nb, dtype=jnp.int32) * Q_BLOCK
    k_pos = jnp.arange(S, dtype=jnp.int32)
    scale = d ** -0.5
    table = rel_bias.astype(jnp.float32)

    def one_block(args):
        q_blk, t0 = args
        rel = (t0 + jnp.arange(Q_BLOCK, dtype=jnp.int32))[:, None] - k_pos[None, :]
        bias = jnp.transpose(table[_relative_bucket(rel)], (2, 0, 1))
        logits = jnp.einsum('bhmqd,bhmkd->bhmqk', q_blk, k).astype(jnp.float32) * scale
        logits = logits + bias[None, :, None]
        logits = jnp.where(rel >= 0, logits, -jnp.inf)
        p = jax.nn.softmax(logits, axis=-1)
        w = p[:, :, 0] - lam * p[:, :, 1]
        return jnp.einsum('bhqk,bhkd->bhqd', w.astype(v.dtype), v)

    out = lax.map(one_block, (qb, starts))
    return out.transpose(1, 2, 0, 3, 4).reshape(B, H, S, v.shape[-1])

def _stick_breaking_attention(q, k, v):
    B, H, S, d = q.shape
    nb = S // Q_BLOCK
    qb = q.reshape(B, H, nb, Q_BLOCK, d).transpose(2, 0, 1, 3, 4)
    starts = jnp.arange(nb, dtype=jnp.int32) * Q_BLOCK
    k_pos = jnp.arange(S, dtype=jnp.int32)
    scale = d ** -0.5

    def one_block(args):
        q_blk, t0 = args
        rel = (t0 + jnp.arange(Q_BLOCK, dtype=jnp.int32))[:, None] - k_pos[None, :]
        strict = rel > 0
        z = jnp.einsum('bhqd,bhkd->bhqk', q_blk, k).astype(jnp.float32) * scale
        log_beta = jax.nn.log_sigmoid(z)
        log_1mb = jnp.where(strict, jax.nn.log_sigmoid(-z), 0.0)
        between = lax.cumsum(log_1mb, axis=3, reverse=True) - log_1mb
        a = jnp.where(strict, jnp.exp(log_beta + between), 0.0)
        return jnp.einsum('bhqk,bhkd->bhqd', a.astype(v.dtype), v)

    out = lax.map(one_block, (qb, starts))
    return out.transpose(1, 2, 0, 3, 4).reshape(B, H, S, d)

def _causal_depthwise_conv(u, w, b):
    S = u.shape[1]
    up = jnp.pad(u, ((0, 0), (CONV_WIDTH - 1, 0), (0, 0)))
    y = b
    for i in range(CONV_WIDTH):
        y = y + up[:, i:i + S] * w[i]
    return y

def first_inputs(seed: int = 0) -> dict:
    key = jax.random.key(seed)
    ks = jax.random.split(key, 18)

    def nrm(k, shape, scale):
        return jax.random.normal(k, shape, jnp.float32) * scale

    def gain(k, shape):
        return 1.0 + 0.05 * jax.random.normal(k, shape, jnp.float32)

    return {
        'x': nrm(ks[0], (BATCH, SEQ, D_MODEL), 1.0),
        'attn_pre_norm': gain(ks[1], (DEPTH, D_MODEL)),
        'w_qkv': nrm(ks[2], (DEPTH, D_MODEL, QKV_WIDTH), D_MODEL ** -0.5),
        'lambda_q1': nrm(ks[3], (DEPTH, HEAD_DIM), 0.1),
        'lambda_k1': nrm(ks[4], (DEPTH, HEAD_DIM), 0.1),
        'lambda_q2': nrm(ks[5], (DEPTH, HEAD_DIM), 0.1),
        'lambda_k2': nrm(ks[6], (DEPTH, HEAD_DIM), 0.1),
        'diff_subln': gain(ks[7], (DEPTH, DIFF_V_DIM)),
        'sb_norm': gain(ks[8], (DEPTH, HEAD_DIM)),
        'rel_bias': nrm(ks[9], (N_BUCKETS, N_DIFF_HEADS), 0.5),
        'w_o': nrm(ks[10], (DEPTH, MIX_WIDTH, D_MODEL), MIX_WIDTH ** -0.5),
        'attn_post_norm': gain(ks[11], (DEPTH, D_MODEL)),
        'ffn_pre_norm': gain(ks[12], (DEPTH, D_MODEL)),
        'w_up': nrm(ks[13], (DEPTH, D_MODEL, 2 * D_FF), D_MODEL ** -0.5),
        'conv_w': nrm(ks[14], (DEPTH, CONV_WIDTH, 2 * D_FF), CONV_WIDTH ** -0.5),
        'conv_b': nrm(ks[15], (DEPTH, 2 * D_FF), 0.01),
        'w_down': nrm(ks[16], (DEPTH, D_FF, D_MODEL), D_FF ** -0.5),
        'ffn_post_norm': gain(ks[17], (DEPTH, D_MODEL)),
    }

def first_block(x, attn_pre_norm, w_qkv, lambda_q1, lambda_k1, lambda_q2, lambda_k2,
              diff_subln, sb_norm, rel_bias, w_o, attn_post_norm, ffn_pre_norm,
              w_up, conv_w, conv_b, w_down, ffn_post_norm):
    B, S, _ = x.shape
    for l in range(DEPTH):
        lam_init = _lambda_init(l)
        h = _rmsnorm(x, attn_pre_norm[l])
        qkv = h @ w_qkv[l]
        dq, dk, dv, sq, sk, sv = jnp.split(qkv, QKV_SPLITS, axis=-1)
        dq = dq.reshape(B, S, N_DIFF_HEADS, 2, HEAD_DIM).transpose(0, 2, 3, 1, 4)
        dk = dk.reshape(B, S, N_DIFF_HEADS, 2, HEAD_DIM).transpose(0, 2, 3, 1, 4)
        dv = dv.reshape(B, S, N_DIFF_HEADS, DIFF_V_DIM).transpose(0, 2, 1, 3)
        lam = (jnp.exp(jnp.sum(lambda_q1[l].astype(jnp.float32) * lambda_k1[l].astype(jnp.float32)))
               - jnp.exp(jnp.sum(lambda_q2[l].astype(jnp.float32) * lambda_k2[l].astype(jnp.float32)))
               + lam_init)
        diff_o = _diff_attention(dq, dk, dv, lam, rel_bias)
        diff_o = _rmsnorm(diff_o, diff_subln[l]) * (1.0 - lam_init)
        diff_o = diff_o.transpose(0, 2, 1, 3).reshape(B, S, DIFF_V_WIDTH)

        sq = sq.reshape(B, S, N_SB_HEADS, HEAD_DIM).transpose(0, 2, 1, 3)
        sk = sk.reshape(B, S, N_SB_HEADS, HEAD_DIM).transpose(0, 2, 1, 3)
        sv = sv.reshape(B, S, N_SB_HEADS, HEAD_DIM).transpose(0, 2, 1, 3)
        sb_o = _rmsnorm(_stick_breaking_attention(sq, sk, sv), sb_norm[l])
        sb_o = sb_o.transpose(0, 2, 1, 3).reshape(B, S, SB_WIDTH)

        mix = jnp.concatenate([diff_o, sb_o], axis=-1) @ w_o[l]
        x = x + _rmsnorm(mix, attn_post_norm[l])

        h = _rmsnorm(x, ffn_pre_norm[l])
        u = _causal_depthwise_conv(h @ w_up[l], conv_w[l], conv_b[l])
        gate, val = jnp.split(u, 2, axis=-1)
        y = (jax.nn.gelu(gate, approximate=True) * val) @ w_down[l]
        x = x + _rmsnorm(y, ffn_post_norm[l])
    return x


MIX_WIDTH_2 = D_MODEL
NSA_HEADS = MIX_WIDTH_2 // 2 // HEAD_DIM
NSA_KV_HEADS = 2
SWA_HEADS = MIX_WIDTH_2 // 2 // HEAD_DIM
SWA_KV_HEADS = 2
CMP_BLOCK = 32
CMP_STRIDE = 16
CMP_HIDDEN = 256
SEL_BLOCK = 64
SEL_TOPK = 16
SEL_Q_CHUNK = 64
NSA_WINDOW = 512
SWA_WINDOW = 128
BAND_BLOCK = 128
N_NSA_BRANCHES = 3
NORM_EPS = 1e-6
NEG_INF = -1e30
FORCE_SCORE = 1e9
ATTN_SCALE = HEAD_DIM ** -0.5
PROJ_SPLITS = (NSA_HEADS * HEAD_DIM, 2 * N_NSA_BRANCHES * NSA_KV_HEADS * HEAD_DIM, N_NSA_BRANCHES * NSA_HEADS, SWA_HEADS * HEAD_DIM, 2 * SWA_KV_HEADS * HEAD_DIM)
PROJ_WIDTH = sum(PROJ_SPLITS)


def alibi_slopes(n_heads, n_groups):
    slopes = 2.0 ** (-8.0 * np.arange(1, n_heads + 1) / n_heads)
    return jnp.asarray(slopes.reshape(n_groups, n_heads // n_groups), jnp.float32)

def rmsnorm(x, g):
    xf = x.astype(jnp.float32)
    y = xf * lax.rsqrt(jnp.mean(xf * xf, axis=-1, keepdims=True) + NORM_EPS)
    return (y * g.astype(jnp.float32)).astype(x.dtype)

def swiglu(x, w_in, w_out):
    gate, up = jnp.split(x @ w_in, 2, axis=-1)
    return (jax.nn.silu(gate) * up) @ w_out

def banded_attention(q, k, v, slopes, window, sinks=None):
    B, T, G, R, D = q.shape
    nb = T // BAND_BLOCK
    n_prev = -(-(window - 1) // BAND_BLOCK)
    pad = n_prev * BAND_BLOCK
    kw_len = (n_prev + 1) * BAND_BLOCK
    kp = jnp.pad(k, ((0, 0), (pad, 0), (0, 0), (0, 0))).reshape(B, nb + n_prev, BAND_BLOCK, G, D)
    vp = jnp.pad(v, ((0, 0), (pad, 0), (0, 0), (0, 0))).reshape(B, nb + n_prev, BAND_BLOCK, G, D)
    kw = jnp.concatenate([kp[:, j:j + nb] for j in range(n_prev + 1)], axis=2)
    vw = jnp.concatenate([vp[:, j:j + nb] for j in range(n_prev + 1)], axis=2)
    qb = q.reshape(B, nb, BAND_BLOCK, G, R, D)
    s = jnp.einsum('bnqgrd,bnkgd->bngrqk', qb, kw) * ATTN_SCALE
    t_pos = np.arange(nb)[:, None] * BAND_BLOCK + np.arange(BAND_BLOCK)[None, :]
    s_pos = np.arange(nb)[:, None] * BAND_BLOCK - pad + np.arange(kw_len)[None, :]
    dist = t_pos[:, :, None] - s_pos[:, None, :]
    mask = jnp.asarray((dist >= 0) & (dist < window) & (s_pos[:, None, :] >= 0))
    bias = -slopes[None, :, :, None, None] * jnp.asarray(dist, jnp.float32)[:, None, None]
    s = jnp.where(mask[:, None, None], s + bias, NEG_INF)
    if sinks is not None:
        sink = jnp.broadcast_to(sinks[None, None, :, :, None, None], s.shape[:-1] + (1,))
        p = jax.nn.softmax(jnp.concatenate([s, sink], axis=-1), axis=-1)[..., :-1]
    else:
        p = jax.nn.softmax(s, axis=-1)
    o = jnp.einsum('bngrqk,bnkgd->bnqgrd', p, vw)
    return o.reshape(B, T, G, R, D)

def compress_blocks(kr, pos, w1, b1, w2):
    B, T, G, D = kr.shape
    nc = (T - CMP_BLOCK) // CMP_STRIDE + 1
    idx = np.arange(nc)[:, None] * CMP_STRIDE + np.arange(CMP_BLOCK)[None, :]
    blk = kr[:, idx] + pos[None, None, :, None, :]
    flat = blk.transpose(0, 1, 3, 2, 4).reshape(B, nc, G, CMP_BLOCK * D)
    return jax.nn.gelu(flat @ w1 + b1) @ w2

def selected_attention(q, k, v, sel_idx, slopes):
    B, T, G, R, D = q.shape
    ns = T // SEL_BLOCK
    n_sel = sel_idx.shape[-1]
    nq = T // SEL_Q_CHUNK
    kb = k.reshape(B, ns, SEL_BLOCK, G, D).transpose(0, 3, 1, 2, 4)
    vb = v.reshape(B, ns, SEL_BLOCK, G, D).transpose(0, 3, 1, 2, 4)
    qc = q.reshape(B, nq, SEL_Q_CHUNK, G, R, D).transpose(1, 0, 2, 3, 4, 5)
    ic = sel_idx.reshape(B, nq, SEL_Q_CHUNK, G, n_sel).transpose(1, 0, 2, 3, 4)
    tc = jnp.arange(T).reshape(nq, SEL_Q_CHUNK)
    b_ix = jnp.arange(B)[:, None, None, None]
    g_ix = jnp.arange(G)[None, None, :, None]

    def chunk(args):
        qx, ix, tx = args
        kg = kb[b_ix, g_ix, ix]
        vg = vb[b_ix, g_ix, ix]
        s = jnp.einsum('bcgrd,bcgkld->bcgrkl', qx, kg) * ATTN_SCALE
        spos = ix[..., None] * SEL_BLOCK + jnp.arange(SEL_BLOCK)
        dist = tx[None, :, None, None, None] - spos
        mask = (dist >= 0)[:, :, :, None]
        bias = -slopes[None, None, :, :, None, None] * dist.astype(jnp.float32)[:, :, :, None]
        s = jnp.where(mask, s + bias, NEG_INF)
        C = qx.shape[1]
        p = jax.nn.softmax(s.reshape(B, C, G, R, n_sel * SEL_BLOCK), axis=-1).reshape(s.shape)
        return jnp.einsum('bcgrkl,bcgkld->bcgrd', p, vg)

    o = lax.map(chunk, (qc, ic, tc))
    return o.transpose(1, 0, 2, 3, 4, 5).reshape(B, T, G, R, D)

def nsa_group(q, kc_raw, vc_raw, ks, vs, kw, vw, gate_logits, ck_pos, ck_w1, ck_b1, ck_w2, cv_pos, cv_w1, cv_b1, cv_w2, slopes):
    B, T, G, R, D = q.shape
    kc = compress_blocks(kc_raw, ck_pos, ck_w1, ck_b1, ck_w2).astype(jnp.float32)
    vc = compress_blocks(vc_raw, cv_pos, cv_w1, cv_b1, cv_w2).astype(jnp.float32)
    nc = kc.shape[1]
    blk_end = np.arange(nc) * CMP_STRIDE + CMP_BLOCK - 1
    dist_c = np.arange(T)[:, None] - blk_end[None, :]
    mask_c = jnp.asarray(dist_c >= 0)
    s = jnp.einsum('btgrd,bcgd->bgrtc', q, kc) * ATTN_SCALE
    s = jnp.where(mask_c, s - slopes[:, :, None, None] * jnp.asarray(dist_c, jnp.float32), NEG_INF)
    p_cmp = jnp.where(mask_c, jax.nn.softmax(s, axis=-1), 0.0)
    o_cmp = jnp.einsum('bgrtc,bcgd->btgrd', p_cmp, vc)
    ns = T // SEL_BLOCK
    c_start = np.arange(nc) * CMP_STRIDE
    s_start = np.arange(ns) * SEL_BLOCK
    overlap = np.clip(np.minimum(c_start[:, None] + CMP_BLOCK, s_start[None, :] + SEL_BLOCK) - np.maximum(c_start[:, None], s_start[None, :]), 0, None) / CMP_BLOCK
    p_slc = jnp.einsum('bgrtc,cs->btgs', p_cmp, jnp.asarray(overlap, jnp.float32))
    cur = np.arange(T) // SEL_BLOCK
    blk = np.arange(ns)
    valid = jnp.asarray(blk[None, :] <= cur[:, None])[None, :, None, :]
    forced = jnp.asarray((blk[None, :] == 0) | (blk[None, :] == cur[:, None]) | (blk[None, :] == cur[:, None] - 1))[None, :, None, :]
    score = jnp.where(forced, FORCE_SCORE, jnp.where(valid, p_slc, NEG_INF))
    _, sel_idx = lax.top_k(score, min(SEL_TOPK, ns))
    o_slc = selected_attention(q, ks, vs, sel_idx, slopes)
    o_win = banded_attention(q, kw, vw, slopes, NSA_WINDOW)
    g = jax.nn.sigmoid(gate_logits)
    return g[..., 0:1] * o_cmp + g[..., 1:2] * o_slc + g[..., 2:3] * o_win

def hybrid_mixer(xn, w_in, ck_pos, ck_w1, ck_b1, ck_w2, cv_pos, cv_w1, cv_b1, cv_w2, sinks, w_out):
    B, T, _ = xn.shape
    D = HEAD_DIM
    ga, ra = NSA_KV_HEADS, NSA_HEADS // NSA_KV_HEADS
    gb, rb = SWA_KV_HEADS, SWA_HEADS // SWA_KV_HEADS
    proj = (xn @ w_in).astype(jnp.float32)
    offsets = [int(o) for o in np.cumsum(PROJ_SPLITS)[:-1]]
    q_a, kv_a, gate_a, q_b, kv_b = jnp.split(proj, offsets, axis=-1)
    q_a = q_a.reshape(B, T, ga, ra, D)
    kc_raw, vc_raw, ks, vs, kw, vw = [t.reshape(B, T, ga, D) for t in jnp.split(kv_a, 2 * N_NSA_BRANCHES, axis=-1)]
    gate_a = gate_a.reshape(B, T, ga, ra, N_NSA_BRANCHES)
    o_a = nsa_group(q_a, kc_raw, vc_raw, ks, vs, kw, vw, gate_a, ck_pos, ck_w1, ck_b1, ck_w2, cv_pos, cv_w1, cv_b1, cv_w2, alibi_slopes(NSA_HEADS, NSA_KV_HEADS))
    q_b = q_b.reshape(B, T, gb, rb, D)
    k_b, v_b = [t.reshape(B, T, gb, D) for t in jnp.split(kv_b, 2, axis=-1)]
    o_b = banded_attention(q_b, k_b, v_b, alibi_slopes(SWA_HEADS, SWA_KV_HEADS), SWA_WINDOW, sinks.astype(jnp.float32).reshape(gb, rb))
    o = jnp.concatenate([o_a.reshape(B, T, NSA_HEADS * D), o_b.reshape(B, T, SWA_HEADS * D)], axis=-1)
    return o.astype(xn.dtype) @ w_out

def second_inputs(seed: int = 0) -> dict:
    key = jax.random.key(seed)
    ks = jax.random.split(key, 24)
    L = DEPTH

    def nrm(k, shape, fan_in):
        return jax.random.normal(k, shape, jnp.float32) * fan_in ** -0.5

    def gain(k, shape):
        return 1.0 + 0.1 * jax.random.normal(k, shape, jnp.float32)

    return {
        'x': jax.random.normal(ks[0], (BATCH, SEQ, D_MODEL), jnp.float32),
        'ffn1_norm': gain(ks[1], (L, D_MODEL)),
        'ffn1_w_in': nrm(ks[2], (L, D_MODEL, 2 * D_FF), D_MODEL),
        'ffn1_w_out': nrm(ks[3], (L, D_FF, D_MODEL), D_FF),
        'mix_norm': gain(ks[4], (L, D_MODEL)),
        'w_mix_in': nrm(ks[5], (L, D_MODEL, PROJ_WIDTH), D_MODEL),
        'cmp_k_pos': 0.5 * jax.random.normal(ks[6], (L, CMP_BLOCK, HEAD_DIM), jnp.float32),
        'cmp_k_w1': nrm(ks[7], (L, CMP_BLOCK * HEAD_DIM, CMP_HIDDEN), CMP_BLOCK * HEAD_DIM),
        'cmp_k_b1': 0.02 * jax.random.normal(ks[8], (L, CMP_HIDDEN), jnp.float32),
        'cmp_k_w2': nrm(ks[9], (L, CMP_HIDDEN, HEAD_DIM), CMP_HIDDEN),
        'cmp_v_pos': 0.5 * jax.random.normal(ks[10], (L, CMP_BLOCK, HEAD_DIM), jnp.float32),
        'cmp_v_w1': nrm(ks[11], (L, CMP_BLOCK * HEAD_DIM, CMP_HIDDEN), CMP_BLOCK * HEAD_DIM),
        'cmp_v_b1': 0.02 * jax.random.normal(ks[12], (L, CMP_HIDDEN), jnp.float32),
        'cmp_v_w2': nrm(ks[13], (L, CMP_HIDDEN, HEAD_DIM), CMP_HIDDEN),
        'swa_sinks': 0.5 * jax.random.normal(ks[14], (L, SWA_HEADS), jnp.float32),
        'w_mix_out': nrm(ks[15], (L, MIX_WIDTH_2, D_MODEL), MIX_WIDTH_2),
        'ffn2_norm': gain(ks[16], (L, D_MODEL)),
        'ffn2_w_in': nrm(ks[17], (L, D_MODEL, 2 * D_FF), D_MODEL),
        'ffn2_w_out': nrm(ks[18], (L, D_FF, D_MODEL), D_FF),
        'final_norm': gain(ks[19], (D_MODEL,)),
    }

def second_block(x, ffn1_norm, ffn1_w_in, ffn1_w_out, mix_norm, w_mix_in, cmp_k_pos, cmp_k_w1, cmp_k_b1, cmp_k_w2, cmp_v_pos, cmp_v_w1, cmp_v_b1, cmp_v_w2, swa_sinks, w_mix_out, ffn2_norm, ffn2_w_in, ffn2_w_out, final_norm):
    h = x
    for l in range(DEPTH):
        h = h + 0.5 * swiglu(rmsnorm(h, ffn1_norm[l]), ffn1_w_in[l], ffn1_w_out[l])
        h = h + hybrid_mixer(rmsnorm(h, mix_norm[l]), w_mix_in[l], cmp_k_pos[l], cmp_k_w1[l], cmp_k_b1[l], cmp_k_w2[l], cmp_v_pos[l], cmp_v_w1[l], cmp_v_b1[l], cmp_v_w2[l], swa_sinks[l], w_mix_out[l])
        h = h + 0.5 * swiglu(rmsnorm(h, ffn2_norm[l]), ffn2_w_in[l], ffn2_w_out[l])
    return rmsnorm(h, final_norm)


def setup_inputs(seed=0):
    out = dict(first_inputs(seed))
    for name, value in second_inputs(seed + 1).items():
        if name != "x":
            out[name + "_2"] = value
    return out


def reference(
    x, attn_pre_norm, w_qkv, lambda_q1, lambda_k1, lambda_q2, lambda_k2, diff_subln, sb_norm,
    rel_bias, w_o, attn_post_norm, ffn_pre_norm, w_up, conv_w, conv_b, w_down, ffn_post_norm,
    ffn1_norm_2, ffn1_w_in_2, ffn1_w_out_2, mix_norm_2, w_mix_in_2, cmp_k_pos_2, cmp_k_w1_2,
    cmp_k_b1_2, cmp_k_w2_2, cmp_v_pos_2, cmp_v_w1_2, cmp_v_b1_2, cmp_v_w2_2, swa_sinks_2,
    w_mix_out_2, ffn2_norm_2, ffn2_w_in_2, ffn2_w_out_2, final_norm_2,
):
    x = first_block(
        x, attn_pre_norm, w_qkv, lambda_q1, lambda_k1, lambda_q2, lambda_k2, diff_subln,
        sb_norm, rel_bias, w_o, attn_post_norm, ffn_pre_norm, w_up, conv_w, conv_b, w_down,
        ffn_post_norm,
    )
    return second_block(
        x, ffn1_norm_2, ffn1_w_in_2, ffn1_w_out_2, mix_norm_2, w_mix_in_2, cmp_k_pos_2,
        cmp_k_w1_2, cmp_k_b1_2, cmp_k_w2_2, cmp_v_pos_2, cmp_v_w1_2, cmp_v_b1_2, cmp_v_w2_2,
        swa_sinks_2, w_mix_out_2, ffn2_norm_2, ffn2_w_in_2, ffn2_w_out_2, final_norm_2,
    )


_drawn_inputs = setup_inputs


def setup_inputs(seed=0):
    import zlib

    import numpy as np

    out = dict(_drawn_inputs(seed))
    spreads = {}
    factors = {'lambda_q1': 3.721,
     'lambda_k1': 2.7,
     'lambda_q2': 64.0,
     'conv_b': 6.533,
     'cmp_k_pos_2': 27.021,
     'cmp_k_b1_2': 64.0,
     'cmp_v_b1_2': 21.551,
     'swa_sinks_2': 6.992}
    for name, (base, spread) in spreads.items():
        noise = np.random.default_rng([zlib.crc32(name.encode()), seed]).standard_normal(out[name].shape)
        drawn = base * np.exp(spread * noise) if base else spread * noise
        out[name] = jnp.asarray(drawn.astype(out[name].dtype))
    for name, factor in factors.items():
        out[name] = (out[name] * factor).astype(out[name].dtype)
    return out
```

```python
from contextlib import ExitStack
import math

import numpy as np

import concourse.bass as bass
from concourse import mybir

F32 = mybir.dt.float32
F32R = mybir.dt.float32r
I32 = mybir.dt.int32
ALU = mybir.AluOpType
ACT = mybir.ActivationFunctionType
AX_X = mybir.AxisListType.X

P = 128
T = 512
TB = T // P
D = 1024
KC = D // P
HD = 64
FF = 2816
FC = FF // P
UNIT = 1024
RING = 4
EPS = 1e-6
LAM_INIT = 0.8 - 0.6 * math.exp(-0.3 * 0)
SCALE = HD ** -0.5
MASKED = -1e30
FAR = 1e33
N_BUCKETS, MAX_DISTANCE = 32, 128
N_DIFF, N_SB, N_NSA, N_SWA = 4, 8, 8, 8
CMP_BLOCK, CMP_STRIDE, CMP_HID = 32, 16, 256
NCMP = (T - CMP_BLOCK) // CMP_STRIDE + 1
SWA_WINDOW = 128
LINE = T + P
NAT2 = 3 * P + 3 * N_NSA

U_QKV = 0
U_WO = U_QKV + 24
U_UP1 = U_WO + 8
U_DN1 = U_UP1 + 2 * FC
U_UP2 = U_DN1 + FC
U_DN2 = U_UP2 + 2 * FC
U_MIX = U_DN2 + FC
U_CMP = U_MIX + 17
U_WO2 = U_CMP + 8
U_UP3 = U_WO2 + 8
U_DN3 = U_UP3 + 2 * FC
N_UNITS = U_DN3 + FC

PARAMS = {}
_at = 0
for _name, _n in (("attn_pre", KC), ("attn_post", KC), ("ffn_pre", KC), ("ffn_post", KC),
                  ("ffn1", KC), ("mix", KC), ("ffn2", KC), ("final", KC),
                  ("conv_w", 3 * 2 * FC), ("conv_b", 2 * FC), ("pos_k", 16), ("pos_v", 16),
                  ("b1_k", 2), ("b1_v", 2), ("w2_k", 2 * HD), ("w2_v", 2 * HD)):
    PARAMS[_name] = (_at, _n)
    _at += _n
N_PARAMS = _at
ROW_LAM, ROW_SUB, ROW_SBN, ROW_SINK = 0, 4 * HD, 4 * HD + 2 * HD, 4 * HD + 3 * HD
N_ROW = ROW_SINK + N_SWA

DOWN_ORDER = [4, 5, 6, 7, 0, 1, 2, 3]


def bucket_runs():
    exact = N_BUCKETS // 2
    runs = [(b, b, b) for b in range(exact)]
    d = np.arange(exact, T)
    large = exact + (np.log(d.astype(np.float32) / exact) / math.log(MAX_DISTANCE / exact)
                     * (N_BUCKETS - exact)).astype(np.int32)
    large = np.minimum(large, N_BUCKETS - 1)
    for b in range(exact, N_BUCKETS):
        at = d[large == b]
        if len(at):
            runs.append((b, int(at[0]), int(at[-1])))
    return runs


def build(nc, weights, x_t, params, rows, table_t, bias_line, out_t):
    with ExitStack() as top:
        def sem(name):
            return top.enter_context(nc.semaphore(name))

        def sb(name, shape, dtype=F32, ctx=top):
            return ctx.enter_context(nc.sbuf_tensor(name, shape, dtype))

        stage = sb("stage", [P, RING, UNIT])
        w_hi = sb("w_hi", [P, RING, UNIT], F32R)
        w_lo = sb("w_lo", [P, RING, UNIT], F32R)
        X = sb("X", [P, KC, T])
        par = sb("par", [P, N_PARAMS])
        row = sb("row", [P, N_ROW])
        ones = sb("ones", [P, P])
        ident = sb("ident", [P, P])
        epsc = sb("epsc", [P, 1])
        sq = sb("sq", [P, 2, T])
        rstd = sb("rstd", [P, T])
        tmp = sb("tmp", [P, 2, T])
        with ExitStack() as scope:
            Y2 = sb("Y2", [P, KC, T], ctx=scope)
        H_hi = sb("H_hi", [P, KC, T], F32R)
        H_lo = sb("H_lo", [P, KC, T], F32R)
        with ExitStack() as scope:
            A_hi = sb("A_hi", [P, FC, T], F32R, scope)
            A_lo = sb("A_lo", [P, FC, T], F32R, scope)
            conv = sb("conv", [P, 2, 2, T], ctx=scope)
        with ExitStack() as scope:
            QK = sb("QK", [P, 16, T], ctx=scope)
            V = sb("V", [P, 2, TB, T], ctx=scope)
            O = sb("O", [P, TB, D], ctx=scope)
            strip = sb("strip", [P, 8, T], ctx=scope)
            L = sb("L", [P, 2, 2, T], ctx=scope)
            stat = sb("stat", [P, 4, 8], ctx=scope)
            small = sb("small", [P, 64], ctx=scope)
            line = sb("line", [N_DIFF, LINE], ctx=scope)
            tab = sb("tab", [N_DIFF, N_BUCKETS], ctx=scope)
            gates = sb("gates", [P, TB, 3 * N_NSA], ctx=scope)
            cdist = sb("cdist", [P, P], ctx=scope)
            hid = sb("hid", [P, 2, 2, 2 * NCMP], ctx=scope)
            kcT = sb("kcT", [P, 32], ctx=scope)
            vc = sb("vc", [P, 2, HD], ctx=scope)
        W, WT = sq, tmp
        kpair = V[:, 1, 0:2, :]

        def as_windows(t):
            return t.rearrange("p a n -> p (a n)")[:, 0:16 * 2 * NCMP].rearrange("p (j n) -> p j n", j=16)

        kp, kp_hi, kp_lo = as_windows(W[:, :, :]), as_windows(H_hi[:, 0:2, :]), as_windows(H_lo[:, 0:2, :])

        def cmp_L(g):
            return L[:, g, 0, :]

        def cmp_PT(h):
            return WT[:, h // 4, bass.ts(h % 4, P)]

        def swa_strip(h):
            home = QK[:, 13 + h // 2, :] if h < 6 else V[:, 1, 2, :]
            return home[:, (h % 2) * 256:(h % 2 + 1) * 256]

        PS = top.enter_context(nc.psum_tensor("PS", [P, 8, T], F32))

        def pc(name, k, n=1):
            a, _ = PARAMS[name]
            return par[:, a + k:a + k + n]

        loaded = [sem(f"loaded{i}") for i in range(RING)]
        hi_done = sem("hi_done")
        lo_done = sem("lo_done")
        unit_done = sem("unit_done")
        x_loaded, par_loaded, row_loaded, tab_loaded = map(sem, ("x_loaded", "par_loaded", "row_loaded", "tab_loaded"))
        const_done = sem("const_done")
        dve_self = sem("dve_self")
        act_self = sem("act_self")
        line_out = sem("line_out")
        out_done = [sem("out_done0"), sem("out_done1")]

        block = top.enter_context(nc.Block())

        class Norm:
            def __init__(self, name, gain, src, order, to):
                self.name, self.gain, self.src, self.order, self.to = name, gain, src, order, to
                self.ready = sem(f"{name}_ready")
                self.squared = sem(f"{name}_squared")
                self.summed = sem(f"{name}_summed")
                self.root = sem(f"{name}_root")
                self.inverse = sem(f"{name}_inverse")
                self.scaled = sem(f"{name}_scaled")
                self.hi = sem(f"{name}_hi")
                self.done = sem(f"{name}_done")

        plain = list(range(KC))
        n_attn_pre = Norm("attn_pre", "attn_pre", X, plain, "H")
        n_attn_post = Norm("attn_post", "attn_post", QK, plain, "X")
        n_ffn_pre = Norm("ffn_pre", "ffn_pre", X, plain, "H")
        n_ffn_post = Norm("ffn_post", "ffn_post", Y2, DOWN_ORDER, "X")
        n_ffn1 = Norm("ffn1", "ffn1", X, DOWN_ORDER, "H")
        n_mix = Norm("mix", "mix", X, DOWN_ORDER, "H")
        n_ffn2 = Norm("ffn2", "ffn2", X, plain, "H")
        n_final = Norm("final", "final", X, DOWN_ORDER, "out")

        def pe_norm(pe, n):
            bank = n.order[0]
            for at in range(KC):
                pe.wait_ge(n.squared, at + 1)
                pe.matmul(PS[:, bank, :], ones[:, :], sq[:, at % 2, :], start=(at == 0),
                          stop=(at == KC - 1)).then_inc(n.summed, 1)

        def act_norm(act, n):
            for at, k in enumerate(n.order):
                act.wait_ge(n.ready, at + 1)
                if at >= 2:
                    act.wait_ge(n.summed, at - 1)
                act.activation(sq[:, at % 2, :], n.src[:, k, :], ACT.Square).then_inc(n.squared, 1)
            act.wait_ge(n.summed, KC)
            act.activation(rstd[:, :], PS[:, n.order[0], :], ACT.Sqrt, bias=epsc[:, 0:1]).then_inc(n.root, 1)
            if n.to == "H":
                for at, k in enumerate(n.order):
                    act.wait_ge(n.scaled, at + 1)
                    act.activation(H_hi[:, k, :], tmp[:, at % 2, :], ACT.Copy).then_inc(n.hi, 1)

        def dve_norm(dve, n, then_ready=None):
            dve.wait_ge(n.root, 1)
            dve.reciprocal(rstd[:, :], rstd[:, :]).then_inc(n.inverse, 1)
            dve.wait_ge(n.inverse, 1)
            for at, k in enumerate(n.order):
                if n.to == "H" and at >= 2:
                    dve.wait_ge(n.done, at - 1)
                if n.to == "X" and at >= 2:
                    dve.wait_ge(then_ready, at - 1)
                if n.to == "out" and at >= 2:
                    dve.wait_ge(out_done[at % 2], 16 * (at // 2))
                dve.scalar_tensor_tensor(out=tmp[:, at % 2, :], in0=n.src[:, k, :], scalar=pc(n.gain, k),
                                         in1=rstd[:, :], op0=ALU.mult, op1=ALU.mult).then_inc(n.scaled, 1)
                if n.to == "X":
                    dve.wait_ge(n.scaled, at + 1)
                    dve.tensor_tensor(X[:, k, :], X[:, k, :], tmp[:, at % 2, :], ALU.add).then_inc(then_ready, 1)
                if n.to == "H":
                    dve.wait_ge(n.hi, at + 1)
                    dve.tensor_tensor(H_lo[:, k, :], tmp[:, at % 2, :], H_hi[:, k, :].bitcast(F32),
                                      ALU.subtract).then_inc(n.done, 1)

        def split_matmul(pe, out, w_slot, w_cols, h_hi, h_lo, first, last, skip=False):
            a, b = w_hi[:, w_slot, w_cols], w_lo[:, w_slot, w_cols]
            pe.matmul(out, a, h_hi, start=first, stop=False, skip_group_check=skip)
            pe.matmul(out, a, h_lo, start=False, stop=False, skip_group_check=skip)
            return pe.matmul(out, b, h_hi, start=False, stop=last, skip_group_check=skip)

        def pe_chunk(pe, slot, bank, order=plain, ready=None):
            for at, k in enumerate(order):
                if ready is not None:
                    pe.wait_ge(ready, at + 1)
                m = split_matmul(pe, PS[:, bank, :], slot, bass.ts(k, P), H_hi[:, k, :], H_lo[:, k, :],
                                 at == 0, at == KC - 1)
            m.then_inc(unit_done, 1)

        def pe_by_token(pe, u0, bank0, width, free=None):
            for t in range(4):
                u = u0 + t
                pe.wait_ge(lo_done, u + 1)
                for tb in range(TB):
                    for kk in range(2):
                        k = 2 * t + kk
                        wh = w_hi[:, u % RING, kk * T:kk * T + width]
                        wl = w_lo[:, u % RING, kk * T:kk * T + width]
                        hh, hl = H_hi[:, k, bass.ts(tb, P)], H_lo[:, k, bass.ts(tb, P)]
                        o = PS[:, bank0 + tb, 0:width]
                        pe.matmul(o, hh, wh, start=(k == 0), stop=False)
                        pe.matmul(o, hh, wl, start=False, stop=False)
                        m = pe.matmul(o, hl, wh, start=False, stop=(k == KC - 1))
                m.then_inc(unit_done, 1)

        def act_hi(act, slot, u=None, n_loaded=None, wait_free=True):
            if wait_free:
                act.wait_ge(unit_done, u - RING + 1)
            act.wait_ge(loaded[slot], n_loaded)
            act.activation(w_hi[:, slot, :], stage[:, slot, :], ACT.Copy).then_inc(hi_done, 1)

        def act_hi_static(act, u):
            v = u + RING
            if v < N_UNITS:
                act_hi(act, v % RING, v, 16 * (v // RING + 1))
            else:
                act.wait_ge(unit_done, u + 1)

        ffn_free = sem("ffn_free")
        conv_in = sem("conv_in")
        conv_step = sem("conv_step")
        gated = sem("gated")
        prod = sem("prod")
        y_done = [sem(f"y_done{i}") for i in range(3)]

        def pe_ffn(pe, inst, u_up, u_dn, norm):
            g0 = inst * FC
            for i in range(2):
                pe.wait_ge(lo_done, u_up + i + 1)
                if i == 0:
                    pe.wait_ge(ffn_free, g0 + 1)
                pe_chunk(pe, (u_up + i) % RING, i, norm.order, norm.done if i == 0 else None)
            for i in range(2, 4):
                pe.wait_ge(lo_done, u_up + i + 1)
                if i == 2:
                    pe.wait_ge(ffn_free, g0 + 2)
                pe_chunk(pe, (u_up + i) % RING, i)
            with pe.Fori(1, FC // 2) as r:
                for i in range(4):
                    pe.wait_ge(lo_done, r * 4 + (u_up + i + 1))
                    if i % 2 == 0:
                        pe.wait_ge(ffn_free, r * 2 + (g0 + i // 2 + 1))
                    pe_chunk(pe, (u_up + i) % RING, i)

            def down(slot, a_hi, a_lo, first, last):
                for at, m in enumerate(DOWN_ORDER):
                    if first and at == 4:
                        pe.wait_ge(ffn_free, g0 + FC + 2)
                    mm = split_matmul(pe, PS[:, m, :], slot, bass.ts(m, P), a_hi, a_lo, first, last)
                    if last:
                        mm.then_inc(y_done[inst], 1)
                if not last:
                    mm.then_inc(unit_done, 1)
                else:
                    pe.wait_ge(y_done[inst], KC)
                    pe.sem_inc(unit_done, 1)

            pe.wait_ge(lo_done, u_dn + 1)
            down(u_dn % RING, A_hi[:, 0, :], A_lo[:, 0, :], True, False)
            with pe.Fori(0, (FC - 2) // 4) as r:
                for i in range(4):
                    pe.wait_ge(lo_done, r * 4 + (u_dn + i + 2))
                    f = bass.ds(r * 4 + (i + 1), 1)
                    down((u_dn + i + 1) % RING, A_hi[:, f, :].rearrange("p a n -> p (a n)"),
                         A_lo[:, f, :].rearrange("p a n -> p (a n)"), False, False)
            pe.wait_ge(lo_done, u_dn + FC)
            down((u_dn + FC - 1) % RING, A_hi[:, FC - 1, :], A_lo[:, FC - 1, :], False, True)

        def act_ffn(act, inst, u_up, u_dn, convolved):
            g0 = inst * FC
            with act.Fori(0, FC // 2) as r:
                for i in range(2):
                    ua, ub = u_up + 2 * i, u_up + 2 * i + 1
                    act.wait_ge(unit_done, r * 4 + (ub + 1))
                    act.wait_ge(ffn_free, r * 2 + (g0 + i + 1))
                    for u in (ua, ub):
                        v = u + RING
                        act_hi(act, v % RING, None, r * 16 + 16 * (v // RING + 1), wait_free=False)
                    fe = r * 2 + i
                    if convolved:
                        for j in range(2):
                            c2 = par[:, bass.ds(fe + (PARAMS["conv_w"][0] + (2 * 2 + j) * FC), 1)]
                            cb = par[:, bass.ds(fe + (PARAMS["conv_b"][0] + j * FC), 1)]
                            act.activation(conv[:, i, j, :], PS[:, 2 * i + j, :], ACT.Identity,
                                           bias=cb, scale=c2).then_inc(conv_in, 1)
                        act.wait_ge(conv_step, r * 8 + 4 * i + 3)
                        act.activation(conv[:, i, 0, :], conv[:, i, 0, :], ACT.Gelu_apprx_tanh).then_inc(gated, 1)
                    else:
                        act.activation(conv[:, i, 0, :], PS[:, 2 * i, :], ACT.Silu).then_inc(gated, 1)
            rounds = FC // 4 if u_dn + FC < N_UNITS else FC // 4 - 1
            with act.Fori(0, rounds) as r:
                for i in range(4):
                    v = u_dn + i + RING
                    act_hi(act, v % RING, r * 4 + v, r * 16 + 16 * (v // RING + 1))
            for u in range(u_dn + rounds * 4, u_dn + FC - 1):
                act_hi_static(act, u)

        def dve_ffn(dve, inst, convolved):
            g0 = inst * FC
            with dve.Fori(0, FC // 2) as r:
                for i in range(2):
                    fe = r * 2 + i
                    if convolved:
                        def tap(back, j):
                            c = par[:, bass.ds(fe + (PARAMS["conv_w"][0] + (2 * (2 - back) + j) * FC), 1)]
                            z = conv[:, i, j, back:T]
                            dve.scalar_tensor_tensor(out=z, in0=PS[:, 2 * i + j, 0:T - back], scalar=c, in1=z,
                                                     op0=ALU.mult, op1=ALU.add).then_inc(conv_step, 1)
                        for j in range(2):
                            dve.wait_ge(conv_in, r * 4 + 2 * i + j + 1)
                            tap(1, j)
                        for j in range(2):
                            dve.wait_ge(conv_step, r * 8 + 4 * i + j + 1)
                            tap(2, j)
                        dve.wait_ge(conv_step, r * 8 + 4 * i + 4)
                        value = conv[:, i, 1, :]
                    else:
                        value = PS[:, 2 * i + 1, :]
                    dve.wait_ge(gated, r * 2 + (g0 + i + 1))
                    f = bass.ds(fe, 1)
                    ah = A_hi[:, f, :].rearrange("p a n -> p (a n)")
                    al = A_lo[:, f, :].rearrange("p a n -> p (a n)")
                    dve.tensor_tensor(ah, conv[:, i, 0, :], value, ALU.mult).then_inc(prod, 1)
                    dve.tensor_tensor(conv[:, i, 0, :], conv[:, i, 0, :], value, ALU.mult).then_inc(prod, 1)
                    dve.wait_ge(prod, r * 4 + (2 * g0 + 2 * i + 2))
                    dve.tensor_tensor(al, conv[:, i, 0, :], ah.bitcast(F32), ALU.subtract).then_inc(ffn_free, 1)

        class Item:
            pass

        def full(i):
            return 0, (i + 1) * P, (TB - 1 - i) * P

        items1, items2 = [], []
        for i in range(TB):
            k0, nk, s0 = full(i)
            for h in range(N_DIFF):
                it = Item()
                it.kind, it.i, it.k0, it.nk = "diff", i, k0, nk
                it.maps = [(QK[m * HD:(m + 1) * HD, 4 * h, bass.ts(i, P)], QK[m * HD:(m + 1) * HD, 4 * h + 1, k0:k0 + nk])
                           for m in range(2)]
                it.bias = strip[:, h, s0:s0 + nk]
                it.v = [V[:, 0, kb, bass.ts(h, P)] for kb in range(nk // P)]
                it.out = O[:, i, bass.ts(h, P)]
                items1.append(it)
            for h in range(N_SB):
                it = Item()
                it.kind, it.i, it.k0, it.nk = "sb", i, k0, nk
                b = (h % 2) * HD
                it.maps = [(QK[b:b + HD, 4 * (h // 2) + 2, bass.ts(i, P)], QK[b:b + HD, 4 * (h // 2) + 3, k0:k0 + nk])]
                it.v = [V[:, 1, kb, bass.ts(h, HD)] for kb in range(nk // P)]
                it.out = O[:, i, T + h * HD:T + (h + 1) * HD]
                items1.append(it)
        for i in range(TB):
            k0, nk, s0 = full(i)
            for h in range(N_NSA):
                g, c = h // 4, h % 4
                for branch in range(2):
                    it = Item()
                    it.kind, it.i, it.k0, it.nk = "soft", i, k0, nk
                    it.maps = [(QK[g * HD:(g + 1) * HD, c, bass.ts(i, P)], QK[g * HD:(g + 1) * HD, 4 + branch, k0:k0 + nk])]
                    it.bias = strip[:, h, s0:s0 + nk]
                    it.v = [V[:, 0, kb, branch * P + g * HD:branch * P + (g + 1) * HD] for kb in range(nk // P)]
                    it.out = O[:, i, bass.ts(h, HD)]
                    it.gate = gates[:, i, 3 * h + 1 + branch:3 * h + 2 + branch]
                    it.sink = None
                    items2.append(it)
            for h in range(N_SWA):
                g, c = h // 4, h % 4
                it = Item()
                it.kind, it.i = "soft", i
                it.k0, it.nk = max(i - 1, 0) * P, min(i + 1, 2) * P
                it.maps = [(QK[g * HD:(g + 1) * HD, 8 + c, bass.ts(i, P)], QK[g * HD:(g + 1) * HD, 12, it.k0:it.k0 + it.nk])]
                it.bias = swa_strip(h)[:, 256 - it.nk:256]
                it.v = [V[:, 0, it.k0 // P + kb, 2 * P + g * HD:2 * P + (g + 1) * HD] for kb in range(it.nk // P)]
                it.out = O[:, i, T + h * HD:T + (h + 1) * HD]
                it.gate = None
                it.sink = row[:, ROW_SINK + h:ROW_SINK + h + 1]
                items2.append(it)
        for items in (items1, items2):
            pre = 0
            for n, it in enumerate(items):
                it.n = n
                it.dv = it.out.shape[-1]
                it.st = stat[:, n % 4, :]
                pre += it.kind == "sb"
                it.pre = pre

        class Attn:
            def __init__(self, name, items, scale):
                self.name, self.items, self.scale = name, items, scale
                self.qk_done = sem(f"{name}_qk_done")
                self.s_read = sem(f"{name}_s_read")
                self.pre_done = sem(f"{name}_pre_done")
                self.logits = sem(f"{name}_logits")
                self.exp_done = sem(f"{name}_exp_done")
                self.comb = sem(f"{name}_comb")
                self.turned = sem(f"{name}_turned")
                self.wt_ready = sem(f"{name}_wt_ready")
                self.pv_done = sem(f"{name}_pv_done")
                self.o_done = sem(f"{name}_o_done")

        at1 = Attn("at1", items1, 1.0)
        at2 = Attn("at2", items2, SCALE)
        v_ready = [sem("v_ready1"), sem("v_ready2")]
        strips_done = [sem("strips_done1"), sem("strips_done2")]

        def pe_attn(pe, a):
            items = a.items
            for n in range(len(items) + 3):
                if n < len(items):
                    it = items[n]
                    if n >= 2:
                        pe.wait_ge(a.s_read, n - 1)
                    for m, (q, k) in enumerate(it.maps):
                        mm = pe.matmul(PS[:, 2 * (n % 2) + m, 0:it.nk], q, k, start=True, stop=True)
                    mm.then_inc(a.qk_done, 1)
                if 2 <= n < len(items) + 2:
                    it = items[n - 2]
                    pe.wait_ge(a.comb, it.n + 1)
                    pe.wait_ge(a.exp_done, it.n + 1)
                    if it.n >= 2:
                        pe.wait_ge(a.wt_ready, it.n - 1)
                    for kb in range(it.nk // P):
                        mm = pe.transpose(PS[:, 4 + it.n % 2, bass.ts(kb, P)], W[:, it.n % 2, bass.ts(kb, P)], ident[:, :])
                    mm.then_inc(a.turned, 1)
                if n >= 3:
                    it = items[n - 3]
                    pe.wait_ge(a.wt_ready, it.n + 1)
                    if it.n >= 2:
                        pe.wait_ge(a.o_done, it.n - 1)
                    for kb in range(it.nk // P):
                        mm = pe.matmul(PS[:, 6 + it.n % 2, 0:it.dv], WT[:, it.n % 2, bass.ts(kb, P)], it.v[kb],
                                       start=(kb == 0), stop=(kb == it.nk // P - 1))
                    mm.then_inc(a.pv_done, 1)

        def act_attn(act, a, link, after):
            items = a.items
            for n in range(len(items) + 2):
                if n < len(items) and items[n].kind == "sb":
                    it = items[n]
                    if n >= 2:
                        act.wait_ge(a.comb, n - 1)
                    act.wait_ge(a.qk_done, n + 1)
                    z = L[:, n % 2, 0, 0:it.nk]
                    c = link(act.activation(z, PS[:, 2 * (n % 2), 0:it.nk], ACT.Abs))
                    after(c)
                    c = link(act.activation(z, z, ACT.Exp, scale=-1.0))
                    after(c)
                    act.activation(z, z, ACT.Ln, bias=1.0).then_inc(a.pre_done, 1)
                if 1 <= n < len(items) + 1:
                    it = items[n - 1]
                    if it.kind != "diff" and it.n >= 2:
                        act.wait_ge(a.turned, it.n - 1)
                    act.wait_ge(a.logits, it.n + 1)
                    if it.kind == "sb":
                        act.activation(W[:, it.n % 2, 0:it.nk], L[:, it.n % 2, 1, 0:it.nk], ACT.Exp).then_inc(a.exp_done, 1)
                    elif it.kind == "diff":
                        for m in range(2):
                            z = L[:, it.n % 2, m, 0:it.nk]
                            x = act.activation(z, z, ACT.Exp, bias=it.st[:, 2 + m:3 + m], accum_out=it.st[:, 4 + m:5 + m])
                        x.then_inc(a.exp_done, 1)
                    else:
                        if it.sink is not None:
                            act.activation(it.st[:, 5:6], it.sink, ACT.Exp, bias=it.st[:, 2:3])
                        act.activation(W[:, it.n % 2, 0:it.nk], L[:, it.n % 2, 0, 0:it.nk], ACT.Exp,
                                       bias=it.st[:, 2:3], accum_out=it.st[:, 4:5]).then_inc(a.exp_done, 1)
                if n >= 2:
                    it = items[n - 2]
                    act.wait_ge(a.turned, it.n + 1)
                    if it.n >= 2:
                        act.wait_ge(a.pv_done, it.n - 1)
                    act.activation(WT[:, it.n % 2, 0:it.nk], PS[:, 4 + it.n % 2, 0:it.nk], ACT.Copy).then_inc(a.wt_ready, 1)

        def dve_attn(dve, a, link, after):
            items = a.items
            for n in range(len(items) + 4):
                if n < len(items):
                    it = items[n]
                    dve.wait_ge(a.qk_done, n + 1)
                    if n >= 2:
                        dve.wait_ge(a.exp_done, n - 1)
                        dve.wait_ge(a.comb, n - 1)
                    S = PS[:, 2 * (n % 2), 0:it.nk]
                    if it.kind == "sb":
                        dve.wait_ge(a.pre_done, it.pre)
                        u, z = L[:, n % 2, 0, 0:it.nk], L[:, n % 2, 1, 0:it.nk]
                        c = link(dve.scalar_tensor_tensor(out=u, in0=S, scalar=0.0, in1=u, op0=ALU.max, op1=ALU.add))
                        diag = u[:, it.nk - P:it.nk]
                        after(c)
                        c = link(dve.tensor_tensor(diag, diag, strip[:, 4, 0:P], ALU.mult))
                        after(c)
                        c = link(dve.tensor_tensor_scan(z[:, ::-1], u[:, ::-1], u[:, ::-1], 0.0, ALU.add, ALU.max))
                        after(c)
                        c = link(dve.tensor_tensor(z, S, z, ALU.subtract))
                        after(c)
                        dve.sem_inc(a.s_read, 1)
                        diag = z[:, it.nk - P:it.nk]
                        dve.tensor_tensor(diag, diag, strip[:, 4, P:2 * P], ALU.add).then_inc(a.logits, 1)
                    else:
                        for m in range(len(it.maps)):
                            c = link(dve.tensor_tensor_reduce(
                                out=L[:, n % 2, m, 0:it.nk], in0=PS[:, 2 * (n % 2) + m, 0:it.nk], in1=it.bias,
                                scale=a.scale, scalar=-3e38, op0=ALU.add, op1=ALU.max, accum_out=it.st[:, m:m + 1]))
                        after(c)
                        dve.sem_inc(a.s_read, 1)
                        nm = len(it.maps)
                        if it.kind == "soft" and it.sink is not None:
                            dve.tensor_scalar(it.st[:, 2:3], it.st[:, 0:1], it.sink, -1.0, ALU.max, ALU.mult).then_inc(a.logits, 1)
                        else:
                            dve.tensor_scalar(it.st[:, 2:2 + nm], it.st[:, 0:nm], -1.0, None, ALU.mult).then_inc(a.logits, 1)
                if 1 <= n < len(items) + 1:
                    it = items[n - 1]
                    dve.wait_ge(a.exp_done, it.n + 1)
                    if it.kind == "sb":
                        dve.sem_inc(a.comb, 1)
                    elif it.kind == "diff":
                        if it.n >= 2:
                            dve.wait_ge(a.turned, it.n - 1)
                        c = link(dve.reciprocal(it.st[:, 6:8], it.st[:, 4:6]))
                        after(c)
                        c = link(dve.tensor_tensor(it.st[:, 7:8], it.st[:, 7:8], small[:, 0:1], ALU.mult))
                        after(c)
                        z0, z1 = L[:, it.n % 2, 0, 0:it.nk], L[:, it.n % 2, 1, 0:it.nk]
                        c = link(dve.tensor_scalar(z1, z1, it.st[:, 7:8], None, ALU.mult))
                        after(c)
                        dve.scalar_tensor_tensor(out=W[:, it.n % 2, 0:it.nk], in0=z0, scalar=it.st[:, 6:7], in1=z1,
                                                 op0=ALU.mult, op1=ALU.add).then_inc(a.comb, 1)
                    else:
                        if it.sink is not None:
                            after(link(dve.tensor_tensor(it.st[:, 4:5], it.st[:, 4:5], it.st[:, 5:6], ALU.add)))
                        c = link(dve.reciprocal(it.st[:, 6:7], it.st[:, 4:5]))
                        after(c)
                        if it.gate is not None:
                            c = link(dve.tensor_tensor(it.st[:, 6:7], it.st[:, 6:7], it.gate, ALU.mult))
                            after(c)
                        dve.sem_inc(a.comb, 1)
                if n >= 4:
                    it = items[n - 4]
                    dve.wait_ge(a.pv_done, it.n + 1)
                    pv = PS[:, 6 + it.n % 2, 0:it.dv]
                    if it.kind == "soft" and it.gate is not None:
                        dve.scalar_tensor_tensor(out=it.out, in0=pv, scalar=it.st[:, 6:7], in1=it.out,
                                                 op0=ALU.mult, op1=ALU.add).then_inc(a.o_done, 1)
                    elif it.kind == "soft":
                        dve.tensor_scalar(it.out, pv, it.st[:, 6:7], None, ALU.mult).then_inc(a.o_done, 1)
                    else:
                        dve.tensor_copy(it.out, pv).then_inc(a.o_done, 1)
                    if it.n >= 0:
                        dve.wait_ge(a.o_done, it.n + 1)

        o_ready = [sem("o_ready1"), sem("o_ready2")]
        o_turned = [sem("o_turned1"), sem("o_turned2")]
        o_hi = [sem("o_hi1"), sem("o_hi2")]
        o_split = [sem("o_split1"), sem("o_split2")]
        wo_out = [sem("wo_out1"), sem("wo_out2")]

        def pe_turn(pe, b):
            for n in range(2 * TB):
                i, half = n // 2, n % 2
                pe.wait_ge(o_ready[b], i + 1)
                if n >= 4:
                    pe.wait_ge(o_split[b], n - 3)
                for c in range(4):
                    mm = pe.transpose(PS[:, n % 4, bass.ts(c, P)], O[:, i, bass.ts(half * 4 + c, P)], ident[:, :])
                mm.then_inc(o_turned[b], 1)

        def turned_aps(n):
            i, half = n // 2, n % 2
            src = PS[:, n % 4, :].rearrange("p (c n) -> p c n", c=4)
            return src, H_hi[:, 4 * half:4 * half + 4, bass.ts(i, P)], H_lo[:, 4 * half:4 * half + 4, bass.ts(i, P)]

        def act_turn(act, b):
            for n in range(2 * TB):
                src, hi, _ = turned_aps(n)
                act.wait_ge(o_turned[b], n + 1)
                act.activation(hi, src, ACT.Copy).then_inc(o_hi[b], 1)

        def dve_turn(dve, b):
            for n in range(2 * TB):
                src, hi, lo = turned_aps(n)
                dve.wait_ge(o_hi[b], n + 1)
                dve.tensor_tensor(lo, src, hi.bitcast(F32), ALU.subtract).then_inc(o_split[b], 1)

        def pe_wo(pe, b, u0):
            for j in range(KC):
                pe.wait_ge(lo_done, u0 + j + 1)
                if j == 0:
                    pe.wait_ge(o_split[b], 2 * TB)
                pe_chunk(pe, (u0 + j) % RING, j)

        head = sem("head")
        head_root = sem("head_root")

        def head_parts(i):
            d = O[:, i, 0:T].rearrange("p (h d) -> p h d", d=P)
            s = O[:, i, T:2 * T].rearrange("p (h d) -> p h d", d=HD)
            return d, s

        qk_evac = [sem("qk_evac1"), sem("qk_evac2")]
        cm = {k: sem("cm_" + k) for k in (
            "raw", "kp", "kp_hi", "kp_lo", "mlp", "hid", "kv", "kv_sb", "s", "l", "e", "p", "t", "pt", "pv", "used")}
        gate_e = sem("gate_e")
        lam_e = sem("lam_e")

        @block.sync
        def _(sp):
            sp.dma_start(X[:, :, :], x_t).then_inc(x_loaded, 16)
            sp.dma_start(par[:, :], params).then_inc(par_loaded, 16)
            for u in range(RING):
                sp.dma_start(stage[:, u, :], weights[u]).then_inc(loaded[u], 16)
            sp.dma_start(row[:, :], rows.to_broadcast([P, N_ROW])).then_inc(row_loaded, 16)
            sp.dma_start(tab[:, :], table_t).then_inc(tab_loaded, 16)
            sp.wait_ge(strips_done[0], 1)
            sp.dma_start(bias_line[:, :, 0:LINE], line[:, :].unsqueeze(1).to_broadcast([N_DIFF, P, LINE])).then_inc(line_out, 16)
            sp.wait_ge(line_out, 16)
            sp.dma_start(strip[:, 0:N_DIFF, :], bass.AP(
                tensor=bias_line.tensor, offset=P - 1,
                ap=[[LINE, P], [P * (LINE + 1), N_DIFF], [1, T]])).then_inc(strips_done[0], 16)
            rounds = N_UNITS // RING
            with sp.Fori(1, rounds) as r:
                for i in range(RING):
                    sp.wait_ge(lo_done, r * RING + (i + 1 - RING))
                    sp.dma_start(stage[:, i, :], weights[i:rounds * RING:RING][bass.ds(r, 1)].rearrange(
                        "a p n -> p (a n)")).then_inc(loaded[i], 16)
            for u in range(rounds * RING, N_UNITS):
                sp.wait_ge(lo_done, u + 1 - RING)
                sp.dma_start(stage[:, u % RING, :], weights[u]).then_inc(loaded[u % RING], 16)
            for at, k in enumerate(DOWN_ORDER):
                sp.wait_ge(n_final.scaled, at + 1)
                sp.dma_start(out_t[:, k, :], tmp[:, at % 2, :]).then_inc(out_done[at % 2], 16)
            for p in range(2):
                sp.wait_ge(out_done[p], 16 * KC // 2)

        @block.gpsimd
        def _(pool):
            pool.memset(ones[:, :], 1.0 / D).then_inc(const_done, 1)
            pool.memset(ident[:, :], 0.0).then_inc(const_done, 1)
            pool.memset(epsc[:, :], EPS).then_inc(const_done, 1)
            pool.memset(strip[:, 4, 0:P], 1.0).then_inc(const_done, 1)
            pool.memset(strip[:, 4, P:2 * P], 0.0).then_inc(const_done, 1)
            pool.wait_ge(const_done, 5)
            pool.affine_select(out=ident[:, :], in_=ident[:, :], compare_op=ALU.not_equal, fill=1.0, base=0,
                               pattern=[[-1, P]], channel_multiplier=1).then_inc(const_done, 1)
            pool.affine_select(out=strip[:, 4, 0:P], in_=strip[:, 4, 0:P], compare_op=ALU.is_gt, fill=0.0, base=0,
                               pattern=[[-1, P]], channel_multiplier=1).then_inc(const_done, 1)
            pool.affine_select(out=strip[:, 4, P:2 * P], in_=strip[:, 4, P:2 * P], compare_op=ALU.is_gt, fill=MASKED,
                               base=0, pattern=[[-1, P]], channel_multiplier=1).then_inc(const_done, 1)

            def rest(u_of, slot):
                pool.wait_ge(hi_done, u_of)
                pool.tensor_tensor(w_lo[:, slot, :], stage[:, slot, :], w_hi[:, slot, :].bitcast(F32),
                                   ALU.subtract).then_inc(lo_done, 1)

            def run(u0, u1):
                with pool.Fori(u0 // RING, u1 // RING) as r:
                    for i in range(RING):
                        rest(r * RING + (i + 1), i)
                for u in range(u1 // RING * RING, u1):
                    rest(u + 1, u % RING)

            mid = U_MIX + RING
            run(0, mid)
            di = L[:, 0, 0, :].bitcast(I32)
            pool.wait_ge(n_mix.done, KC)
            pool.iota(di, pattern=[[-1, T]], base=3 * P, channel_multiplier=1).then_inc(const_done, 1)
            pool.iota(L[:, 0, 1, 0:4 * 32].bitcast(I32).rearrange("p (i c) -> p i c", i=4),
                      pattern=[[P, 4], [-CMP_STRIDE, 32]], base=-(CMP_BLOCK - 1), channel_multiplier=1).then_inc(const_done, 1)
            pool.wait_ge(const_done, 10)
            pool.tensor_copy(L[:, 1, 0, :], di).then_inc(const_done, 1)
            pool.tensor_copy(L[:, 1, 1, 0:P], L[:, 0, 1, 0:P].bitcast(I32)).then_inc(const_done, 1)
            pool.wait_ge(const_done, 12)
            pool.affine_select(out=WT[:, 1, 0:256], in_=L[:, 1, 0, 256:512], compare_op=ALU.is_ge, fill=FAR,
                               base=P, pattern=[[-1, 256]], channel_multiplier=1).then_inc(const_done, 1)
            pool.wait_ge(const_done, 13)
            pool.affine_select(out=WT[:, 1, 0:256], in_=WT[:, 1, 0:256], compare_op=ALU.is_gt, fill=FAR,
                               base=0, pattern=[[1, 256]], channel_multiplier=-1).then_inc(const_done, 1)
            pool.affine_select(out=L[:, 1, 0, :], in_=L[:, 1, 0, :], compare_op=ALU.is_ge, fill=FAR,
                               base=3 * P, pattern=[[-1, T]], channel_multiplier=1).then_inc(const_done, 1)
            pool.affine_select(out=L[:, 1, 1, 0:P].rearrange("p (i c) -> p i c", i=4),
                               in_=L[:, 1, 1, 0:P].rearrange("p (i c) -> p i c", i=4), compare_op=ALU.is_ge, fill=FAR,
                               base=-(CMP_BLOCK - 1), pattern=[[P, 4], [-CMP_STRIDE, 32]], channel_multiplier=1).then_inc(const_done, 1)
            run(mid, N_UNITS)

        @block.scalar
        def _(act):
            count = [0]

            def link(ins):
                ins.then_inc(act_self, 1)
                count[0] += 1
                return count[0]

            def after(c):
                act.wait_ge(act_self, c)

            for u in range(RING):
                act_hi(act, u, None, 16, wait_free=False)
            act.wait_ge(const_done, 3)
            act.wait_ge(x_loaded, 16)
            act.sem_inc(n_attn_pre.ready, KC)
            act_norm(act, n_attn_pre)

            with act.Fori(0, 4) as r:
                for i in range(4):
                    v = U_QKV + i + RING
                    act_hi(act, v % RING, r * 4 + v, r * 16 + 16 * (v // RING + 1))
                    act.activation(QK[:, bass.ds(r * 4 + i, 1), :].rearrange("p a n -> p (a n)"), PS[:, i, :],
                                   ACT.Copy, scale=SCALE if i % 2 == 0 else 1.0).then_inc(qk_evac[0], 1)
            for g in range(2):
                for t in range(4):
                    act_hi_static(act, U_QKV + 16 + 4 * g + t)
                for tb in range(TB):
                    act.activation(V[:, g, tb, :], PS[:, (4 if g == 0 else 0) + tb, :], ACT.Copy).then_inc(v_ready[0], 1)
            act.wait_ge(lam_e, 2)
            act.activation(small[:, 4:6], small[:, 2:4], ACT.Exp).then_inc(lam_e, 1)
            act_attn(act, at1, link, after)
            for i in range(TB):
                act.wait_ge(head, 3 * i + 1)
                act.activation(small[:, 16:16 + 12], small[:, 32:32 + 12], ACT.Sqrt, bias=epsc[:, 0:1]).then_inc(head_root, 1)
            act_turn(act, 0)
            for j in range(KC):
                act_hi_static(act, U_WO + j)
                act.activation(QK[:, j, :], PS[:, j, :], ACT.Copy).then_inc(n_attn_post.ready, 1)
            act_norm(act, n_attn_post)
            act_norm(act, n_ffn_pre)
            act_ffn(act, 0, U_UP1, U_DN1, True)
            for at, k in enumerate(DOWN_ORDER):
                act.wait_ge(y_done[0], at + 1)
                act.activation(Y2[:, k, :], PS[:, k, :], ACT.Copy).then_inc(n_ffn_post.ready, 1)
            act_hi_static(act, U_DN1 + FC - 1)
            act_norm(act, n_ffn_post)
            act_norm(act, n_ffn1)
            act_ffn(act, 1, U_UP2, U_DN2, False)
            act_hi_static(act, U_DN2 + FC - 1)
            act_norm(act, n_mix)
            with act.Fori(0, 3) as r:
                for i in range(4):
                    v = U_MIX + i + RING
                    act_hi(act, v % RING, r * 4 + v, r * 16 + 16 * (v // RING + 1))
                    act.activation(QK[:, bass.ds(r * 4 + i, 1), :].rearrange("p a n -> p (a n)"), PS[:, i, :],
                                   ACT.Copy).then_inc(qk_evac[1], 1)
            act_hi_static(act, U_MIX + 12)
            act.activation(QK[:, 12, :], PS[:, 0, :], ACT.Copy).then_inc(qk_evac[1], 1)
            for t in range(4):
                act_hi_static(act, U_MIX + 13 + t)
            for tb in range(TB):
                act.activation(V[:, 0, tb, 0:NAT2], PS[:, 4 + tb, 0:NAT2], ACT.Copy).then_inc(v_ready[1], 1)
            act.wait_ge(v_ready[1], TB)
            act.activation(gates[:, :, :], V[:, 0, :, 3 * P:NAT2], ACT.Exp, scale=-1.0).then_inc(gate_e, 1)
            for s in range(2):
                if s == 1:
                    act.wait_ge(cm["kp"], 1)
                for g in range(2):
                    src = QK[g * HD:(g + 1) * HD, 6 + s, :]
                    act.dma_start(kpair[0:HD, g, :], src).then_inc(cm["raw"], 16)
                    act.dma_start(kpair[HD:P, g, 0:T - 1], src[:, 1:T]).then_inc(cm["raw"], 16)
                act.wait_ge(cm["kp"], s + 1)
                if s == 1:
                    act.wait_ge(unit_done, U_CMP + 4)
                act.activation(kp_hi, kp, ACT.Copy).then_inc(cm["kp_hi"], 1)
                for t in range(4):
                    act_hi_static(act, U_CMP + 4 * s + t)
                for half in range(2):
                    act.activation(hid[:, s, half, :], PS[:, 2 * s + half, 0:2 * NCMP], ACT.Gelu_apprx_tanh,
                                   bias=pc("b1_k" if s == 0 else "b1_v", half)).then_inc(cm["hid"], 1)
            act.wait_ge(cm["kv"], 1)
            act.activation(kcT[:, 0:NCMP], PS[:, 4, 0:NCMP], ACT.Copy).then_inc(cm["kv_sb"], 1)
            for i in range(4):
                act.activation(vc[32 * i:32 * i + NCMP, :, :], PS[32 * i:32 * i + NCMP, 5, 0:2 * HD].rearrange(
                    "p (g d) -> p g d", g=2), ACT.Copy).then_inc(cm["kv_sb"], 1)
            for g in range(2):
                act.wait_ge(cm["l"], g + 1)
                z = cmp_L(g)
                act.activation(z, z, ACT.Exp, scale=SCALE).then_inc(cm["e"], 1)
            for h in range(N_NSA):
                act.wait_ge(cm["t"], h // 4 + 1)
                act.activation(cmp_PT(h), PS[:, 6 + h // 4, bass.ts(h % 4, P)],
                               ACT.Copy).then_inc(cm["pt"], 1)
            act_attn(act, at2, link, after)
            act_turn(act, 1)
            for j in range(KC):
                act_hi_static(act, U_WO2 + j)
            act_norm(act, n_ffn2)
            act_ffn(act, 2, U_UP3, U_DN3, False)
            act_norm(act, n_final)

        @block.tensor
        def _(pe):
            pe.sem_inc(ffn_free, 2)
            pe.sem_inc(qk_evac[0], 4)
            pe.sem_inc(qk_evac[1], 4)
            pe.wait_ge(const_done, 8)
            pe_norm(pe, n_attn_pre)
            for k in range(1):
                pe.wait_ge(n_attn_pre.done, KC)
            with pe.Fori(0, 4) as r:
                for i in range(4):
                    pe.wait_ge(lo_done, r * 4 + (U_QKV + i + 1))
                    pe.wait_ge(qk_evac[0], r * 4 + (i + 1))
                    pe_chunk(pe, (U_QKV + i) % RING, i)
            pe_by_token(pe, U_QKV + 16, 4, T)
            pe.wait_ge(qk_evac[0], 20)
            pe_by_token(pe, U_QKV + 20, 0, T)
            pe.wait_ge(v_ready[0], 2 * TB)
            pe_attn(pe, at1)
            pe.wait_ge(at1.o_done, len(items1))
            pe_turn(pe, 0)
            pe_wo(pe, 0, U_WO)
            pe_norm(pe, n_attn_post)
            pe_norm(pe, n_ffn_pre)
            pe_ffn(pe, 0, U_UP1, U_DN1, n_ffn_pre)
            pe_norm(pe, n_ffn_post)
            pe_norm(pe, n_ffn1)
            pe_ffn(pe, 1, U_UP2, U_DN2, n_ffn1)
            pe_norm(pe, n_mix)
            pe.wait_ge(n_mix.done, KC)
            with pe.Fori(0, 3) as r:
                for i in range(4):
                    pe.wait_ge(lo_done, r * 4 + (U_MIX + i + 1))
                    pe.wait_ge(qk_evac[1], r * 4 + (i + 1))
                    pe_chunk(pe, (U_MIX + i) % RING, i)
            pe.wait_ge(lo_done, U_MIX + 13)
            pe.wait_ge(qk_evac[1], 13)
            pe_chunk(pe, (U_MIX + 12) % RING, 0)
            pe_by_token(pe, U_MIX + 13, 4, NAT2)
            pe.wait_ge(qk_evac[1], 17)
            for s in range(2):
                pe.wait_ge(cm["kp_lo"], s + 1)
                for t in range(4):
                    u = U_CMP + 4 * s + t
                    pe.wait_ge(lo_done, u + 1)
                    for j4 in range(4):
                        j = 4 * t + j4
                        for half in range(2):
                            cols = slice(j4 * CMP_HID + half * P, j4 * CMP_HID + (half + 1) * P)
                            mm = split_matmul(pe, PS[:, 2 * s + half, 0:2 * NCMP], u % RING, cols,
                                              kp_hi[:, j, :], kp_lo[:, j, :], j == 0, j == 15)
                    mm.then_inc(unit_done, 1)
            pe.wait_ge(cm["hid"], 4)
            pe.wait_ge(v_ready[1], TB)
            for g in range(2):
                for half in range(2):
                    pe.matmul(PS[g * HD:(g + 1) * HD, 4, 0:NCMP], pc("w2_k", half * HD, HD),
                              hid[:, 0, half, g * NCMP:(g + 1) * NCMP], start=(half == 0), stop=(half == 1))
            for i in range(4):
                for g in range(2):
                    for half in range(2):
                        mm = pe.matmul(PS[32 * i:32 * i + NCMP, 5, g * HD:(g + 1) * HD],
                                       hid[:, 1, half, g * NCMP:(g + 1) * NCMP], pc("w2_v", half * HD, HD),
                                       start=(half == 0), stop=(half == 1))
            mm.then_inc(cm["kv"], 1)
            pe.wait_ge(cm["kv_sb"], 5)
            for g in range(2):
                for r in range(4):
                    for i in range(TB):
                        mm = pe.matmul(PS[:, g, r * P + i * 32:r * P + i * 32 + NCMP],
                                       QK[g * HD:(g + 1) * HD, r, bass.ts(i, P)], kcT[g * HD:(g + 1) * HD, 0:NCMP],
                                       start=True, stop=True)
                mm.then_inc(cm["s"], 1)
            for g in range(2):
                pe.wait_ge(cm["p"], g + 1)
                for r in range(4):
                    mm = pe.transpose(PS[:, 6 + g, bass.ts(r, P)], cmp_L(g)[:, bass.ts(r, P)], ident[:, :])
                mm.then_inc(cm["t"], 1)
            pe.wait_ge(cm["pt"], N_NSA)
            for i in range(TB):
                for h in range(N_NSA):
                    mm = pe.matmul(PS[:, i, bass.ts(h, HD)], cmp_PT(h)[32 * i:32 * i + NCMP, :],
                                   vc[32 * i:32 * i + NCMP, h // 4, :], start=True, stop=True)
                mm.then_inc(cm["pv"], 1)
            pe.wait_ge(cm["used"], TB)
            pe_attn(pe, at2)
            pe.wait_ge(at2.o_done, len(items2))
            pe_turn(pe, 1)
            pe_wo(pe, 1, U_WO2)
            pe_norm(pe, n_ffn2)
            pe_ffn(pe, 2, U_UP3, U_DN3, n_ffn2)
            pe_norm(pe, n_final)

        @block.vector
        def _(dve):
            count = [0]

            def link(ins):
                ins.then_inc(dve_self, 1)
                count[0] += 1
                return count[0]

            def after(c):
                dve.wait_ge(dve_self, c)

            dve.wait_ge(row_loaded, 16)
            for m in range(2):
                a = row[:, ROW_LAM + 2 * m * HD:ROW_LAM + (2 * m + 1) * HD]
                b = row[:, ROW_LAM + (2 * m + 1) * HD:ROW_LAM + (2 * m + 2) * HD]
                dve.tensor_tensor_reduce(out=tmp[:, 0, m * HD:(m + 1) * HD], in0=a, in1=b, scale=1.0, scalar=0.0, op0=ALU.mult,
                                         op1=ALU.add, accum_out=small[:, 2 + m:3 + m]).then_inc(lam_e, 1)
            dve.wait_ge(tab_loaded, 16)
            for b, lo, hi in bucket_runs():
                c = link(dve.tensor_copy(line[:, T - 1 - hi:T - lo],
                                         tab[:, b:b + 1].to_broadcast([N_DIFF, hi - lo + 1])))
            c = link(dve.memset(line[:, T:LINE], MASKED))
            after(c)
            dve.sem_inc(strips_done[0], 1)
            dve.wait_ge(par_loaded, 16)
            dve_norm(dve, n_attn_pre)
            dve.wait_ge(lam_e, 3)
            after(link(dve.tensor_tensor(small[:, 0:1], small[:, 5:6], small[:, 4:5], ALU.subtract)))
            after(link(dve.tensor_scalar(small[:, 0:1], small[:, 0:1], LAM_INIT, None, ALU.subtract)))
            dve.wait_ge(strips_done[0], 17)
            dve.wait_ge(const_done, 8)
            dve_attn(dve, at1, link, after)
            for i in range(TB):
                d, s = head_parts(i)
                gd = row[:, ROW_SUB:ROW_SUB + P].unsqueeze(1).to_broadcast([P, N_DIFF, P])
                gs = row[:, ROW_SBN:ROW_SBN + HD].unsqueeze(1).to_broadcast([P, N_SB, HD])
                z = L[:, 0, :, :].rearrange("p a n -> p (a n)")
                after(link(dve.tensor_tensor(z, O[:, i, :], O[:, i, :], ALU.mult)))
                link(dve.tensor_reduce(small[:, 44:48], z[:, 0:T].rearrange("p (h d) -> p h d", d=P), AX_X, ALU.add))
                after(link(dve.tensor_reduce(small[:, 48:56], z[:, T:2 * T].rearrange("p (h d) -> p h d", d=HD), AX_X, ALU.add)))
                link(dve.tensor_scalar(small[:, 32:36], small[:, 44:48], 1.0 / P, None, ALU.mult))
                after(link(dve.tensor_scalar(small[:, 36:44], small[:, 48:56], 1.0 / HD, None, ALU.mult)))
                dve.sem_inc(head, 1)
                dve.wait_ge(head_root, i + 1)
                after(link(dve.reciprocal(small[:, 16:28], small[:, 16:28])))
                after(link(dve.tensor_scalar(small[:, 16:20], small[:, 16:20], 1.0 - LAM_INIT, None, ALU.mult)))
                link(dve.tensor_tensor(d, d, small[:, 16:20].unsqueeze(2).to_broadcast([P, N_DIFF, P]), ALU.mult))
                after(link(dve.tensor_tensor(s, s, small[:, 20:28].unsqueeze(2).to_broadcast([P, N_SB, HD]), ALU.mult)))
                link(dve.tensor_tensor(d, d, gd, ALU.mult))
                after(link(dve.tensor_tensor(s, s, gs, ALU.mult)))
                dve.sem_inc(head, 2)
                dve.sem_inc(o_ready[0], 1)
            dve_turn(dve, 0)
            dve_norm(dve, n_attn_post, n_ffn_pre.ready)
            dve_norm(dve, n_ffn_pre)
            dve_ffn(dve, 0, True)
            dve_norm(dve, n_ffn_post, n_ffn1.ready)
            dve_norm(dve, n_ffn1)
            dve_ffn(dve, 1, False)

            def residual(inst, norm):
                for at, k in enumerate(DOWN_ORDER):
                    dve.wait_ge(y_done[inst], at + 1)
                    dve.scalar_tensor_tensor(out=X[:, k, :], in0=PS[:, k, :], scalar=0.5, in1=X[:, k, :],
                                             op0=ALU.mult, op1=ALU.add).then_inc(norm.ready, 1)
            residual(1, n_mix)
            dve_norm(dve, n_mix)
            dve.wait_ge(const_done, 16)
            for h in range(N_NSA):
                f = -2.0 ** (-8.0 * (h + 1) / N_NSA) / SCALE
                link(dve.tensor_scalar(strip[:, h, :], L[:, 1, 0, :], f, None, ALU.mult))
                c = link(dve.tensor_scalar(swa_strip(h), WT[:, 1, 0:256], f, None, ALU.mult))
            c = link(dve.tensor_copy(cdist[:, :], L[:, 1, 1, 0:P]))
            after(c)
            dve.wait_ge(gate_e, 1)
            after(link(dve.tensor_scalar(gates[:, :, :], gates[:, :, :], 1.0, None, ALU.add)))
            after(link(dve.reciprocal(gates[:, :, :], gates[:, :, :])))
            for s in range(2):
                dve.wait_ge(cm["raw"], 64 * (s + 1))
                if s == 1:
                    dve.wait_ge(cm["kp_lo"], 1)
                whole = kpair
                win = bass.AP(tensor=whole.tensor, offset=whole.offset,
                              ap=[whole.ap[0], [2, 16], [T, 2], [CMP_STRIDE, NCMP]])
                pos = pc("pos_k" if s == 0 else "pos_v", 0, 16).unsqueeze(2).unsqueeze(3).to_broadcast([P, 16, 2, NCMP])
                dve.tensor_tensor(kp.rearrange("p j (g c) -> p j g c", g=2), win, pos, ALU.add).then_inc(cm["kp"], 1)
                dve.wait_ge(cm["kp_hi"], s + 1)
                dve.tensor_tensor(kp_lo, kp, kp_hi.bitcast(F32), ALU.subtract).then_inc(cm["kp_lo"], 1)
            dist = cdist[:, :].rearrange("p (i c) -> p i c", i=4)
            for g in range(2):
                dve.wait_ge(cm["s"], g + 1)
                z = cmp_L(g).rearrange("p (h i c) -> p h i c", h=4, i=4)
                zs = PS[:, g, :].rearrange("p (h i c) -> p h i c", h=4, i=4)
                after(link(dve.memset(cmp_L(g), 0.0)))
                for r in range(4):
                    h = 4 * g + r
                    f = -2.0 ** (-8.0 * (h + 1) / N_NSA) / SCALE
                    c = link(dve.scalar_tensor_tensor(out=z[:, r, :, 0:NCMP], in0=dist[:, :, 0:NCMP], scalar=f,
                                                      in1=zs[:, r, :, 0:NCMP], op0=ALU.mult, op1=ALU.add))
                after(c)
                zz = cmp_L(g).rearrange("p (h c) -> p h c", c=32)[:, :, 0:NCMP]
                mx = small[:, 32:48]
                after(link(dve.tensor_reduce(mx, zz, AX_X, ALU.max)))
                after(link(dve.tensor_scalar(mx, mx, MASKED / SCALE, None, ALU.max)))
                dve.tensor_tensor(zz, zz, mx.unsqueeze(2).to_broadcast([P, 16, NCMP]), ALU.subtract).then_inc(cm["l"], 1)
                dve.wait_ge(cm["e"], g + 1)
                after(link(dve.tensor_reduce(mx, zz, AX_X, ALU.add)))
                after(link(dve.tensor_scalar(mx, mx, 0.5, None, ALU.max)))
                after(link(dve.reciprocal(mx, mx)))
                gv = gates[:, :, 12 * g:12 * g + 12].rearrange("p i (r b) -> p r i b", b=3)[:, :, :, 0]
                m4 = mx.rearrange("p (r i) -> p r i", i=4)
                after(link(dve.tensor_tensor(m4, m4, gv, ALU.mult)))
                dve.tensor_tensor(zz, zz, mx.unsqueeze(2).to_broadcast([P, 16, NCMP]), ALU.mult).then_inc(cm["p"], 1)
            for i in range(TB):
                dve.wait_ge(cm["pv"], i + 1)
                dve.tensor_copy(O[:, i, 0:T], PS[:, i, :]).then_inc(cm["used"], 1)
            dve.wait_ge(cm["used"], TB)
            dve_attn(dve, at2, link, after)
            dve.sem_inc(o_ready[1], TB)
            dve_turn(dve, 1)
            for j in range(KC):
                dve.wait_ge(unit_done, U_WO2 + j + 1)
                dve.tensor_tensor(X[:, j, :], X[:, j, :], PS[:, j, :], ALU.add).then_inc(n_ffn2.ready, 1)
            dve_norm(dve, n_ffn2)
            dve_ffn(dve, 2, False)
            residual(2, n_final)
            dve_norm(dve, n_final)


def kernel(**inp):
    import concourse.bacc as bacc
    from concourse.bass_utils import run_bass_kernel_spmd

    f32 = np.float32

    def chunks(w):
        w = w.reshape(KC, P, -1, P)
        return w.transpose(2, 1, 0, 3).reshape(-1, P, UNIT)

    def by_token(w):
        wide = np.zeros((D, T), f32)
        wide[:, :w.shape[1]] = w
        return wide.reshape(4, 2, P, T).transpose(0, 2, 1, 3).reshape(4, P, UNIT)

    def up(w):
        w = w.reshape(D, 2, FC, P).transpose(0, 2, 1, 3).reshape(D, 2 * FF)
        return chunks(w)

    def pairs(w):
        return w.reshape(D, 2, 4, HD).transpose(0, 2, 1, 3).reshape(D, 8 * HD)

    def cmp1(w):
        return w.reshape(4, 4, P, CMP_HID).transpose(0, 2, 1, 3).reshape(4, P, UNIT)

    w = np.asarray(inp["w_qkv"][0])
    dq, dk, dv, sq_, sk, sv = np.split(w, 6, axis=1)
    qk = np.stack([a.reshape(D, 4, P) for a in (dq, dk, sq_, sk)], axis=2).reshape(D, 16 * P)
    m = np.asarray(inp["w_mix_in_2"][0])
    qa, kva, ga, qb, kvb = np.split(m, np.cumsum([512, 768, 24, 512]).tolist(), axis=1)
    kc, vcr, ks, vs, kw, vw = np.split(kva, 6, axis=1)
    kb, vb = np.split(kvb, 2, axis=1)
    mix_t = np.concatenate([pairs(qa), ks, kw, kc, vcr, pairs(qb), kb], axis=1)
    mix_n = np.concatenate([vs, vw, vb, ga], axis=1)
    weights = np.concatenate([
        chunks(qk), by_token(dv), by_token(sv), chunks(np.asarray(inp["w_o"][0])),
        up(np.asarray(inp["w_up"][0])), np.asarray(inp["w_down"][0]).reshape(FC, P, UNIT),
        up(np.asarray(inp["ffn1_w_in_2"][0])), np.asarray(inp["ffn1_w_out_2"][0]).reshape(FC, P, UNIT),
        chunks(mix_t), by_token(mix_n),
        cmp1(np.asarray(inp["cmp_k_w1_2"][0])), cmp1(np.asarray(inp["cmp_v_w1_2"][0])),
        chunks(np.asarray(inp["w_mix_out_2"][0])),
        up(np.asarray(inp["ffn2_w_in_2"][0])), np.asarray(inp["ffn2_w_out_2"][0]).reshape(FC, P, UNIT)], axis=0)
    assert weights.shape[0] == N_UNITS

    def cols(v):
        return np.asarray(v).reshape(-1, P).T

    params = np.concatenate(
        [cols(inp[n]) for n in ("attn_pre_norm", "attn_post_norm", "ffn_pre_norm", "ffn_post_norm",
                                "ffn1_norm_2", "mix_norm_2", "ffn2_norm_2", "final_norm_2", "conv_w", "conv_b",
                                "cmp_k_pos_2", "cmp_v_pos_2", "cmp_k_b1_2", "cmp_v_b1_2")]
        + [np.asarray(inp[n][0]).reshape(2, P, HD).transpose(1, 0, 2).reshape(P, 2 * HD)
           for n in ("cmp_k_w2_2", "cmp_v_w2_2")], axis=1)
    assert params.shape == (P, N_PARAMS)
    rows = np.concatenate([np.asarray(inp[n]).reshape(-1) for n in (
        "lambda_q1", "lambda_k1", "lambda_q2", "lambda_k2", "diff_subln", "sb_norm", "swa_sinks_2")])[None]
    x_t = np.asarray(inp["x"])[0].T.reshape(KC, P, T).transpose(1, 0, 2)
    arrays = {"weights": weights, "x_t": x_t, "params": params, "rows": rows, "table_t": np.asarray(inp["rel_bias"]).T}
    nc = bacc.Bacc("TRN2", target_bir_lowering=False, num_devices=1)
    args, given = [], {}
    for name, a in arrays.items():
        given["in_" + name] = np.ascontiguousarray(a)
        args.append(nc.dram_tensor("in_" + name, a.shape, F32, kind="ExternalInput").ap())
    args.append(nc.dram_tensor("bias_line", (N_DIFF, P, LINE + 1), F32, kind="Internal").ap())
    args.append(nc.dram_tensor("out_t", (P, KC, T), F32, kind="ExternalOutput").ap())
    build(nc, *args)
    r = run_bass_kernel_spmd(nc, [given], core_ids=[0])
    out = r.results[0]["out_t"]
    return np.ascontiguousarray(out.transpose(2, 1, 0).reshape(1, T, D))
```

```python
from contextlib import ExitStack
import math

import numpy as np

import concourse.bass as bass
from concourse import mybir

F32 = mybir.dt.float32
F32R = mybir.dt.float32r
I32 = mybir.dt.int32
ALU = mybir.AluOpType
ACT = mybir.ActivationFunctionType
AX_X = mybir.AxisListType.X

P = 128
T = 512
TB = T // P
D = 1024
KC = D // P
HD = 64
FF = 2816
FC = FF // P
UNIT = 1024
RING = 4
EPS = 1e-6
LAM_INIT = 0.8 - 0.6 * math.exp(-0.3 * 0)
SCALE = HD ** -0.5
MASKED = -1e30
FAR = 1e33
N_BUCKETS, MAX_DISTANCE = 32, 128
N_DIFF, N_SB, N_NSA, N_SWA = 4, 8, 8, 8
CMP_BLOCK, CMP_STRIDE, CMP_HID = 32, 16, 256
NCMP = (T - CMP_BLOCK) // CMP_STRIDE + 1
SWA_WINDOW = 128
LINE = T + P
NAT2 = 3 * P + 3 * N_NSA

U_QKV = 0
U_WO = U_QKV + 24
U_UP1 = U_WO + 8
U_DN1 = U_UP1 + 2 * FC
U_UP2 = U_DN1 + FC
U_DN2 = U_UP2 + 2 * FC
U_MIX = U_DN2 + FC
U_CMP = U_MIX + 17
U_WO2 = U_CMP + 8
U_UP3 = U_WO2 + 8
U_DN3 = U_UP3 + 2 * FC
N_UNITS = U_DN3 + FC

PARAMS = {}
_at = 0
for _name, _n in (("attn_pre", KC), ("attn_post", KC), ("ffn_pre", KC), ("ffn_post", KC),
                  ("ffn1", KC), ("mix", KC), ("ffn2", KC), ("final", KC),
                  ("conv_w", 3 * 2 * FC), ("conv_b", 2 * FC), ("pos_k", 16), ("pos_v", 16),
                  ("b1_k", 2), ("b1_v", 2), ("w2_k", 2 * HD), ("w2_v", 2 * HD)):
    PARAMS[_name] = (_at, _n)
    _at += _n
N_PARAMS = _at
ROW_LAM, ROW_SUB, ROW_SBN, ROW_SINK = 0, 4 * HD, 4 * HD + 2 * HD, 4 * HD + 3 * HD
N_ROW = ROW_SINK + N_SWA

FIRST_ORDER = [4, 5, 6, 7, 0, 1, 2, 3]


def bucket_runs():
    exact = N_BUCKETS // 2
    runs = [(b, b, b) for b in range(exact)]
    d = np.arange(exact, T)
    large = exact + (np.log(d.astype(np.float32) / exact) / math.log(MAX_DISTANCE / exact)
                     * (N_BUCKETS - exact)).astype(np.int32)
    large = np.minimum(large, N_BUCKETS - 1)
    for b in range(exact, N_BUCKETS):
        at = d[large == b]
        if len(at):
            runs.append((b, int(at[0]), int(at[-1])))
    return runs


def build(nc, weights, x_t, params, rows, table_t, bias_line, out_t):
    with ExitStack() as top:
        def sem(name):
            return top.enter_context(nc.semaphore(name))

        def sb(name, shape, dtype=F32, ctx=top):
            return ctx.enter_context(nc.sbuf_tensor(name, shape, dtype))

        stage = sb("stage", [P, RING, UNIT])
        w_hi = sb("w_hi", [P, RING, UNIT], F32R)
        w_lo = sb("w_lo", [P, RING, UNIT], F32R)
        X = sb("X", [P, KC, T])
        par = sb("par", [P, N_PARAMS])
        row = sb("row", [P, N_ROW])
        ones = sb("ones", [P, P])
        ident = sb("ident", [P, P])
        epsc = sb("epsc", [P, 1])
        sq = sb("sq", [P, 2, T])
        rstd = sb("rstd", [P, T])
        tmp = sb("tmp", [P, 2, T])
        rcol = sb("rcol", [P, TB])
        with ExitStack() as scope:
            Y2 = sb("Y2", [P, KC, T], ctx=scope)
        H_hi = sb("H_hi", [P, KC, T], F32R)
        H_lo = sb("H_lo", [P, KC, T], F32R)
        with ExitStack() as scope:
            A_hi = sb("A_hi", [P, FC, T], F32R, scope)
            A_lo = sb("A_lo", [P, FC, T], F32R, scope)
            conv = sb("conv", [P, 2, 2, T], ctx=scope)
        with ExitStack() as scope:
            with ExitStack() as inner:
                kp_hi_flat = sb("kp_hi", [P, 2 * T], F32R, inner)
                kp_lo_flat = sb("kp_lo", [P, 2 * T], F32R, inner)
            L1 = sb("L1", [P, 2, T], ctx=scope)
            scratch = sb("scratch", [P, 2 * T], ctx=scope)
            QK = sb("QK", [P, 16, T], ctx=scope)
            V = sb("V", [P, 2, TB, T], ctx=scope)
            O = sb("O", [P, TB, D], ctx=scope)
            strip = sb("strip", [P, 8, T], ctx=scope)
            L0 = sb("L0", [P, 2, T], ctx=scope)
            stat = sb("stat", [P, 4, 8], ctx=scope)
            small = sb("small", [P, 64], ctx=scope)
            tab = sb("tab", [N_DIFF, N_BUCKETS], ctx=scope)
            gates = sb("gates", [P, TB, 3 * N_NSA], ctx=scope)
            cdist = sb("cdist", [P, P], ctx=scope)
            hid = sb("hid", [P, 2, 2, 2 * NCMP], ctx=scope)
            kcT = sb("kcT", [P, 32], ctx=scope)
            vc = sb("vc", [P, 2, HD], ctx=scope)
            ident_r = sb("ident_r", [P, P], F32R, scope)
            mask_r = sb("mask_r", [P, P], F32R, scope)
        W, WT = sq, tmp
        line = O[0:N_DIFF, 0, 0:LINE]
        kpair = V[:, 1, 0:2, :]

        def as_windows(t):
            return t[:, 0:16 * 2 * NCMP].rearrange("p (j n) -> p j n", j=16)

        kp_hi, kp_lo = as_windows(kp_hi_flat), as_windows(kp_lo_flat)
        kp = as_windows(sq.rearrange("p a n -> p (a n)"))

        K2 = [H_hi[:, t, :] for t in range(6)]
        QD_hi = [H_lo[:, t, :] for t in range(4)]
        QD_lo = [H_lo[:, 4 + t, :] for t in range(4)]

        def LM(m, n):
            return (L0, L1)[m][:, n % 2, :]

        hidden = L0[0:2 * NCMP, 1, 0:CMP_HID]

        def cmp_L(g):
            return L1[:, g, :]

        def cmp_PT(h):
            return scratch[:, bass.ts(h, P)]

        def swa_strip(h):
            home = QK[:, 13 + h // 2, :] if h < 6 else V[:, 1, 2, :]
            return home[:, (h % 2) * 256:(h % 2 + 1) * 256]

        PS = top.enter_context(nc.psum_tensor("PS", [P, 8, T], F32))

        def pc(name, k, n=1):
            a, _ = PARAMS[name]
            return par[:, a + k:a + k + n]

        loaded = [sem(f"loaded{i}") for i in range(RING)]
        hi_done = sem("hi_done")
        lo_done = sem("lo_done")
        unit_done = sem("unit_done")
        x_loaded, par_loaded, row_loaded, tab_loaded = map(sem, ("x_loaded", "par_loaded", "row_loaded", "tab_loaded"))
        const_done = sem("const_done")
        dve_self = sem("dve_self")
        act_self = sem("act_self")
        line_out = sem("line_out")
        out_done = [sem("out_done0"), sem("out_done1")]

        block = top.enter_context(nc.Block())

        norm_summed = sem("norm_summed")
        norm_root = sem("norm_root")
        norm_inverse = sem("norm_inverse")

        class Norm:

            def __init__(self, name, at, kind, src, before=None):
                self.name, self.at, self.src, self.before = name, at, src, before
                if before is None:
                    self.ready = sem(f"{name}_ready")
                self.squared = sem(f"{name}_squared")
                self.added = sem(f"{name}_added")
                if kind == "fold":
                    self.hi = sem(f"{name}_hi")
                    self.done = sem(f"{name}_done")
                else:
                    self.scaled = sem(f"{name}_scaled")
                if kind == "post":
                    self.even = sem(f"{name}_even")
                    self.odd = sem(f"{name}_odd")

            def wait_ready(self, eng, k):
                if self.before is None:
                    eng.wait_ge(self.ready, k + 1)
                else:
                    eng.wait_ge(self.before.odd if k % 2 else self.before.even, k // 2 + 1)

        n_attn_pre = Norm("attn_pre", 1, "fold", X)
        n_attn_post = Norm("attn_post", 2, "post", QK)
        n_ffn_pre = Norm("ffn_pre", 3, "fold", X, n_attn_post)
        n_ffn_post = Norm("ffn_post", 4, "post", Y2)
        n_ffn1 = Norm("ffn1", 5, "fold", X, n_ffn_post)
        n_mix = Norm("mix", 6, "fold", X)
        n_ffn2 = Norm("ffn2", 7, "fold", X)
        n_final = Norm("final", 8, "final", X)
        STAT = 7

        def act_square(act, n, k):
            if k >= 2:
                act.wait_ge(n.added, max(1, k - 2))
            if n.src is not X:
                act.wait_ge(n.ready, k + 1)
            act.activation(sq[:, k % 2, :], n.src[:, k, :], ACT.Square).then_inc(n.squared, 1)

        def act_root(act, n):
            act.preload_act_table_set("sqrt_and_others")
            act.wait_ge(norm_summed, n.at)
            act.activation(rstd[:, :], PS[:, STAT, :], ACT.Sqrt, bias=epsc[:, 0:1]).then_inc(norm_root, 1)

        def pool_sum(pool, n, between=None):
            for k in range(KC):
                if between:
                    between(k)
                if k == 0:
                    continue
                pool.wait_ge(n.squared, k + 1)
                if k >= 2:
                    pool.wait_ge(n.added, k - 1)
                pool.tensor_tensor(rstd[:, :], sq[:, 0, :] if k == 1 else rstd[:, :], sq[:, k % 2, :],
                                   ALU.add).then_inc(n.added, 1)

        def pe_stat(pe, n):
            pe.wait_ge(n.added, KC - 1)
            pe.matmul(PS[:, STAT, :], ones[:, :], rstd[:, :], start=True, stop=True).then_inc(norm_summed, 1)

        def dve_inverse(dve, n):
            dve.wait_ge(norm_root, n.at)
            dve.reciprocal(rstd[:, :], rstd[:, :]).then_inc(norm_inverse, 1)

        def act_fold(act, n, unit=None):
            for k in range(KC):
                n.wait_ready(act, k)
                act.activation(H_hi[:, k, :], X[:, k, :], ACT.Copy, scale=pc(n.name, k)).then_inc(n.hi, 1)
            if unit is not None:
                act_hi_static(act, unit)
            for k in range(KC):
                act_square(act, n, k)
            act_root(act, n)

        def dve_fold(dve, n):
            for k in range(KC):
                dve.wait_ge(n.hi, k + 1)
                dve.scalar_tensor_tensor(out=H_lo[:, k, :], in0=X[:, k, :], scalar=pc(n.name, k),
                                         in1=H_hi[:, k, :].bitcast(F32), op0=ALU.mult,
                                         op1=ALU.subtract).then_inc(n.done, 1)
            dve_inverse(dve, n)
            dve.wait_ge(norm_inverse, n.at)

        def pe_first_pair(pe, n, u0):
            pe.wait_ge(lo_done, u0 + 2)
            for k in range(KC):
                pe.wait_ge(n.hi, max(k + 1, 2))
                for j in range(2):
                    for w in (w_hi, w_lo):
                        pe.matmul(PS[:, j, :], w[:, (u0 + j) % RING, bass.ts(k, P)], H_hi[:, k, :],
                                  start=(k == 0 and w is w_hi), stop=False)
            for j in range(2):
                for k in range(KC):
                    if j == 0:
                        pe.wait_ge(n.done, k + 1)
                    m = pe.matmul(PS[:, j, :], w_hi[:, (u0 + j) % RING, bass.ts(k, P)], H_lo[:, k, :],
                                  start=False, stop=(k == KC - 1))
                m.then_inc(unit_done, 1)

        def dve_post(dve, n):
            dve_inverse(dve, n)
            dve.wait_ge(norm_inverse, n.at)
            for k in range(KC):
                if k >= 2:
                    dve.wait_ge(n.odd if k % 2 else n.even, k // 2)
                dve.scalar_tensor_tensor(out=tmp[:, k % 2, :], in0=n.src[:, k, :], scalar=pc(n.name, k),
                                         in1=rstd[:, :], op0=ALU.mult, op1=ALU.mult).then_inc(n.scaled, 1)
                if k % 2:
                    dve.wait_ge(n.scaled, k + 1)
                    dve.tensor_tensor(X[:, k, :], X[:, k, :], tmp[:, 1, :], ALU.add).then_inc(n.odd, 1)

        def pool_post(pool, n):
            for k in range(0, KC, 2):
                pool.wait_ge(n.scaled, k + 1)
                pool.tensor_tensor(X[:, k, :], X[:, k, :], tmp[:, 0, :], ALU.add).then_inc(n.even, 1)

        def split_matmul(pe, out, w_slot, w_cols, h_hi, h_lo, first, last, skip=False):
            a, b = w_hi[:, w_slot, w_cols], w_lo[:, w_slot, w_cols]
            pe.matmul(out, a, h_hi, start=first, stop=False, skip_group_check=skip)
            pe.matmul(out, a, h_lo, start=False, stop=False, skip_group_check=skip)
            return pe.matmul(out, b, h_hi, start=False, stop=last, skip_group_check=skip)

        def pe_chunk(pe, slot, bank):
            for k in range(KC):
                m = split_matmul(pe, PS[:, bank, :], slot, bass.ts(k, P), H_hi[:, k, :], H_lo[:, k, :],
                                 k == 0, k == KC - 1)
            m.then_inc(unit_done, 1)

        def pe_by_token(pe, u0, bank0, width, free=None):
            for t in range(4):
                u = u0 + t
                pe.wait_ge(lo_done, u + 1)
                for tb in range(TB):
                    for kk in range(2):
                        k = 2 * t + kk
                        wh = w_hi[:, u % RING, kk * T:kk * T + width]
                        wl = w_lo[:, u % RING, kk * T:kk * T + width]
                        hh, hl = H_hi[:, k, bass.ts(tb, P)], H_lo[:, k, bass.ts(tb, P)]
                        o = PS[:, bank0 + tb, 0:width]
                        pe.matmul(o, hh, wh, start=(k == 0), stop=False)
                        pe.matmul(o, hh, wl, start=False, stop=False)
                        m = pe.matmul(o, hl, wh, start=False, stop=(k == KC - 1))
                m.then_inc(unit_done, 1)

        def act_hi(act, slot, u=None, n_loaded=None, wait_free=True):
            if wait_free:
                act.wait_ge(unit_done, u - RING + 1)
            act.wait_ge(loaded[slot], n_loaded)
            act.activation(w_hi[:, slot, :], stage[:, slot, :], ACT.Copy).then_inc(hi_done, 1)

        def act_hi_static(act, u):
            v = u + RING
            if v < N_UNITS:
                act_hi(act, v % RING, v, 16 * (v // RING + 1))
            else:
                act.wait_ge(unit_done, u + 1)

        ffn_free = sem("ffn_free")
        zs = sem("zs")
        conv_in = sem("conv_in")
        conv_step = sem("conv_step")
        gated = sem("gated")
        prod = sem("prod")
        y_done = [sem(f"y_done{i}") for i in range(3)]

        def pe_ffn(pe, inst, u_up, u_dn, norm):
            g0 = inst * FC
            pe_first_pair(pe, norm, u_up)
            pe_stat(pe, norm)
            for i in range(2, 4):
                pe.wait_ge(lo_done, u_up + i + 1)
                if i == 2:
                    pe.wait_ge(ffn_free, g0 + 2)
                pe_chunk(pe, (u_up + i) % RING, i)
            with pe.Fori(1, FC // 2) as r:
                for i in range(4):
                    pe.wait_ge(lo_done, r * 4 + (u_up + i + 1))
                    if i % 2 == 0:
                        pe.wait_ge(ffn_free, r * 2 + (g0 + i // 2 + 1))
                    pe_chunk(pe, (u_up + i) % RING, i)

            def down(slot, a_hi, a_lo, first, last):
                for at, m in enumerate(FIRST_ORDER if first else range(KC)):
                    if first and at == 4:
                        pe.wait_ge(ffn_free, g0 + FC + 2)
                    mm = split_matmul(pe, PS[:, m, :], slot, bass.ts(m, P), a_hi, a_lo, first, last)
                    if last:
                        mm.then_inc(y_done[inst], 1)
                if not last:
                    mm.then_inc(unit_done, 1)
                else:
                    pe.wait_ge(y_done[inst], KC)
                    pe.sem_inc(unit_done, 1)

            pe.wait_ge(lo_done, u_dn + 1)
            down(u_dn % RING, A_hi[:, 0, :], A_lo[:, 0, :], True, False)
            with pe.Fori(0, (FC - 2) // 4) as r:
                for i in range(4):
                    pe.wait_ge(lo_done, r * 4 + (u_dn + i + 2))
                    f = bass.ds(r * 4 + (i + 1), 1)
                    down((u_dn + i + 1) % RING, A_hi[:, f, :].rearrange("p a n -> p (a n)"),
                         A_lo[:, f, :].rearrange("p a n -> p (a n)"), False, False)
            pe.wait_ge(lo_done, u_dn + FC)
            down((u_dn + FC - 1) % RING, A_hi[:, FC - 1, :], A_lo[:, FC - 1, :], False, True)

        def act_ffn(act, inst, u_up, u_dn, convolved):
            g0 = inst * FC
            with act.Fori(0, FC // 2) as r:
                for i in range(2):
                    ua, ub = u_up + 2 * i, u_up + 2 * i + 1
                    act.wait_ge(unit_done, r * 4 + (ub + 1))
                    act.wait_ge(ffn_free, r * 2 + (g0 + i + 1))
                    va, vb = ua + RING, ub + RING
                    act_hi(act, va % RING, None, r * 16 + 16 * (va // RING + 1), wait_free=False)
                    fe = r * 2 + i
                    if convolved:
                        act.wait_ge(zs, r * 4 + (2 * g0 + 2 * i + 2))
                    act_hi(act, vb % RING, None, r * 16 + 16 * (vb // RING + 1), wait_free=False)
                    if convolved:
                        for j in range(2):
                            c2 = par[:, bass.ds(fe + (PARAMS["conv_w"][0] + (2 * 2 + j) * FC), 1)]
                            cb = par[:, bass.ds(fe + (PARAMS["conv_b"][0] + j * FC), 1)]
                            act.activation(conv[:, i, j, :], tmp[:, j, :], ACT.Identity,
                                           bias=cb, scale=c2).then_inc(conv_in, 1)
                        act.wait_ge(conv_step, r * 8 + 4 * i + 3)
                        act.activation(conv[:, i, 0, :], conv[:, i, 0, :], ACT.Gelu_apprx_tanh).then_inc(gated, 1)
                    else:
                        act.wait_ge(zs, r * 4 + (2 * g0 + 2 * i + 1))
                        act.activation(conv[:, i, 0, :], conv[:, i, 0, :], ACT.Silu).then_inc(gated, 1)
            rounds = FC // 4 if u_dn + FC < N_UNITS else FC // 4 - 1
            with act.Fori(0, rounds) as r:
                for i in range(4):
                    v = u_dn + i + RING
                    act_hi(act, v % RING, r * 4 + v, r * 16 + 16 * (v // RING + 1))
            for u in range(u_dn + rounds * 4, u_dn + FC - 1):
                act_hi_static(act, u)

        def dve_ffn(dve, inst, u_up, convolved):
            g0 = inst * FC
            with dve.Fori(0, FC // 2) as r:
                for i in range(2):
                    fe = r * 2 + i
                    z = [tmp[:, j, :] if convolved else conv[:, i, j, :] for j in range(2)]
                    dve.wait_ge(ffn_free, r * 2 + (g0 + i + 1))
                    dve.wait_ge(unit_done, r * 4 + (u_up + 2 * i + 2))
                    for j in range(2):
                        dve.tensor_tensor(z[j], PS[:, 2 * i + j, :], rstd[:, :], ALU.mult).then_inc(zs, 1)
                    if convolved:
                        def tap(back, j):
                            c = par[:, bass.ds(fe + (PARAMS["conv_w"][0] + (2 * (2 - back) + j) * FC), 1)]
                            y = conv[:, i, j, back:T]
                            dve.scalar_tensor_tensor(out=y, in0=z[j][:, 0:T - back], scalar=c, in1=y,
                                                     op0=ALU.mult, op1=ALU.add).then_inc(conv_step, 1)
                        for j in range(2):
                            dve.wait_ge(conv_in, r * 4 + 2 * i + j + 1)
                            tap(1, j)
                        for j in range(2):
                            dve.wait_ge(conv_step, r * 8 + 4 * i + j + 1)
                            tap(2, j)
                        dve.wait_ge(conv_step, r * 8 + 4 * i + 4)
                    value = conv[:, i, 1, :]
                    dve.wait_ge(zs, r * 4 + (2 * g0 + 2 * i + 2))
                    dve.wait_ge(gated, r * 2 + (g0 + i + 1))
                    f = bass.ds(fe, 1)
                    ah = A_hi[:, f, :].rearrange("p a n -> p (a n)")
                    al = A_lo[:, f, :].rearrange("p a n -> p (a n)")
                    dve.tensor_tensor(ah, conv[:, i, 0, :], value, ALU.mult).then_inc(prod, 1)
                    dve.tensor_tensor(conv[:, i, 0, :], conv[:, i, 0, :], value, ALU.mult).then_inc(prod, 1)
                    dve.wait_ge(prod, r * 4 + (2 * g0 + 2 * i + 2))
                    dve.tensor_tensor(al, conv[:, i, 0, :], ah.bitcast(F32), ALU.subtract).then_inc(ffn_free, 1)

        class Item:

            def __init__(self, kind, i, keys, group, maps, v, out, bias=None, add=False, gate=None, sink=None):
                self.kind, self.i, self.group, self.maps, self.v, self.out = kind, i, group, maps, v, out
                self.k0, self.nk = keys
                self.bias, self.add, self.gate, self.sink = bias, add, gate, sink

        def full(i):
            return 0, (i + 1) * P, (TB - 1 - i) * P

        def qk_tiles(qt, kt, i, k0, nk):
            return [(QD_hi[qt][:, bass.ts(i, P)], K2[kt][:, k0:k0 + nk]),
                    (QD_lo[qt][:, bass.ts(i, P)], K2[kt][:, k0:k0 + nk])]

        def item(items, **what):
            items.append(Item(**what))

        items1, items2, groups1, groups2 = [], [], [], []
        for p in range(8):
            c, t0 = p // 2, 2 * (p % 2)
            groups1.append(len(items1))
            for i in range(TB):
                k0, nk, s0 = full(i)
                if p % 2 == 0:
                    item(items1, kind="diff", i=i, keys=(k0, nk), group=p,
                         maps=[qk_tiles(t0 + m, t0 + m, i, k0, nk) for m in range(2)],
                         bias=strip[:, c, s0:s0 + nk],
                         v=[V[:, 0, kb, bass.ts(c, P)] for kb in range(nk // P)],
                         out=O[:, i, bass.ts(c, P)])
                else:
                    for m in range(2):
                        h = 2 * c + m
                        item(items1, kind="sb", i=i, keys=(k0, nk), group=p,
                             maps=[qk_tiles(t0 + m, t0 + m, i, k0, nk)],
                             v=[V[:, 1, kb, bass.ts(h, HD)] for kb in range(nk // P)],
                             out=O[:, i, T + h * HD:T + (h + 1) * HD])
        for p in range(8):
            c, t0 = p % 4, 2 * (p % 2)
            groups2.append(len(items2))
            for i in range(TB):
                for g in range(2):
                    h = 4 * g + c
                    if p < 4:
                        k0, nk, s0 = full(i)
                        for branch in range(2):
                            item(items2, kind="soft", i=i, keys=(k0, nk), group=p,
                                 maps=[qk_tiles(t0 + g, 2 * branch + g, i, k0, nk)],
                                 bias=strip[:, h, s0:s0 + nk],
                                 v=[V[:, 0, kb, branch * P + g * HD:branch * P + (g + 1) * HD] for kb in range(nk // P)],
                                 out=O[:, i, bass.ts(h, HD)], add=True,
                                 gate=gates[:, i, 3 * h + 1 + branch:3 * h + 2 + branch], sink=None)
                    else:
                        k0, nk = max(i - 1, 0) * P, min(i + 1, 2) * P
                        item(items2, kind="soft", i=i, keys=(k0, nk), group=p,
                             maps=[qk_tiles(t0 + g, 4 + g, i, k0, nk)],
                             bias=swa_strip(h)[:, 256 - nk:256],
                             v=[V[:, 0, k0 // P + kb, 2 * P + g * HD:2 * P + (g + 1) * HD] for kb in range(nk // P)],
                             out=O[:, i, T + h * HD:T + (h + 1) * HD], add=False, gate=None,
                             sink=row[:, ROW_SINK + h:ROW_SINK + h + 1])
        for items in (items1, items2):
            pre = 0
            for n, it in enumerate(items):
                it.n = n
                it.dv = it.out.shape[-1]
                it.st = stat[:, n % 4, :]
                pre += it.kind == "sb"
                it.pre = pre

        class Attn:
            def __init__(self, name, items, groups, scale):
                self.name, self.items, self.groups, self.scale = name, items, groups, scale
                self.preps = []
                self.prep_hi = sem(f"{name}_prep_hi")
                self.prep_lo = sem(f"{name}_prep_lo")
                self.moved = [sem(f"{name}_moved{i}") for i in range(4)]
                self.hooks = {"pe": {}, "act": {}, "dve": {}}
                self.qk_done = sem(f"{name}_qk_done")
                self.s_read = sem(f"{name}_s_read")
                self.pre_done = sem(f"{name}_pre_done")
                self.logits = sem(f"{name}_logits")
                self.exp_done = sem(f"{name}_exp_done")
                self.comb = sem(f"{name}_comb")
                self.turned = sem(f"{name}_turned")
                self.wt_ready = sem(f"{name}_wt_ready")
                self.pv_done = sem(f"{name}_pv_done")
                self.o_done = sem(f"{name}_o_done")

        at1 = Attn("at1", items1, groups1, 1.0)
        at2 = Attn("at2", items2, groups2, SCALE)

        class Prep:

            def __init__(self, a, chunk, keys, tiles, slot, group, free_after=0):
                n = len(a.preps)
                self.a, self.chunk, self.keys, self.tiles, self.slot, self.group = a, chunk, keys, tiles, slot, group
                self.free_after = free_after
                self.n = n
                self.moved = a.moved[n % 4]
                self.moves = 4 if keys else 8
                self.count = 16 * self.moves + (a.preps[n - 4].count if n >= 4 else 0)
                self.after = []
                a.preps.append(self)

            def act_split(self, act):
                for q in self.after:
                    act.wait_ge(q.moved, q.count)
                act.activation(self.slot[0], QK[:, self.chunk, :], ACT.Copy).then_inc(self.a.prep_hi, 1)

            def dve_split(self, dve):
                dve.wait_ge(self.a.prep_hi, self.n + 1)
                dve.tensor_tensor(self.slot[1], QK[:, self.chunk, :], self.slot[0].bitcast(F32),
                                  ALU.subtract).then_inc(self.a.prep_lo, 1)

            def move(self, eng):
                eng.wait_ge(self.a.prep_lo, self.n + 1)
                if self.free_after:
                    eng.wait_ge(self.a.qk_done, self.free_after)
                hi, lo = self.slot
                for m in range(2):
                    rows = slice(m * HD, (m + 1) * HD)
                    if self.keys:
                        to = [(K2[self.tiles[m]], hi, 0), (K2[self.tiles[m]], lo, 1)]
                    else:
                        to = [(QD_hi[self.tiles[m]], hi, 0), (QD_hi[self.tiles[m]], hi, 1),
                              (QD_lo[self.tiles[m]], lo, 0), (QD_lo[self.tiles[m]], lo, 1)]
                    for dst, src, half in to:
                        eng.dma_start(dst[half * HD:(half + 1) * HD, :].bitcast(F32),
                                      src[rows, :].bitcast(F32)).then_inc(self.moved, 16)

        def hook(a, engine, step, what):
            a.hooks[engine].setdefault(step, []).append(what)

        slots1 = [(H_hi[:, 6, :], H_hi[:, 7, :]), (H_hi[:, 4, :], H_hi[:, 5, :])]
        for p in range(8):
            for keys in (False, True):
                q = Prep(at1, 2 * p + keys, keys, [2 * (p % 2), 2 * (p % 2) + 1], slots1[keys], p,
                         groups1[p - 1] if p >= 2 else 0)
                if p:
                    q.after = [at1.preps[2 * (p - 1) + keys]]
                if p >= 1:
                    step = groups1[p - 1]
                    hook(at1, "act", step, q.act_split)
                    hook(at1, "dve", step, q.dve_split)
        slot_a, slot_b, slot_c = (H_hi[:, 6, :], H_hi[:, 7, :]), (QD_hi[2], QD_hi[3]), (QD_lo[2], QD_lo[3])
        q0 = Prep(at2, 0, False, [0, 1], slot_a, 0)
        ks_, kw_ = Prep(at2, 4, True, [0, 1], slot_b, 0), Prep(at2, 5, True, [2, 3], slot_c, 0)
        last = q0
        for p in range(1, 8):
            c = p if p < 4 else 8 + p - 4
            q = Prep(at2, c, False, [2 * (p % 2), 2 * (p % 2) + 1], slot_a, p, groups2[p - 1] if p >= 2 else 0)
            q.after = [last] + ([ks_, kw_] if p == 1 else [])
            last = q
            step = groups2[p - 1] + 1
            hook(at2, "act", step, q.act_split)
            hook(at2, "dve", step, q.dve_split)
            if p == 3:
                kb_ = Prep(at2, 12, True, [4, 5], slot_a, 4)
                kb_.after = [last]
                last = kb_
                hook(at2, "act", step + 6, kb_.act_split)
                hook(at2, "dve", step + 6, kb_.dve_split)
        v_ready = [sem("v_ready1"), sem("v_ready2")]
        strips_done = [sem("strips_done1"), sem("strips_done2")]

        def pe_attn(pe, a):
            items = a.items
            for n in range(len(items) + 3):
                if n < len(items):
                    it = items[n]
                    if n >= 2:
                        pe.wait_ge(a.s_read, n - 1)
                    if n in a.groups:
                        for q in a.preps:
                            if q.group == it.group:
                                pe.wait_ge(q.moved, q.count)
                    for m, passes in enumerate(it.maps):
                        for x, (q, k) in enumerate(passes):
                            mm = pe.matmul(PS[:, 2 * (n % 2) + m, 0:it.nk], q, k, start=(x == 0), stop=(x == 1))
                            if x == 0 and it.kind == "sb":
                                pe.matmul(PS[:, 2 * (n % 2) + m, it.nk - P:it.nk], ident_r[:, :], mask_r[:, :],
                                          start=False, stop=False)
                    mm.then_inc(a.qk_done, 1)
                if 2 <= n < len(items) + 2:
                    it = items[n - 2]
                    pe.wait_ge(a.comb if it.kind == "diff" else a.exp_done, it.n + 1)
                    if it.n >= 2:
                        pe.wait_ge(a.wt_ready, it.n - 1)
                    for kb in range(it.nk // P):
                        mm = pe.transpose(PS[:, 4 + it.n % 2, bass.ts(kb, P)], W[:, it.n % 2, bass.ts(kb, P)], ident[:, :])
                    mm.then_inc(a.turned, 1)
                if n >= 3:
                    it = items[n - 3]
                    pe.wait_ge(a.wt_ready, it.n + 1)
                    if it.n >= 2:
                        pe.wait_ge(a.o_done, it.n - 1)
                    for kb in range(it.nk // P):
                        mm = pe.matmul(PS[:, 6 + it.n % 2, 0:it.dv], WT[:, it.n % 2, bass.ts(kb, P)], it.v[kb],
                                       start=(kb == 0), stop=(kb == it.nk // P - 1))
                    mm.then_inc(a.pv_done, 1)
                for what in a.hooks["pe"].get(n, []):
                    what(pe)

        def act_attn(act, a, link, after):
            items = a.items
            for n in range(len(items) + 2):
                if n < len(items) and items[n].kind == "sb":
                    it = items[n]
                    if n >= 2:
                        act.wait_ge(a.comb if items[n - 2].kind == "diff" else a.logits, n - 1)
                    act.wait_ge(a.qk_done, n + 1)
                    z = LM(0, n)[:, 0:it.nk]
                    c = link(act.activation(z, PS[:, 2 * (n % 2), 0:it.nk], ACT.Abs))
                    after(c)
                    c = link(act.activation(z, z, ACT.Exp, scale=-1.0))
                    after(c)
                    act.activation(z, z, ACT.Ln, bias=1.0).then_inc(a.pre_done, 1)
                if 1 <= n < len(items) + 1:
                    it = items[n - 1]
                    if it.kind != "diff" and it.n >= 2:
                        act.wait_ge(a.turned, it.n - 1)
                    act.wait_ge(a.logits, it.n + 1)
                    if it.kind == "sb":
                        act.activation(W[:, it.n % 2, 0:it.nk], LM(1, it.n)[:, 0:it.nk], ACT.Exp).then_inc(a.exp_done, 1)
                    elif it.kind == "diff":
                        for m in range(2):
                            z = LM(m, it.n)[:, 0:it.nk]
                            x = act.activation(z, z, ACT.Exp, bias=it.st[:, 2 + m:3 + m], accum_out=it.st[:, 4 + m:5 + m])
                        x.then_inc(a.exp_done, 1)
                    else:
                        if it.sink is not None:
                            act.activation(it.st[:, 5:6], it.sink, ACT.Exp, bias=it.st[:, 2:3])
                        act.activation(W[:, it.n % 2, 0:it.nk], LM(0, it.n)[:, 0:it.nk], ACT.Exp,
                                       bias=it.st[:, 2:3], accum_out=it.st[:, 4:5]).then_inc(a.exp_done, 1)
                if n >= 2:
                    it = items[n - 2]
                    act.wait_ge(a.turned, it.n + 1)
                    if it.n >= 2:
                        act.wait_ge(a.pv_done, it.n - 1)
                    act.activation(WT[:, it.n % 2, 0:it.nk], PS[:, 4 + it.n % 2, 0:it.nk], ACT.Copy).then_inc(a.wt_ready, 1)
                for what in a.hooks["act"].get(n, []):
                    what(act)

        def dve_attn(dve, a, link, after):
            items = a.items
            for n in range(len(items) + 4):
                if n < len(items):
                    it = items[n]
                    dve.wait_ge(a.qk_done, n + 1)
                    if n >= 2:
                        dve.wait_ge(a.exp_done, n - 1)
                        dve.wait_ge(a.comb, n - 1)
                    S = PS[:, 2 * (n % 2), 0:it.nk]
                    if it.kind == "sb":
                        dve.wait_ge(a.pre_done, it.pre)
                        u, z = LM(0, n)[:, 0:it.nk], LM(1, n)[:, 0:it.nk]
                        c = link(dve.scalar_tensor_tensor(out=u, in0=S, scalar=0.0, in1=u, op0=ALU.max, op1=ALU.add))
                        after(c)
                        c = link(dve.tensor_tensor_scan(z[:, ::-1], u[:, ::-1], u[:, ::-1], 0.0, ALU.add, ALU.max))
                        after(c)
                        dve.tensor_tensor(z, S, z, ALU.subtract).then_inc(a.logits, 1)
                        dve.wait_ge(a.logits, n + 1)
                        dve.sem_inc(a.s_read, 1)
                    else:
                        for m in range(len(it.maps)):
                            c = link(dve.tensor_tensor_reduce(
                                out=LM(m, n)[:, 0:it.nk], in0=PS[:, 2 * (n % 2) + m, 0:it.nk], in1=it.bias,
                                scale=a.scale, scalar=-3e38, op0=ALU.add, op1=ALU.max, accum_out=it.st[:, m:m + 1]))
                        after(c)
                        dve.sem_inc(a.s_read, 1)
                        nm = len(it.maps)
                        if it.kind == "soft" and it.sink is not None:
                            dve.tensor_scalar(it.st[:, 2:3], it.st[:, 0:1], it.sink, -1.0, ALU.max, ALU.mult).then_inc(a.logits, 1)
                        else:
                            dve.tensor_scalar(it.st[:, 2:2 + nm], it.st[:, 0:nm], -1.0, None, ALU.mult).then_inc(a.logits, 1)
                if 1 <= n < len(items) + 1:
                    it = items[n - 1]
                    dve.wait_ge(a.exp_done, it.n + 1)
                    if it.kind == "sb":
                        dve.sem_inc(a.comb, 1)
                    elif it.kind == "diff":
                        if it.n >= 2:
                            dve.wait_ge(a.turned, it.n - 1)
                        c = link(dve.reciprocal(it.st[:, 6:8], it.st[:, 4:6]))
                        after(c)
                        c = link(dve.tensor_tensor(it.st[:, 7:8], it.st[:, 7:8], small[:, 0:1], ALU.mult))
                        after(c)
                        z0, z1 = LM(0, it.n)[:, 0:it.nk], LM(1, it.n)[:, 0:it.nk]
                        c = link(dve.tensor_scalar(z1, z1, it.st[:, 7:8], None, ALU.mult))
                        after(c)
                        dve.scalar_tensor_tensor(out=W[:, it.n % 2, 0:it.nk], in0=z0, scalar=it.st[:, 6:7], in1=z1,
                                                 op0=ALU.mult, op1=ALU.add).then_inc(a.comb, 1)
                    else:
                        if it.sink is not None:
                            after(link(dve.tensor_tensor(it.st[:, 4:5], it.st[:, 4:5], it.st[:, 5:6], ALU.add)))
                        c = link(dve.reciprocal(it.st[:, 6:7], it.st[:, 4:5]))
                        after(c)
                        if it.gate is not None:
                            c = link(dve.tensor_tensor(it.st[:, 6:7], it.st[:, 6:7], it.gate, ALU.mult))
                            after(c)
                        dve.sem_inc(a.comb, 1)
                if n >= 4:
                    it = items[n - 4]
                    dve.wait_ge(a.pv_done, it.n + 1)
                    pv = PS[:, 6 + it.n % 2, 0:it.dv]
                    if it.kind == "soft" and it.add:
                        dve.scalar_tensor_tensor(out=it.out, in0=pv, scalar=it.st[:, 6:7], in1=it.out,
                                                 op0=ALU.mult, op1=ALU.add).then_inc(a.o_done, 1)
                    elif it.kind == "soft":
                        dve.tensor_scalar(it.out, pv, it.st[:, 6:7], None, ALU.mult).then_inc(a.o_done, 1)
                    else:
                        dve.tensor_copy(it.out, pv).then_inc(a.o_done, 1)
                    dve.wait_ge(a.o_done, it.n + 1)
                for what in a.hooks["dve"].get(n, []):
                    what(dve)

        o_ready = [sem("o_ready1"), sem("o_ready2")]
        o_turned = [sem("o_turned1"), sem("o_turned2")]
        o_hi = [sem("o_hi1"), sem("o_hi2")]
        o_split = [sem("o_split1"), sem("o_split2")]

        def pe_turn(pe, b):
            for n in range(2 * TB):
                half, i = n // TB, n % TB
                pe.wait_ge(o_ready[b], 7 + half)
                if n >= 4:
                    pe.wait_ge(o_split[b], n - 3)
                for c in range(4):
                    mm = pe.transpose(PS[:, n % 4, bass.ts(c, P)], O[:, i, bass.ts(half * 4 + c, P)], ident[:, :])
                mm.then_inc(o_turned[b], 1)

        def turned_aps(n):
            half, i = n // TB, n % TB
            src = PS[:, n % 4, :].rearrange("p (c n) -> p c n", c=4)
            return src, H_hi[:, 4 * half:4 * half + 4, bass.ts(i, P)], H_lo[:, 4 * half:4 * half + 4, bass.ts(i, P)]

        def act_turn(act, b):
            for n in range(2 * TB):
                src, hi, _ = turned_aps(n)
                act.wait_ge(o_turned[b], n + 1)
                act.activation(hi, src, ACT.Copy).then_inc(o_hi[b], 1)

        def dve_turn(dve, b):
            for n in range(2 * TB):
                src, hi, lo = turned_aps(n)
                dve.wait_ge(o_hi[b], n + 1)
                dve.tensor_tensor(lo, src, hi.bitcast(F32), ALU.subtract).then_inc(o_split[b], 1)

        def pe_wo(pe, b, u0):
            for j in range(KC):
                pe.wait_ge(lo_done, u0 + j + 1)
                if j == 0:
                    pe.wait_ge(o_split[b], 2 * TB)
                pe_chunk(pe, (u0 + j) % RING, j)

        head_sq = sem("head_sq")
        head_sum = sem("head_sum")
        head_ln = sem("head_ln")
        head_root = sem("head_root")
        head_mul = sem("head_mul")
        gain_ready = sem("gain_ready")

        def head_group(p):
            c = p // 2
            heads = 1 if p % 2 == 0 else 2
            cols = O[:, :, (T if p % 2 else 0) + c * P:(T if p % 2 else 0) + (c + 1) * P]
            done = groups1[p + 1] if p < 7 else len(items1)
            return cols, heads, done

        def pool_heads(pool):
            for p in range(8):
                cols, heads, done = head_group(p)
                pool.wait_ge(at1.o_done, done)
                z = scratch[:, 0:T].rearrange("p (i d) -> p i d", i=TB)
                pool.tensor_tensor(z, cols, cols, ALU.mult).then_inc(head_sq, 1)
                pool.wait_ge(head_root, p + 1)
                if heads == 1:
                    x = cols
                    r = small[:, 24:24 + TB].unsqueeze(2).to_broadcast([P, TB, P])
                    g = row[:, ROW_SUB:ROW_SUB + P].unsqueeze(1).to_broadcast([P, TB, P])
                    pool.wait_ge(gain_ready, 1)
                    pool.tensor_tensor(x, x, r, ALU.mult).then_inc(head_mul, 1)
                    pool.wait_ge(head_mul, 2 * p + 1)
                    pool.tensor_tensor(x, x, g, ALU.mult).then_inc(head_mul, 1)
                    pool.wait_ge(head_mul, 2 * p + 2)
                else:
                    x = cols.rearrange("p i (h d) -> p i h d", h=2)
                    r = small[:, 24:24 + 2 * TB].rearrange("p (i h) -> p i h", h=2).unsqueeze(3).to_broadcast([P, TB, 2, HD])
                    g = row[:, ROW_SBN:ROW_SBN + HD].unsqueeze(1).unsqueeze(2).to_broadcast([P, TB, 2, HD])
                    pool.tensor_tensor(x, x, r, ALU.mult).then_inc(head_mul, 1)
                    pool.wait_ge(head_mul, 2 * p + 1)
                    pool.tensor_tensor(x, x, g, ALU.mult).then_inc(head_mul, 1)
                    pool.wait_ge(head_mul, 2 * p + 2)
                pool.sem_inc(o_ready[0], 1)

        def dve_head(p):
            def what(dve):
                _, heads, _ = head_group(p)
                dve.wait_ge(head_sq, p + 1)
                dve.tensor_reduce(small[:, 16:16 + heads * TB], scratch[:, 0:T].rearrange(
                    "p (n d) -> p n d", n=heads * TB), AX_X, ALU.add).then_inc(head_sum, 1)
            return what

        def act_head(p):
            def what(act):
                _, heads, _ = head_group(p)
                act.wait_ge(head_sum, p + 1)
                a, r = small[:, 16:16 + heads * TB], small[:, 24:24 + heads * TB]
                act.activation(r, a, ACT.Ln, bias=epsc[:, 0:1], scale=heads / P).then_inc(head_ln, 1)
                act.wait_ge(head_ln, p + 1)
                act.activation(r, r, ACT.Exp, scale=-0.5).then_inc(head_root, 1)
            return what

        for p in range(7):
            hook(at1, "dve", groups1[p + 1] + 5, dve_head(p))
            hook(at1, "act", groups1[p + 1] + 6, act_head(p))

        rcol_turned = sem("rcol_turned")
        rcol_done = sem("rcol_done")

        def pe_rcol(pe, n):
            pe.wait_ge(norm_inverse, n.at)
            for tb in range(TB):
                mm = pe.transpose(PS[:, STAT, bass.ts(tb, P)], rstd[:, bass.ts(tb, P)], ident[:, :])
            mm.then_inc(rcol_turned, 1)

        def dve_rcol(dve, b):
            dve.wait_ge(rcol_turned, b + 1)
            dve.tensor_copy(rcol[:, :], PS[:, STAT, :].rearrange("p (b c) -> p b c", b=TB)[:, :, 0]).then_inc(rcol_done, 1)

        qk_evac = [sem("qk_evac1"), sem("qk_evac2")]
        cm = {k: sem("cm_" + k) for k in (
            "raw", "kp", "kp_hi", "kp_lo", "mlp", "pre_t", "hid", "kv", "kv_sb", "s", "l", "e", "p", "t", "pt", "pv", "used")}
        gate_e = sem("gate_e")
        lam_e = sem("lam_e")

        @block.sync
        def _(sp):
            sp.dma_start(X[:, :, :], x_t).then_inc(x_loaded, 16)
            sp.dma_start(par[:, :], params).then_inc(par_loaded, 16)
            for u in range(RING):
                sp.dma_start(stage[:, u, :], weights[u]).then_inc(loaded[u], 16)
            sp.dma_start(row[:, :], rows.to_broadcast([P, N_ROW])).then_inc(row_loaded, 16)
            sp.dma_start(tab[:, :], table_t).then_inc(tab_loaded, 16)
            sp.wait_ge(strips_done[0], 1)
            sp.dma_start(bias_line[:, :, 0:LINE], line[:, :].unsqueeze(1).to_broadcast([N_DIFF, P, LINE])).then_inc(line_out, 16)
            sp.wait_ge(line_out, 16)
            sp.dma_start(strip[:, 0:N_DIFF, :], bass.AP(
                tensor=bias_line.tensor, offset=P - 1,
                ap=[[LINE, P], [P * (LINE + 1), N_DIFF], [1, T]])).then_inc(strips_done[0], 16)

            def load(u0, u1):
                rounds = (u1 - u0) // RING
                with sp.Fori(0, rounds) as r:
                    for i in range(RING):
                        sp.wait_ge(lo_done, r * RING + (u0 + i + 1 - RING))
                        sp.dma_start(stage[:, (u0 + i) % RING, :], weights[u0 + i:u0 + rounds * RING:RING][
                            bass.ds(r, 1)].rearrange("a p n -> p (a n)")).then_inc(loaded[(u0 + i) % RING], 16)
                for u in range(u0 + rounds * RING, u1):
                    sp.wait_ge(lo_done, u + 1 - RING)
                    sp.dma_start(stage[:, u % RING, :], weights[u]).then_inc(loaded[u % RING], 16)

            load(RING, U_WO + 2 * RING)
            for q in at1.preps[1:]:
                q.move(sp)
            load(U_WO + 2 * RING, U_CMP + 2 * RING)
            for q in (ks_, kw_):
                q.move(sp)
            load(U_CMP + 2 * RING, U_WO2 + 2 * RING)
            for q in at2.preps[3:]:
                q.move(sp)
            load(U_WO2 + 2 * RING, N_UNITS)
            for k in range(KC):
                sp.wait_ge(n_final.scaled, k + 1)
                sp.dma_start(out_t[:, k, :], tmp[:, k % 2, :]).then_inc(out_done[k % 2], 16)
            for p in range(2):
                sp.wait_ge(out_done[p], 16 * KC // 2)

        @block.gpsimd
        def _(pool):
            pool.memset(ones[:, :], 1.0 / D).then_inc(const_done, 1)
            pool.memset(ident[:, :], 0.0).then_inc(const_done, 1)
            pool.memset(epsc[:, :], EPS).then_inc(const_done, 1)
            pool.memset(strip[:, N_DIFF, 0:P], 0.0).then_inc(const_done, 1)
            pool.wait_ge(const_done, 4)
            pool.affine_select(out=ident[:, :], in_=ident[:, :], compare_op=ALU.not_equal, fill=1.0, base=0,
                               pattern=[[-1, P]], channel_multiplier=1).then_inc(const_done, 1)
            pool.affine_select(out=strip[:, N_DIFF, 0:P], in_=strip[:, N_DIFF, 0:P], compare_op=ALU.is_gt, fill=MASKED,
                               base=0, pattern=[[-1, P]], channel_multiplier=1).then_inc(const_done, 1)
            pool.wait_ge(const_done, 6)
            pool.tensor_copy(ident_r[:, :], ident[:, :]).then_inc(const_done, 1)
            pool.tensor_copy(mask_r[:, :], strip[:, N_DIFF, 0:P]).then_inc(const_done, 1)

            def rest(u_of, slot):
                pool.wait_ge(hi_done, u_of)
                pool.tensor_tensor(w_lo[:, slot, :], stage[:, slot, :], w_hi[:, slot, :].bitcast(F32),
                                   ALU.subtract).then_inc(lo_done, 1)

            def run(u0, u1):
                rounds = (u1 - u0) // RING
                if rounds > 1:
                    with pool.Fori(0, rounds) as r:
                        for i in range(RING):
                            rest(r * RING + (u0 + i + 1), (u0 + i) % RING)
                    u0 += rounds * RING
                for u in range(u0, u1):
                    rest(u + 1, u % RING)

            run(0, RING)
            pool_sum(pool, n_attn_pre)
            run(RING, U_WO + RING)
            pool_heads(pool)
            pool_sum(pool, n_attn_post, lambda k: rest(U_WO + RING + k + 1, (U_WO + RING + k) % RING))
            pool_post(pool, n_attn_post)
            pool_sum(pool, n_ffn_pre)
            run(U_UP1 + RING, U_UP2 + RING - 1)
            pool_sum(pool, n_ffn_post)
            run(U_UP2 + RING - 1, U_UP2 + RING)
            pool_post(pool, n_ffn_post)
            pool_sum(pool, n_ffn1)
            run(U_UP2 + RING, U_MIX + RING)
            pool_sum(pool, n_mix)
            di, ci = L0[:, 0, :].bitcast(I32), L0[:, 1, 0:P].bitcast(I32)
            dist, cd = L1[:, 0, :], L1[:, 1, 0:P]
            pool.iota(di, pattern=[[-1, T]], base=3 * P, channel_multiplier=1).then_inc(const_done, 1)
            pool.iota(ci.rearrange("p (i c) -> p i c", i=4),
                      pattern=[[P, 4], [-CMP_STRIDE, 32]], base=-(CMP_BLOCK - 1), channel_multiplier=1).then_inc(const_done, 1)
            pool.wait_ge(const_done, 10)
            pool.tensor_copy(dist, di).then_inc(const_done, 1)
            pool.tensor_copy(cd, ci).then_inc(const_done, 1)
            pool.wait_ge(const_done, 12)
            pool.affine_select(out=WT[:, 1, 0:256], in_=dist[:, 256:512], compare_op=ALU.is_ge, fill=FAR,
                               base=P, pattern=[[-1, 256]], channel_multiplier=1).then_inc(const_done, 1)
            pool.wait_ge(const_done, 13)
            pool.affine_select(out=WT[:, 1, 0:256], in_=WT[:, 1, 0:256], compare_op=ALU.is_gt, fill=FAR,
                               base=0, pattern=[[1, 256]], channel_multiplier=-1).then_inc(const_done, 1)
            pool.affine_select(out=dist, in_=dist, compare_op=ALU.is_ge, fill=FAR,
                               base=3 * P, pattern=[[-1, T]], channel_multiplier=1).then_inc(const_done, 1)
            pool.affine_select(out=cd.rearrange("p (i c) -> p i c", i=4),
                               in_=cd.rearrange("p (i c) -> p i c", i=4), compare_op=ALU.is_ge, fill=FAR,
                               base=-(CMP_BLOCK - 1), pattern=[[P, 4], [-CMP_STRIDE, 32]], channel_multiplier=1).then_inc(const_done, 1)
            run(U_MIX + RING, U_UP3 + RING)
            pool_sum(pool, n_ffn2)
            run(U_UP3 + RING, N_UNITS)
            pool_sum(pool, n_final)

        @block.scalar
        def _(act):
            count = [0]

            def link(ins):
                ins.then_inc(act_self, 1)
                count[0] += 1
                return count[0]

            def after(c):
                act.wait_ge(act_self, c)

            for u in range(RING):
                act_hi(act, u, None, 16, wait_free=False)
            act.wait_ge(const_done, 3)
            act.wait_ge(x_loaded, 16)
            act.wait_ge(par_loaded, 16)
            act.sem_inc(n_attn_pre.ready, KC)
            act_fold(act, n_attn_pre)
            with act.Fori(0, 4) as r:
                for i in range(4):
                    v = U_QKV + i + RING
                    act_hi(act, v % RING, r * 4 + v, r * 16 + 16 * (v // RING + 1))
            act.wait_ge(rcol_done, 1)
            for g in range(2):
                for t in range(4):
                    act_hi_static(act, U_QKV + 16 + 4 * g + t)
                for tb in range(TB):
                    act.activation(V[:, g, tb, :], PS[:, (4 if g == 0 else 0) + tb, :], ACT.Copy,
                                   scale=rcol[:, tb:tb + 1]).then_inc(v_ready[0], 1)
            act.wait_ge(lam_e, 2)
            act.activation(small[:, 4:6], small[:, 2:4], ACT.Exp).then_inc(lam_e, 1)
            act.preload_act_table_set("natural_log_exp_and_others")
            act.wait_ge(qk_evac[0], 4 + 16)
            for q in at1.preps[0:2]:
                q.act_split(act)
            at1.preps[0].move(act)
            act_attn(act, at1, link, after)
            act_head(7)(act)
            act_turn(act, 0)
            for j in range(KC):
                act_hi_static(act, U_WO + j)
                act.activation(QK[:, j, :], PS[:, j, :], ACT.Copy).then_inc(n_attn_post.ready, 1)
                act_square(act, n_attn_post, j)
            act_root(act, n_attn_post)
            act_fold(act, n_ffn_pre)
            act_ffn(act, 0, U_UP1, U_DN1, True)
            for k in range(KC):
                act.wait_ge(y_done[0], k + 1)
                act.activation(Y2[:, k, :], PS[:, k, :], ACT.Copy).then_inc(n_ffn_post.ready, 1)
                act_square(act, n_ffn_post, k)
            act_root(act, n_ffn_post)
            act_hi_static(act, U_DN1 + FC - 1)
            act_fold(act, n_ffn1)
            act_ffn(act, 1, U_UP2, U_DN2, False)
            act_fold(act, n_mix, U_DN2 + FC - 1)
            with act.Fori(0, 3) as r:
                for i in range(4):
                    v = U_MIX + i + RING
                    act_hi(act, v % RING, r * 4 + v, r * 16 + 16 * (v // RING + 1))
            act_hi_static(act, U_MIX + 12)
            for t in range(4):
                act_hi_static(act, U_MIX + 13 + t)
            act.wait_ge(rcol_done, 2)
            for tb in range(TB):
                act.activation(V[:, 0, tb, 0:NAT2], PS[:, 4 + tb, 0:NAT2], ACT.Copy,
                               scale=rcol[:, tb:tb + 1]).then_inc(v_ready[1], 1)
            act.wait_ge(v_ready[1], TB)
            act.activation(gates[:, :, :], V[:, 0, :, 3 * P:NAT2], ACT.Exp, scale=-1.0).then_inc(gate_e, 1)
            act.wait_ge(qk_evac[1], 4 + 13)
            for q in (q0, ks_, kw_):
                q.act_split(act)
            for s in range(2):
                if s == 1:
                    act.wait_ge(cm["kp"], 1)
                for g in range(2):
                    src = QK[g * HD:(g + 1) * HD, 6 + s, :]
                    act.dma_start(kpair[0:HD, g, :], src).then_inc(cm["raw"], 16)
                    act.dma_start(kpair[HD:P, g, 0:T - 1], src[:, 1:T]).then_inc(cm["raw"], 16)
                act.wait_ge(cm["kp"], s + 1)
                if s == 1:
                    act.wait_ge(unit_done, U_CMP + 4)
                act.activation(kp_hi, kp, ACT.Copy).then_inc(cm["kp_hi"], 1)
                if s == 0:
                    q0.move(act)
                for t in range(4):
                    act_hi_static(act, U_CMP + 4 * s + t)
                act.activation(hidden, PS[0:2 * NCMP, s, 0:CMP_HID], ACT.Copy).then_inc(cm["mlp"], 1)
                act.wait_ge(cm["pre_t"], s + 1)
                for half in range(2):
                    act.activation(hid[:, s, half, :], PS[:, 2 + s, half * P:half * P + 2 * NCMP], ACT.Gelu_apprx_tanh,
                                   bias=pc("b1_k" if s == 0 else "b1_v", half)).then_inc(cm["hid"], 1)
            act.wait_ge(cm["kv"], 1)
            act.activation(kcT[:, 0:NCMP], PS[:, 4, 0:NCMP], ACT.Copy).then_inc(cm["kv_sb"], 1)
            for i in range(4):
                act.activation(vc[32 * i:32 * i + NCMP, :, :], PS[32 * i:32 * i + NCMP, 5, 0:2 * HD].rearrange(
                    "p (g d) -> p g d", g=2), ACT.Copy).then_inc(cm["kv_sb"], 1)
            for g in range(2):
                act.wait_ge(cm["l"], g + 1)
                z = cmp_L(g)
                act.activation(z, z, ACT.Exp, scale=SCALE).then_inc(cm["e"], 1)
            for h in range(N_NSA):
                act.wait_ge(cm["t"], h // 4 + 1)
                act.activation(cmp_PT(h), PS[:, 6 + h // 4, bass.ts(h % 4, P)],
                               ACT.Copy).then_inc(cm["pt"], 1)
            act.preload_act_table_set("natural_log_exp_and_others")
            act_attn(act, at2, link, after)
            act_turn(act, 1)
            for j in range(KC):
                act_hi_static(act, U_WO2 + j)
            act_fold(act, n_ffn2)
            act_ffn(act, 2, U_UP3, U_DN3, False)
            for k in range(KC):
                n_final.wait_ready(act, k)
                act_square(act, n_final, k)
            act_root(act, n_final)

        @block.tensor
        def _(pe):
            pe.sem_inc(ffn_free, 2)
            pe.sem_inc(qk_evac[0], 4)
            pe.sem_inc(qk_evac[1], 4)
            pe.wait_ge(const_done, 8)
            pe_first_pair(pe, n_attn_pre, U_QKV)
            pe_stat(pe, n_attn_pre)
            for i in range(2, 4):
                pe.wait_ge(lo_done, U_QKV + i + 1)
                pe_chunk(pe, (U_QKV + i) % RING, i)
            pe_rcol(pe, n_attn_pre)
            with pe.Fori(1, 4) as r:
                for i in range(4):
                    pe.wait_ge(lo_done, r * 4 + (U_QKV + i + 1))
                    pe.wait_ge(qk_evac[0], r * 4 + (i + 1))
                    pe_chunk(pe, (U_QKV + i) % RING, i)
            pe.wait_ge(rcol_done, 1)
            pe_by_token(pe, U_QKV + 16, 4, T)
            pe.wait_ge(qk_evac[0], 20)
            pe_by_token(pe, U_QKV + 20, 0, T)
            pe.wait_ge(v_ready[0], 2 * TB)
            pe_attn(pe, at1)
            pe.wait_ge(at1.o_done, len(items1))
            pe_turn(pe, 0)
            pe_wo(pe, 0, U_WO)
            pe_stat(pe, n_attn_post)
            pe_ffn(pe, 0, U_UP1, U_DN1, n_ffn_pre)
            pe_stat(pe, n_ffn_post)
            pe_ffn(pe, 1, U_UP2, U_DN2, n_ffn1)
            pe_first_pair(pe, n_mix, U_MIX)
            pe_stat(pe, n_mix)
            for i in range(2, 4):
                pe.wait_ge(lo_done, U_MIX + i + 1)
                pe_chunk(pe, (U_MIX + i) % RING, i)
            pe_rcol(pe, n_mix)
            with pe.Fori(1, 3) as r:
                for i in range(4):
                    pe.wait_ge(lo_done, r * 4 + (U_MIX + i + 1))
                    pe.wait_ge(qk_evac[1], r * 4 + (i + 1))
                    pe_chunk(pe, (U_MIX + i) % RING, i)
            pe.wait_ge(lo_done, U_MIX + 13)
            pe.wait_ge(qk_evac[1], 13)
            pe_chunk(pe, (U_MIX + 12) % RING, 0)
            pe.wait_ge(rcol_done, 2)
            pe_by_token(pe, U_MIX + 13, 4, NAT2)
            pe.wait_ge(qk_evac[1], 17)
            for s in range(2):
                pe.wait_ge(cm["kp_lo"], s + 1)
                for t in range(4):
                    u = U_CMP + 4 * s + t
                    pe.wait_ge(lo_done, u + 1)
                    for j4 in range(4):
                        j = 4 * t + j4
                        cols = slice(j4 * CMP_HID, (j4 + 1) * CMP_HID)
                        o = PS[0:2 * NCMP, s, 0:CMP_HID]
                        pe.matmul(o, kp_hi[:, j, :], w_hi[:, u % RING, cols], start=(j == 0), stop=False)
                        pe.matmul(o, kp_hi[:, j, :], w_lo[:, u % RING, cols], start=False, stop=False)
                        mm = pe.matmul(o, kp_lo[:, j, :], w_hi[:, u % RING, cols], start=False, stop=(j == 15))
                    mm.then_inc(unit_done, 1)
                pe.wait_ge(cm["mlp"], s + 1)
                for half in range(2):
                    mm = pe.transpose(PS[:, 2 + s, half * P:half * P + 2 * NCMP],
                                      hidden[:, bass.ts(half, P)], ident[0:2 * NCMP, 0:2 * NCMP])
                mm.then_inc(cm["pre_t"], 1)
            pe.wait_ge(cm["hid"], 4)
            pe.wait_ge(v_ready[1], TB)
            for g in range(2):
                for half in range(2):
                    pe.matmul(PS[g * HD:(g + 1) * HD, 4, 0:NCMP], pc("w2_k", half * HD, HD),
                              hid[:, 0, half, g * NCMP:(g + 1) * NCMP], start=(half == 0), stop=(half == 1))
            for i in range(4):
                for g in range(2):
                    for half in range(2):
                        mm = pe.matmul(PS[32 * i:32 * i + NCMP, 5, g * HD:(g + 1) * HD],
                                       hid[:, 1, half, g * NCMP:(g + 1) * NCMP], pc("w2_v", half * HD, HD),
                                       start=(half == 0), stop=(half == 1))
            mm.then_inc(cm["kv"], 1)
            pe.wait_ge(cm["kv_sb"], 5)
            for g in range(2):
                for r in range(4):
                    for i in range(TB):
                        mm = pe.matmul(PS[:, g, r * P + i * 32:r * P + i * 32 + NCMP],
                                       QK[g * HD:(g + 1) * HD, r, bass.ts(i, P)], kcT[g * HD:(g + 1) * HD, 0:NCMP],
                                       start=True, stop=True)
                mm.then_inc(cm["s"], 1)
            for g in range(2):
                pe.wait_ge(cm["p"], g + 1)
                for r in range(4):
                    mm = pe.transpose(PS[:, 6 + g, bass.ts(r, P)], cmp_L(g)[:, bass.ts(r, P)], ident[:, :])
                mm.then_inc(cm["t"], 1)
            pe.wait_ge(cm["pt"], N_NSA)
            for i in range(TB):
                for h in range(N_NSA):
                    mm = pe.matmul(PS[:, i, bass.ts(h, HD)], cmp_PT(h)[32 * i:32 * i + NCMP, :],
                                   vc[32 * i:32 * i + NCMP, h // 4, :], start=True, stop=True)
                mm.then_inc(cm["pv"], 1)
            pe.wait_ge(cm["used"], TB)
            pe_attn(pe, at2)
            pe.wait_ge(at2.o_done, len(items2))
            pe_turn(pe, 1)
            pe_wo(pe, 1, U_WO2)
            pe_ffn(pe, 2, U_UP3, U_DN3, n_ffn2)
            pe_stat(pe, n_final)

        @block.vector
        def _(dve):
            count = [0]

            def link(ins):
                ins.then_inc(dve_self, 1)
                count[0] += 1
                return count[0]

            def after(c):
                dve.wait_ge(dve_self, c)

            dve.wait_ge(row_loaded, 16)
            for m in range(2):
                a = row[:, ROW_LAM + 2 * m * HD:ROW_LAM + (2 * m + 1) * HD]
                b = row[:, ROW_LAM + (2 * m + 1) * HD:ROW_LAM + (2 * m + 2) * HD]
                dve.tensor_tensor_reduce(out=tmp[:, 0, m * HD:(m + 1) * HD], in0=a, in1=b, scale=1.0, scalar=0.0, op0=ALU.mult,
                                         op1=ALU.add, accum_out=small[:, 2 + m:3 + m]).then_inc(lam_e, 1)
            dve.wait_ge(tab_loaded, 16)
            for b, lo, hi in bucket_runs():
                c = link(dve.tensor_copy(line[:, T - 1 - hi:T - lo],
                                         tab[:, b:b + 1].to_broadcast([N_DIFF, hi - lo + 1])))
            c = link(dve.memset(line[:, T:LINE], MASKED))
            after(c)
            dve.sem_inc(strips_done[0], 1)
            dve.wait_ge(par_loaded, 16)
            gain = row[:, ROW_SUB:ROW_SUB + P]
            dve.tensor_scalar(gain, gain, 1.0 - LAM_INIT, None, ALU.mult).then_inc(gain_ready, 1)
            dve_fold(dve, n_attn_pre)

            def evacuate(b, bank, chunk, scale, unit_wait):
                dve.wait_ge(unit_done, unit_wait)
                if scale != 1.0:
                    x = dve.scalar_tensor_tensor(out=chunk, in0=PS[:, bank, :], scalar=scale, in1=rstd[:, :],
                                                 op0=ALU.mult, op1=ALU.mult)
                else:
                    x = dve.tensor_tensor(chunk, PS[:, bank, :], rstd[:, :], ALU.mult)
                x.then_inc(qk_evac[b], 1)

            def projections(b, u0, rounds, scale):
                for i in range(4):
                    evacuate(b, i, QK[:, i, :], scale(i), u0 + i + 1)
                dve_rcol(dve, b)
                with dve.Fori(1, rounds) as r:
                    for i in range(4):
                        evacuate(b, i, QK[:, bass.ds(r * 4 + i, 1), :].rearrange("p a n -> p (a n)"), scale(i),
                                 r * 4 + (u0 + i + 1))

            projections(0, U_QKV, 4, lambda i: SCALE if i % 2 == 0 else 1.0)
            dve.wait_ge(lam_e, 3)
            after(link(dve.tensor_tensor(small[:, 0:1], small[:, 5:6], small[:, 4:5], ALU.subtract)))
            after(link(dve.tensor_scalar(small[:, 0:1], small[:, 0:1], LAM_INIT, None, ALU.subtract)))
            dve.wait_ge(strips_done[0], 17)
            dve.wait_ge(const_done, 8)
            for q in at1.preps[0:2]:
                q.dve_split(dve)
            dve_attn(dve, at1, link, after)
            dve_head(7)(dve)
            dve_turn(dve, 0)
            dve_post(dve, n_attn_post)
            dve_fold(dve, n_ffn_pre)
            dve_ffn(dve, 0, U_UP1, True)
            dve_post(dve, n_ffn_post)
            dve_fold(dve, n_ffn1)
            dve_ffn(dve, 1, U_UP2, False)

            def residual(inst, norm):
                for k in range(KC):
                    dve.wait_ge(y_done[inst], k + 1)
                    dve.scalar_tensor_tensor(out=X[:, k, :], in0=PS[:, k, :], scalar=0.5, in1=X[:, k, :],
                                             op0=ALU.mult, op1=ALU.add).then_inc(norm.ready, 1)
            residual(1, n_mix)
            dve_fold(dve, n_mix)
            projections(1, U_MIX, 3, lambda i: 1.0)
            evacuate(1, 0, QK[:, 12, :], 1.0, U_MIX + 13)
            dve.wait_ge(const_done, 16)
            for h in range(N_NSA):
                f = -2.0 ** (-8.0 * (h + 1) / N_NSA) / SCALE
                link(dve.tensor_scalar(strip[:, h, :], L1[:, 0, :], f, None, ALU.mult))
                c = link(dve.tensor_scalar(swa_strip(h), WT[:, 1, 0:256], f, None, ALU.mult))
            c = link(dve.tensor_copy(cdist[:, :], L1[:, 1, 0:P]))
            after(c)
            dve.wait_ge(gate_e, 1)
            after(link(dve.tensor_scalar(gates[:, :, :], gates[:, :, :], 1.0, None, ALU.add)))
            after(link(dve.reciprocal(gates[:, :, :], gates[:, :, :])))
            for s in range(2):
                dve.wait_ge(cm["raw"], 64 * (s + 1))
                if s == 1:
                    dve.wait_ge(cm["kp_lo"], 1)
                whole = kpair
                win = bass.AP(tensor=whole.tensor, offset=whole.offset,
                              ap=[whole.ap[0], [2, 16], [T, 2], [CMP_STRIDE, NCMP]])
                pos = pc("pos_k" if s == 0 else "pos_v", 0, 16).unsqueeze(2).unsqueeze(3).to_broadcast([P, 16, 2, NCMP])
                dve.tensor_tensor(kp.rearrange("p j (g c) -> p j g c", g=2), win, pos, ALU.add).then_inc(cm["kp"], 1)
                if s == 0:
                    for q in (q0, ks_, kw_):
                        q.dve_split(dve)
                dve.wait_ge(cm["kp_hi"], s + 1)
                dve.tensor_tensor(kp_lo, kp, kp_hi.bitcast(F32), ALU.subtract).then_inc(cm["kp_lo"], 1)
            dist = cdist[:, :].rearrange("p (i c) -> p i c", i=4)
            for g in range(2):
                dve.wait_ge(cm["s"], g + 1)
                z = cmp_L(g).rearrange("p (h i c) -> p h i c", h=4, i=4)
                zs = PS[:, g, :].rearrange("p (h i c) -> p h i c", h=4, i=4)
                after(link(dve.memset(cmp_L(g), 0.0)))
                for r in range(4):
                    h = 4 * g + r
                    f = -2.0 ** (-8.0 * (h + 1) / N_NSA) / SCALE
                    c = link(dve.scalar_tensor_tensor(out=z[:, r, :, 0:NCMP], in0=dist[:, :, 0:NCMP], scalar=f,
                                                      in1=zs[:, r, :, 0:NCMP], op0=ALU.mult, op1=ALU.add))
                after(c)
                zz = cmp_L(g).rearrange("p (h c) -> p h c", c=32)[:, :, 0:NCMP]
                mx = small[:, 32:48]
                after(link(dve.tensor_reduce(mx, zz, AX_X, ALU.max)))
                after(link(dve.tensor_scalar(mx, mx, MASKED / SCALE, None, ALU.max)))
                dve.tensor_tensor(zz, zz, mx.unsqueeze(2).to_broadcast([P, 16, NCMP]), ALU.subtract).then_inc(cm["l"], 1)
                dve.wait_ge(cm["e"], g + 1)
                after(link(dve.tensor_reduce(mx, zz, AX_X, ALU.add)))
                after(link(dve.tensor_scalar(mx, mx, 0.5, None, ALU.max)))
                after(link(dve.reciprocal(mx, mx)))
                gv = gates[:, :, 12 * g:12 * g + 12].rearrange("p i (r b) -> p r i b", b=3)[:, :, :, 0]
                m4 = mx.rearrange("p (r i) -> p r i", i=4)
                after(link(dve.tensor_tensor(m4, m4, gv, ALU.mult)))
                dve.tensor_tensor(zz, zz, mx.unsqueeze(2).to_broadcast([P, 16, NCMP]), ALU.mult).then_inc(cm["p"], 1)
            for i in range(TB):
                dve.wait_ge(cm["pv"], i + 1)
                dve.tensor_copy(O[:, i, 0:T], PS[:, i, :]).then_inc(cm["used"], 1)
            dve.wait_ge(cm["used"], TB)
            dve_attn(dve, at2, link, after)
            dve.sem_inc(o_ready[1], 8)
            dve_turn(dve, 1)
            for j in range(KC):
                dve.wait_ge(unit_done, U_WO2 + j + 1)
                dve.tensor_tensor(X[:, j, :], X[:, j, :], PS[:, j, :], ALU.add).then_inc(n_ffn2.ready, 1)
            dve_fold(dve, n_ffn2)
            dve_ffn(dve, 2, U_UP3, False)
            residual(2, n_final)
            dve_inverse(dve, n_final)
            dve.wait_ge(norm_inverse, n_final.at)
            for k in range(KC):
                if k >= 2:
                    dve.wait_ge(out_done[k % 2], 16 * (k // 2))
                dve.scalar_tensor_tensor(out=tmp[:, k % 2, :], in0=X[:, k, :], scalar=pc("final", k),
                                         in1=rstd[:, :], op0=ALU.mult, op1=ALU.mult).then_inc(n_final.scaled, 1)


def kernel(**inp):
    import concourse.bacc as bacc
    from concourse.bass_utils import run_bass_kernel_spmd

    f32 = np.float32

    def chunks(w):
        w = w.reshape(KC, P, -1, P)
        return w.transpose(2, 1, 0, 3).reshape(-1, P, UNIT)

    def by_token(w):
        wide = np.zeros((D, T), f32)
        wide[:, :w.shape[1]] = w
        return wide.reshape(4, 2, P, T).transpose(0, 2, 1, 3).reshape(4, P, UNIT)

    def up(w):
        w = w.reshape(D, 2, FC, P).transpose(0, 2, 1, 3).reshape(D, 2 * FF)
        return chunks(w)

    def pairs(w):
        return w.reshape(D, 2, 4, HD).transpose(0, 2, 1, 3).reshape(D, 8 * HD)

    def cmp1(w):
        return w.reshape(4, 4, P, CMP_HID).transpose(0, 2, 1, 3).reshape(4, P, UNIT)

    w = np.asarray(inp["w_qkv"][0])
    dq, dk, dv, sq_, sk, sv = np.split(w, 6, axis=1)
    qk = np.stack([a.reshape(D, 4, P) for a in (dq, dk, sq_, sk)], axis=2).reshape(D, 16 * P)
    m = np.asarray(inp["w_mix_in_2"][0])
    qa, kva, ga, qb, kvb = np.split(m, np.cumsum([512, 768, 24, 512]).tolist(), axis=1)
    kc, vcr, ks, vs, kw, vw = np.split(kva, 6, axis=1)
    kb, vb = np.split(kvb, 2, axis=1)
    mix_t = np.concatenate([pairs(qa), ks, kw, kc, vcr, pairs(qb), kb], axis=1)
    mix_n = np.concatenate([vs, vw, vb, ga], axis=1)
    weights = np.concatenate([
        chunks(qk), by_token(dv), by_token(sv), chunks(np.asarray(inp["w_o"][0])),
        up(np.asarray(inp["w_up"][0])), np.asarray(inp["w_down"][0]).reshape(FC, P, UNIT),
        up(np.asarray(inp["ffn1_w_in_2"][0])), np.asarray(inp["ffn1_w_out_2"][0]).reshape(FC, P, UNIT),
        chunks(mix_t), by_token(mix_n),
        cmp1(np.asarray(inp["cmp_k_w1_2"][0])), cmp1(np.asarray(inp["cmp_v_w1_2"][0])),
        chunks(np.asarray(inp["w_mix_out_2"][0])),
        up(np.asarray(inp["ffn2_w_in_2"][0])), np.asarray(inp["ffn2_w_out_2"][0]).reshape(FC, P, UNIT)], axis=0)
    assert weights.shape[0] == N_UNITS

    def cols(v):
        return np.asarray(v).reshape(-1, P).T

    params = np.concatenate(
        [cols(inp[n]) for n in ("attn_pre_norm", "attn_post_norm", "ffn_pre_norm", "ffn_post_norm",
                                "ffn1_norm_2", "mix_norm_2", "ffn2_norm_2", "final_norm_2", "conv_w", "conv_b",
                                "cmp_k_pos_2", "cmp_v_pos_2", "cmp_k_b1_2", "cmp_v_b1_2")]
        + [np.asarray(inp[n][0]).reshape(2, P, HD).transpose(1, 0, 2).reshape(P, 2 * HD)
           for n in ("cmp_k_w2_2", "cmp_v_w2_2")], axis=1)
    assert params.shape == (P, N_PARAMS)
    rows = np.concatenate([np.asarray(inp[n]).reshape(-1) for n in (
        "lambda_q1", "lambda_k1", "lambda_q2", "lambda_k2", "diff_subln", "sb_norm", "swa_sinks_2")])[None]
    x_t = np.asarray(inp["x"])[0].T.reshape(KC, P, T).transpose(1, 0, 2)
    arrays = {"weights": weights, "x_t": x_t, "params": params, "rows": rows, "table_t": np.asarray(inp["rel_bias"]).T}
    nc = bacc.Bacc("TRN2", target_bir_lowering=False, num_devices=1)
    args, given = [], {}
    for name, a in arrays.items():
        given["in_" + name] = np.ascontiguousarray(a)
        args.append(nc.dram_tensor("in_" + name, a.shape, F32, kind="ExternalInput").ap())
    args.append(nc.dram_tensor("bias_line", (N_DIFF, P, LINE + 1), F32, kind="Internal").ap())
    args.append(nc.dram_tensor("out_t", (P, KC, T), F32, kind="ExternalOutput").ap())
    build(nc, *args)
    r = run_bass_kernel_spmd(nc, [given], core_ids=[0])
    out = r.results[0]["out_t"]
    return np.ascontiguousarray(out.transpose(2, 1, 0).reshape(1, T, D))
```

```python
from contextlib import ExitStack
import math

import numpy as np

import concourse.bass as bass
from concourse import mybir

F32 = mybir.dt.float32
F32R = mybir.dt.float32r
I32 = mybir.dt.int32
ALU = mybir.AluOpType
ACT = mybir.ActivationFunctionType
AX_X = mybir.AxisListType.X

P = 128
T = 512
TB = T // P
D = 1024
KC = D // P
HD = 64
FF = 2816
FC = FF // P
UNIT = 1024
RING = 4
EPS = 1e-6
LAM_INIT = 0.8 - 0.6 * math.exp(-0.3 * 0)
SCALE = HD ** -0.5
MASKED = -1e30
FAR = 1e33
N_BUCKETS, MAX_DISTANCE = 32, 128
N_DIFF, N_SB, N_NSA, N_SWA = 4, 8, 8, 8
CMP_BLOCK, CMP_STRIDE, CMP_HID = 32, 16, 256
NCMP = (T - CMP_BLOCK) // CMP_STRIDE + 1
SWA_WINDOW = 128
LINE = T + P
NAT2 = 3 * P + 3 * N_NSA

U_QKV = 0
U_WO = U_QKV + 24
U_UP1 = U_WO + 8
U_DN1 = U_UP1 + 2 * FC
U_UP2 = U_DN1 + FC
U_DN2 = U_UP2 + 2 * FC
U_MIX = U_DN2 + FC
U_CMP = U_MIX + 17
U_WO2 = U_CMP + 8
U_UP3 = U_WO2 + 8
U_DN3 = U_UP3 + 2 * FC
N_UNITS = U_DN3 + FC

PARAMS = {}
_at = 0
for _name, _n in (("attn_pre", KC), ("attn_post", KC), ("ffn_pre", KC), ("ffn_post", KC),
                  ("ffn1", KC), ("mix", KC), ("ffn2", KC), ("final", KC),
                  ("conv_w", 3 * 2 * FC), ("conv_b", 2 * FC), ("pos_k", 16), ("pos_v", 16),
                  ("b1_k", 2), ("b1_v", 2), ("w2_k", 2 * HD), ("w2_v", 2 * HD)):
    PARAMS[_name] = (_at, _n)
    _at += _n
N_PARAMS = _at
ROW_LAM, ROW_SUB, ROW_SBN, ROW_SINK = 0, 4 * HD, 4 * HD + 2 * HD, 4 * HD + 3 * HD
N_ROW = ROW_SINK + N_SWA

FIRST_ORDER = [4, 5, 6, 7, 0, 1, 2, 3]


def bucket_runs():
    exact = N_BUCKETS // 2
    runs = [(b, b, b) for b in range(exact)]
    d = np.arange(exact, T)
    large = exact + (np.log(d.astype(np.float32) / exact) / math.log(MAX_DISTANCE / exact)
                     * (N_BUCKETS - exact)).astype(np.int32)
    large = np.minimum(large, N_BUCKETS - 1)
    for b in range(exact, N_BUCKETS):
        at = d[large == b]
        if len(at):
            runs.append((b, int(at[0]), int(at[-1])))
    return runs


def build(nc, weights, x_t, params, rows, table_t, bias_line, out_t):
    with ExitStack() as top:
        def sem(name):
            return top.enter_context(nc.semaphore(name))

        def sb(name, shape, dtype=F32, ctx=top):
            return ctx.enter_context(nc.sbuf_tensor(name, shape, dtype))

        stage = sb("stage", [P, RING, UNIT])
        w_hi = sb("w_hi", [P, RING, UNIT], F32R)
        w_lo = sb("w_lo", [P, RING, UNIT], F32R)
        X = sb("X", [P, KC, T])
        par = sb("par", [P, N_PARAMS])
        row = sb("row", [P, N_ROW])
        ones = sb("ones", [P, P])
        ident = sb("ident", [P, P])
        epsc = sb("epsc", [P, 1])
        sq = sb("sq", [P, 2, T])
        rstd = sb("rstd", [P, T])
        tmp = sb("tmp", [P, 2, T])
        rcol = sb("rcol", [P, TB])
        with ExitStack() as scope:
            Y2 = sb("Y2", [P, KC, T], ctx=scope)
        H_hi = sb("H_hi", [P, KC, T], F32R)
        H_lo = sb("H_lo", [P, KC, T], F32R)
        with ExitStack() as scope:
            A_hi = sb("A_hi", [P, FC, T], F32R, scope)
            A_lo = sb("A_lo", [P, FC, T], F32R, scope)
            conv = sb("conv", [P, 2, 2, T], ctx=scope)
        with ExitStack() as scope:
            with ExitStack() as inner:
                kp_hi_flat = sb("kp_hi", [P, 2 * T], F32R, inner)
                kp_lo_flat = sb("kp_lo", [P, 2 * T], F32R, inner)
            L1 = sb("L1", [P, 2, T], ctx=scope)
            scratch = sb("scratch", [P, 2 * T], ctx=scope)
            QK = sb("QK", [P, 16, T], ctx=scope)
            V = sb("V", [P, 2, TB, T], ctx=scope)
            O = sb("O", [P, TB, D], ctx=scope)
            strip = sb("strip", [P, 8, T], ctx=scope)
            L0 = sb("L0", [P, 2, T], ctx=scope)
            stat = sb("stat", [P, 4, 8], ctx=scope)
            small = sb("small", [P, 64], ctx=scope)
            tab = sb("tab", [N_DIFF, N_BUCKETS], ctx=scope)
            gates = sb("gates", [P, TB, 3 * N_NSA], ctx=scope)
            cdist = sb("cdist", [P, P], ctx=scope)
            hid = sb("hid", [P, 2, 2, 2 * NCMP], ctx=scope)
            kcT = sb("kcT", [P, 32], ctx=scope)
            vc = sb("vc", [P, 2, HD], ctx=scope)
            ident_r = sb("ident_r", [P, P], F32R, scope)
            mask_r = sb("mask_r", [P, P], F32R, scope)
        W, WT = sq, tmp
        line = O[0:N_DIFF, 0, 0:LINE]
        kpair = V[:, 1, 0:2, :]

        def as_windows(t):
            return t[:, 0:16 * 2 * NCMP].rearrange("p (j n) -> p j n", j=16)

        kp_hi, kp_lo = as_windows(kp_hi_flat), as_windows(kp_lo_flat)
        kp = as_windows(scratch)

        K2 = [H_hi[:, t, :] for t in range(6)]
        QD_hi = [H_lo[:, t, :] for t in range(4)]
        QD_lo = [H_lo[:, 4 + t, :] for t in range(4)]

        def LM(m, n):
            return (L0, L1)[m][:, n % 2, :]

        hidden = QK[0:2 * NCMP, 6, 0:CMP_HID]

        def cmp_L(g):
            return L1[:, g, :]

        def cmp_PT(h):
            return scratch[:, bass.ts(h, P)]

        def swa_strip(h):
            home = QK[:, 13 + h // 2, :] if h < 6 else V[:, 1, 2, :]
            return home[:, (h % 2) * 256:(h % 2 + 1) * 256]

        PS = top.enter_context(nc.psum_tensor("PS", [P, 8, T], F32))

        def pc(name, k, n=1):
            a, _ = PARAMS[name]
            return par[:, a + k:a + k + n]

        loaded = [sem(f"loaded{i}") for i in range(RING)]
        hi_done = sem("hi_done")
        lo_done = sem("lo_done")
        unit_done = sem("unit_done")
        x_loaded = [sem("x_loaded0"), sem("x_loaded1")]
        par_loaded, row_loaded, tab_loaded = map(sem, ("par_loaded", "row_loaded", "tab_loaded"))
        const_done = sem("const_done")
        dve_self = sem("dve_self")
        act_self = sem("act_self")
        line_out = sem("line_out")
        out_done = sem("out_done")

        block = top.enter_context(nc.Block())

        norm_summed = sem("norm_summed")
        norm_log = sem("norm_log")
        norm_inverse = sem("norm_inverse")

        class Norm:

            def __init__(self, name, at, kind, src, before=None):
                self.name, self.at, self.src, self.before = name, at, src, before
                self.total = rstd[:, :] if before is None else conv[:, 0, 0, :]
                if before is None and at > 1:
                    self.ready = sem(f"{name}_ready")
                self.squared = sem(f"{name}_squared")
                self.added = sem(f"{name}_added")
                if kind == "fold":
                    self.hi = sem(f"{name}_hi")
                    self.done = sem(f"{name}_done")
                else:
                    self.scaled = sem(f"{name}_scaled")
                if kind == "post":
                    self.even = sem(f"{name}_even")
                    self.odd = sem(f"{name}_odd")

            def wait_ready(self, eng, k):
                if self.at == 1:
                    eng.wait_ge(x_loaded[k // 4], 16)
                elif self.before is None:
                    eng.wait_ge(self.ready, k + 1)
                else:
                    eng.wait_ge(self.before.odd if k % 2 else self.before.even, k // 2 + 1)

        n_attn_pre = Norm("attn_pre", 1, "fold", X)
        n_attn_post = Norm("attn_post", 2, "post", QK)
        n_ffn_pre = Norm("ffn_pre", 3, "fold", X, n_attn_post)
        n_ffn_post = Norm("ffn_post", 4, "post", Y2)
        n_ffn1 = Norm("ffn1", 5, "fold", X, n_ffn_post)
        n_mix = Norm("mix", 6, "fold", X)
        n_ffn2 = Norm("ffn2", 7, "fold", X)
        n_final = Norm("final", 8, "final", X)
        POOL_ADDS = 5
        STAT = 7

        def act_square(act, n, k, ready=None):
            if k >= 2:
                act.wait_ge(n.added, max(1, k - 2))
            if n.src is not X:
                act.wait_ge(n.ready, ready or k + 1)
            act.activation(sq[:, k % 2, :], n.src[:, k, :], ACT.Square).then_inc(n.squared, 1)

        def pool_sum(pool, n, between=None, upto=KC):
            for k in range(upto):
                if k >= 1:
                    pool.wait_ge(n.squared, k + 1)
                    if k >= 2:
                        pool.wait_ge(n.added, k - 1)
                    pool.tensor_tensor(n.total, sq[:, 0, :] if k == 1 else n.total, sq[:, k % 2, :],
                                       ALU.add).then_inc(n.added, 1)
                if between:
                    between(k)

        def pe_stat(pe, n):
            pe.wait_ge(n.added, KC - 1)
            pe.matmul(PS[:, STAT, :], ones[:, :], n.total, start=True, stop=True).then_inc(norm_summed, 1)

        def act_inverse(act, n):
            act.preload_act_table_set("natural_log_exp_and_others")
            act.wait_ge(norm_summed, n.at)
            act.activation(rstd[:, :], PS[:, STAT, :], ACT.Ln, bias=epsc[:, 0:1]).then_inc(norm_log, 1)
            act.wait_ge(norm_log, n.at)
            act.activation(rstd[:, :], rstd[:, :], ACT.Exp, scale=-0.5).then_inc(norm_inverse, 1)

        def act_fold(act, n, unit=None):
            for k in range(KC + 2):
                if k < KC:
                    n.wait_ready(act, k)
                    act.activation(H_hi[:, k, :], X[:, k, :], ACT.Copy, scale=pc(n.name, k)).then_inc(n.hi, 1)
                if k >= 2:
                    act_square(act, n, k - 2)
            if unit is not None:
                unit()
            act_inverse(act, n)

        def dve_fold(dve, n):
            for k in range(KC):
                dve.wait_ge(n.hi, k + 1)
                dve.scalar_tensor_tensor(out=H_lo[:, k, :], in0=X[:, k, :], scalar=pc(n.name, k),
                                         in1=H_hi[:, k, :].bitcast(F32), op0=ALU.mult,
                                         op1=ALU.subtract).then_inc(n.done, 1)
            dve.wait_ge(norm_inverse, n.at)

        def pe_first_pair(pe, n, u0):
            pe.wait_ge(lo_done, u0 + 2)
            for k in range(KC):
                pe.wait_ge(n.hi, max(k + 1, 2))
                for j in range(2):
                    for w in (w_hi, w_lo):
                        pe.matmul(PS[:, j, :], w[:, (u0 + j) % RING, bass.ts(k, P)], H_hi[:, k, :],
                                  start=(k == 0 and w is w_hi), stop=False)
            for j in range(2):
                for k in range(KC):
                    if j == 0:
                        pe.wait_ge(n.done, k + 1)
                    m = pe.matmul(PS[:, j, :], w_hi[:, (u0 + j) % RING, bass.ts(k, P)], H_lo[:, k, :],
                                  start=False, stop=(k == KC - 1))
                m.then_inc(unit_done, 1)

        def dve_post(dve, n):
            dve.wait_ge(norm_inverse, n.at)
            for k in range(KC):
                if k >= 2:
                    dve.wait_ge(n.odd if k % 2 else n.even, k // 2)
                dve.scalar_tensor_tensor(out=tmp[:, k % 2, :], in0=n.src[:, k, :], scalar=pc(n.name, k),
                                         in1=rstd[:, :], op0=ALU.mult, op1=ALU.mult).then_inc(n.scaled, 1)
                if k % 2:
                    dve.wait_ge(n.scaled, k + 1)
                    dve.tensor_tensor(X[:, k, :], X[:, k, :], tmp[:, 1, :], ALU.add).then_inc(n.odd, 1)

        def pool_post(pool, n):
            for k in range(0, KC, 2):
                pool.wait_ge(n.scaled, k + 1)
                pool.tensor_tensor(X[:, k, :], X[:, k, :], tmp[:, 0, :], ALU.add).then_inc(n.even, 1)

        def split_matmul(pe, out, w_slot, w_cols, h_hi, h_lo, first, last, skip=False):
            a, b = w_hi[:, w_slot, w_cols], w_lo[:, w_slot, w_cols]
            pe.matmul(out, a, h_hi, start=first, stop=False, skip_group_check=skip)
            pe.matmul(out, a, h_lo, start=False, stop=False, skip_group_check=skip)
            return pe.matmul(out, b, h_hi, start=False, stop=last, skip_group_check=skip)

        def pe_chunk(pe, slot, bank):
            for k in range(KC):
                m = split_matmul(pe, PS[:, bank, :], slot, bass.ts(k, P), H_hi[:, k, :], H_lo[:, k, :],
                                 k == 0, k == KC - 1)
            m.then_inc(unit_done, 1)

        def pe_by_token(pe, u0, bank0, width, free=None):
            for t in range(4):
                u = u0 + t
                pe.wait_ge(lo_done, u + 1)
                for tb in range(TB):
                    for kk in range(2):
                        k = 2 * t + kk
                        wh = w_hi[:, u % RING, kk * T:kk * T + width]
                        wl = w_lo[:, u % RING, kk * T:kk * T + width]
                        hh, hl = H_hi[:, k, bass.ts(tb, P)], H_lo[:, k, bass.ts(tb, P)]
                        o = PS[:, bank0 + tb, 0:width]
                        pe.matmul(o, hh, wh, start=(k == 0), stop=False)
                        pe.matmul(o, hh, wl, start=False, stop=False)
                        m = pe.matmul(o, hl, wh, start=False, stop=(k == KC - 1))
                m.then_inc(unit_done, 1)

        def act_hi(act, slot, u=None, n_loaded=None, wait_free=True):
            if wait_free:
                act.wait_ge(unit_done, u - RING + 1)
            act.wait_ge(loaded[slot], n_loaded)
            act.activation(w_hi[:, slot, :], stage[:, slot, :], ACT.Copy).then_inc(hi_done, 1)

        def act_hi_static(act, u):
            v = u + RING
            if v < N_UNITS:
                act_hi(act, v % RING, v, 16 * (v // RING + 1))
            else:
                act.wait_ge(unit_done, u + 1)

        ffn_free = sem("ffn_free")
        zs = sem("zs")
        conv_in = sem("conv_in")
        conv_step = sem("conv_step")
        gated = sem("gated")
        prod = sem("prod")
        y_odd = sem("y_odd")
        y_done = [sem(f"y_done{i}") for i in range(3)]

        def pe_ffn(pe, inst, u_up, u_dn, norm):
            g0 = inst * FC
            pe_first_pair(pe, norm, u_up)
            pe_stat(pe, norm)
            for i in range(2, 4):
                pe.wait_ge(lo_done, u_up + i + 1)
                if i == 2:
                    pe.wait_ge(ffn_free, g0 + 2)
                pe_chunk(pe, (u_up + i) % RING, i)
            with pe.Fori(1, FC // 2) as r:
                for i in range(4):
                    pe.wait_ge(lo_done, r * 4 + (u_up + i + 1))
                    if i % 2 == 0:
                        pe.wait_ge(ffn_free, r * 2 + (g0 + i // 2 + 1))
                    pe_chunk(pe, (u_up + i) % RING, i)

            def down(slot, a_hi, a_lo, first, last):
                for at, m in enumerate(FIRST_ORDER if first else range(KC)):
                    if first and at == 4:
                        pe.wait_ge(ffn_free, g0 + FC + 2)
                    mm = split_matmul(pe, PS[:, m, :], slot, bass.ts(m, P), a_hi, a_lo, first, last)
                    if last:
                        mm.then_inc(y_done[inst], 1)
                if not last:
                    mm.then_inc(unit_done, 1)
                else:
                    pe.wait_ge(y_done[inst], KC)
                    pe.sem_inc(unit_done, 1)

            pe.wait_ge(lo_done, u_dn + 1)
            down(u_dn % RING, A_hi[:, 0, :], A_lo[:, 0, :], True, False)
            with pe.Fori(0, (FC - 2) // 4) as r:
                for i in range(4):
                    pe.wait_ge(lo_done, r * 4 + (u_dn + i + 2))
                    f = bass.ds(r * 4 + (i + 1), 1)
                    down((u_dn + i + 1) % RING, A_hi[:, f, :].rearrange("p a n -> p (a n)"),
                         A_lo[:, f, :].rearrange("p a n -> p (a n)"), False, False)
            pe.wait_ge(lo_done, u_dn + FC)
            down((u_dn + FC - 1) % RING, A_hi[:, FC - 1, :], A_lo[:, FC - 1, :], False, True)

        def act_ffn(act, inst, u_up, u_dn, convolved):
            g0 = inst * FC
            with act.Fori(0, FC // 2) as r:
                for i in range(2):
                    ua, ub = u_up + 2 * i, u_up + 2 * i + 1
                    act.wait_ge(unit_done, r * 4 + (ub + 1))
                    act.wait_ge(ffn_free, r * 2 + (g0 + i + 1))
                    va, vb = ua + RING, ub + RING
                    act_hi(act, va % RING, None, r * 16 + 16 * (va // RING + 1), wait_free=False)
                    fe = r * 2 + i
                    if convolved:
                        act.wait_ge(zs, r * 4 + (2 * g0 + 2 * i + 2))
                    act_hi(act, vb % RING, None, r * 16 + 16 * (vb // RING + 1), wait_free=False)
                    if convolved:
                        for j in range(2):
                            c2 = par[:, bass.ds(fe + (PARAMS["conv_w"][0] + (2 * 2 + j) * FC), 1)]
                            cb = par[:, bass.ds(fe + (PARAMS["conv_b"][0] + j * FC), 1)]
                            act.activation(conv[:, i, j, :], tmp[:, j, :], ACT.Identity,
                                           bias=cb, scale=c2).then_inc(conv_in, 1)
                        act.wait_ge(conv_step, r * 8 + 4 * i + 3)
                        act.activation(conv[:, i, 0, :], conv[:, i, 0, :], ACT.Gelu_apprx_tanh).then_inc(gated, 1)
                    else:
                        act.wait_ge(zs, r * 4 + (2 * g0 + 2 * i + 1))
                        act.activation(conv[:, i, 0, :], conv[:, i, 0, :], ACT.Silu).then_inc(gated, 1)
            rounds = FC // 4 if u_dn + FC < N_UNITS else FC // 4 - 1
            with act.Fori(0, rounds) as r:
                for i in range(4):
                    v = u_dn + i + RING
                    act_hi(act, v % RING, r * 4 + v, r * 16 + 16 * (v // RING + 1))
            for u in range(u_dn + rounds * 4, u_dn + FC - 1):
                act_hi_static(act, u)

        def dve_ffn(dve, inst, u_up, convolved):
            g0 = inst * FC
            with dve.Fori(0, FC // 2) as r:
                for i in range(2):
                    fe = r * 2 + i
                    z = [tmp[:, j, :] if convolved else conv[:, i, j, :] for j in range(2)]
                    dve.wait_ge(ffn_free, r * 2 + (g0 + i + 1))
                    dve.wait_ge(unit_done, r * 4 + (u_up + 2 * i + 2))
                    for j in range(2):
                        dve.tensor_tensor(z[j], PS[:, 2 * i + j, :], rstd[:, :], ALU.mult).then_inc(zs, 1)
                    if convolved:
                        def tap(back, j):
                            c = par[:, bass.ds(fe + (PARAMS["conv_w"][0] + (2 * (2 - back) + j) * FC), 1)]
                            y = conv[:, i, j, back:T]
                            dve.scalar_tensor_tensor(out=y, in0=z[j][:, 0:T - back], scalar=c, in1=y,
                                                     op0=ALU.mult, op1=ALU.add).then_inc(conv_step, 1)
                        for j in range(2):
                            dve.wait_ge(conv_in, r * 4 + 2 * i + j + 1)
                            tap(1, j)
                        for j in range(2):
                            dve.wait_ge(conv_step, r * 8 + 4 * i + j + 1)
                            tap(2, j)
                        dve.wait_ge(conv_step, r * 8 + 4 * i + 4)
                    value = conv[:, i, 1, :]
                    dve.wait_ge(zs, r * 4 + (2 * g0 + 2 * i + 2))
                    dve.wait_ge(gated, r * 2 + (g0 + i + 1))
                    f = bass.ds(fe, 1)
                    ah = A_hi[:, f, :].rearrange("p a n -> p (a n)")
                    al = A_lo[:, f, :].rearrange("p a n -> p (a n)")
                    dve.tensor_tensor(ah, conv[:, i, 0, :], value, ALU.mult).then_inc(prod, 1)
                    dve.tensor_tensor(conv[:, i, 0, :], conv[:, i, 0, :], value, ALU.mult).then_inc(prod, 1)
                    dve.wait_ge(prod, r * 4 + (2 * g0 + 2 * i + 2))
                    dve.tensor_tensor(al, conv[:, i, 0, :], ah.bitcast(F32), ALU.subtract).then_inc(ffn_free, 1)

        class Item:

            def __init__(self, kind, i, keys, group, maps, v, out, bias=None, add=False, gate=None, sink=None):
                self.kind, self.i, self.group, self.maps, self.v, self.out = kind, i, group, maps, v, out
                self.k0, self.nk = keys
                self.bias, self.add, self.gate, self.sink = bias, add, gate, sink

        def full(i):
            return 0, (i + 1) * P, (TB - 1 - i) * P

        def qk_tiles(qt, kt, i, k0, nk):
            return [(QD_hi[qt][:, bass.ts(i, P)], K2[kt][:, k0:k0 + nk]),
                    (QD_lo[qt][:, bass.ts(i, P)], K2[kt][:, k0:k0 + nk])]

        def item(items, **what):
            items.append(Item(**what))

        items1, items2, groups1, groups2 = [], [], [], []
        for p in range(8):
            c, t0 = p // 2, 2 * (p % 2)
            groups1.append(len(items1))
            for i in range(TB):
                k0, nk, s0 = full(i)
                if p % 2 == 0:
                    item(items1, kind="diff", i=i, keys=(k0, nk), group=p,
                         maps=[qk_tiles(t0 + m, t0 + m, i, k0, nk) for m in range(2)],
                         bias=strip[:, c, s0:s0 + nk],
                         v=[V[:, 0, kb, bass.ts(c, P)] for kb in range(nk // P)],
                         out=O[:, i, bass.ts(c, P)])
                else:
                    for m in range(2):
                        h = 2 * c + m
                        item(items1, kind="sb", i=i, keys=(k0, nk), group=p,
                             maps=[qk_tiles(t0 + m, t0 + m, i, k0, nk)],
                             v=[V[:, 1, kb, bass.ts(h, HD)] for kb in range(nk // P)],
                             out=O[:, i, T + h * HD:T + (h + 1) * HD])
        for p in range(8):
            c, t0 = p % 4, 2 * (p % 2)
            groups2.append(len(items2))
            for i in range(TB):
                for g in range(2):
                    h = 4 * g + c
                    if p < 4:
                        k0, nk, s0 = full(i)
                        for branch in range(2):
                            item(items2, kind="soft", i=i, keys=(k0, nk), group=p,
                                 maps=[qk_tiles(t0 + g, 2 * branch + g, i, k0, nk)],
                                 bias=strip[:, h, s0:s0 + nk],
                                 v=[V[:, 0, kb, branch * P + g * HD:branch * P + (g + 1) * HD] for kb in range(nk // P)],
                                 out=O[:, i, bass.ts(h, HD)], add=(branch == 1),
                                 gate=gates[:, i, 3 * h + 1 + branch:3 * h + 2 + branch], sink=None)
                    else:
                        k0, nk = max(i - 1, 0) * P, min(i + 1, 2) * P
                        item(items2, kind="soft", i=i, keys=(k0, nk), group=p,
                             maps=[qk_tiles(t0 + g, 4 + g, i, k0, nk)],
                             bias=swa_strip(h)[:, 256 - nk:256],
                             v=[V[:, 0, k0 // P + kb, 2 * P + g * HD:2 * P + (g + 1) * HD] for kb in range(nk // P)],
                             out=O[:, i, T + h * HD:T + (h + 1) * HD], add=False, gate=None,
                             sink=row[:, ROW_SINK + h:ROW_SINK + h + 1])
        for items in (items1, items2):
            pre = 0
            for n, it in enumerate(items):
                it.n = n
                it.dv = it.out.shape[-1]
                it.st = stat[:, n % 4, :]
                pre += it.kind == "sb"
                it.pre = pre

        class Attn:
            def __init__(self, name, items, groups, scale):
                self.name, self.items, self.groups, self.scale = name, items, groups, scale
                self.preps = []
                self.prep_hi = sem(f"{name}_prep_hi")
                self.prep_lo = sem(f"{name}_prep_lo")
                self.moved = [sem(f"{name}_moved{i}") for i in range(4)]
                self.hooks = {"pe": {}, "act": {}, "dve": {}}
                self.qk_done = sem(f"{name}_qk_done")
                self.s_read = sem(f"{name}_s_read")
                self.pre_done = sem(f"{name}_pre_done")
                self.logits = sem(f"{name}_logits")
                self.exp_done = sem(f"{name}_exp_done")
                self.comb = sem(f"{name}_comb")
                self.turned = sem(f"{name}_turned")
                self.wt_ready = sem(f"{name}_wt_ready")
                self.pv_done = sem(f"{name}_pv_done")
                self.o_done = sem(f"{name}_o_done")

        at1 = Attn("at1", items1, groups1, 1.0)
        at2 = Attn("at2", items2, groups2, SCALE)

        class Prep:

            def __init__(self, a, chunk, keys, tiles, slot, group, free_after=0, own=None):
                n = len(a.preps)
                self.a, self.chunk, self.keys, self.tiles, self.slot, self.group = a, chunk, keys, tiles, slot, group
                self.free_after = free_after
                self.n = n
                self.moved = own or a.moved[n % 4]
                self.count = 16 * (4 if keys else 8)
                for q in a.preps:
                    if q.moved is self.moved:
                        self.count += 16 * (4 if q.keys else 8)
                self.after = []
                a.preps.append(self)

            def act_split(self, act):
                for q in self.after:
                    act.wait_ge(q.moved, q.count)
                act.activation(self.slot[0], QK[:, self.chunk, :], ACT.Copy).then_inc(self.a.prep_hi, 1)

            def dve_split(self, dve):
                dve.wait_ge(self.a.prep_hi, self.n + 1)
                dve.tensor_tensor(self.slot[1], QK[:, self.chunk, :], self.slot[0].bitcast(F32),
                                  ALU.subtract).then_inc(self.a.prep_lo, 1)

            def move(self, eng, parts=("hi", "lo")):
                if "lo" in parts:
                    eng.wait_ge(self.a.prep_lo, self.n + 1)
                else:
                    eng.wait_ge(self.a.prep_hi, self.n + 1)
                if self.free_after:
                    eng.wait_ge(self.a.qk_done, self.free_after)
                hi, lo = self.slot
                for m in range(2):
                    rows = slice(m * HD, (m + 1) * HD)
                    if self.keys:
                        to = [(K2[self.tiles[m]], "hi", 0), (K2[self.tiles[m]], "lo", 1)]
                    else:
                        to = [(QD_hi[self.tiles[m]], "hi", 0), (QD_hi[self.tiles[m]], "hi", 1),
                              (QD_lo[self.tiles[m]], "lo", 0), (QD_lo[self.tiles[m]], "lo", 1)]
                    for dst, part, half in to:
                        if part not in parts:
                            continue
                        src = hi if part == "hi" else lo
                        eng.dma_start(dst[half * HD:(half + 1) * HD, :].bitcast(F32),
                                      src[rows, :].bitcast(F32)).then_inc(self.moved, 16)

        def hook(a, engine, step, what):
            a.hooks[engine].setdefault(step, []).append(what)

        slots1 = [(H_hi[:, 6, :], H_hi[:, 7, :]), (H_hi[:, 4, :], H_hi[:, 5, :])]
        for p in range(8):
            for keys in (False, True):
                q = Prep(at1, 2 * p + keys, keys, [2 * (p % 2), 2 * (p % 2) + 1], slots1[keys], p,
                         groups1[p - 1] if p >= 2 else 0)
                if p:
                    q.after = [at1.preps[2 * (p - 1) + keys]]
                if p >= 1:
                    step = groups1[p - 1]
                    hook(at1, "act", step, q.act_split)
                    hook(at1, "dve", step, q.dve_split)
        slot_a, slot_b, slot_c = (H_hi[:, 6, :], H_hi[:, 7, :]), (QD_hi[2], QD_hi[3]), (QD_lo[2], QD_lo[3])
        ks_, kw_ = Prep(at2, 4, True, [0, 1], slot_b, 0), Prep(at2, 5, True, [2, 3], slot_c, 0, own=sem("kw_moved"))
        q0 = Prep(at2, 0, False, [0, 1], slot_a, 0)
        last = q0
        for p in range(1, 8):
            c = p if p < 4 else 8 + p - 4
            q = Prep(at2, c, False, [2 * (p % 2), 2 * (p % 2) + 1], slot_a, p, groups2[p - 1] if p >= 2 else 0)
            q.after = [last] + ([ks_, kw_] if p == 1 else [])
            last = q
            step = groups2[p - 1] + 1
            hook(at2, "act", step, q.act_split)
            hook(at2, "dve", step, q.dve_split)
            if p == 3:
                kb_ = Prep(at2, 12, True, [4, 5], slot_a, 4)
                kb_.after = [last]
                last = kb_
                hook(at2, "act", step + 6, kb_.act_split)
                hook(at2, "dve", step + 6, kb_.dve_split)
        v_ready = [sem("v_ready1"), sem("v_ready2")]
        strips_done = [sem("strips_done1"), sem("strips_done2")]

        def pe_attn(pe, a):
            items = a.items
            for n in range(len(items) + 3):
                if n < len(items):
                    it = items[n]
                    if n >= 2:
                        pe.wait_ge(a.s_read, n - 1)
                    if n in a.groups:
                        for q in a.preps:
                            if q.group == it.group:
                                pe.wait_ge(q.moved, q.count)
                    for m, passes in enumerate(it.maps):
                        for x, (q, k) in enumerate(passes):
                            mm = pe.matmul(PS[:, 2 * (n % 2) + m, 0:it.nk], q, k, start=(x == 0), stop=(x == 1))
                            if x == 0 and it.kind == "sb":
                                pe.matmul(PS[:, 2 * (n % 2) + m, it.nk - P:it.nk], ident_r[:, :], mask_r[:, :],
                                          start=False, stop=False)
                    mm.then_inc(a.qk_done, 1)
                if 2 <= n < len(items) + 2:
                    it = items[n - 2]
                    pe.wait_ge(a.comb if it.kind == "diff" else a.exp_done, it.n + 1)
                    if it.n >= 2:
                        pe.wait_ge(a.wt_ready, it.n - 1)
                    for kb in range(it.nk // P):
                        mm = pe.transpose(PS[:, 4 + it.n % 2, bass.ts(kb, P)], W[:, it.n % 2, bass.ts(kb, P)], ident[:, :])
                    mm.then_inc(a.turned, 1)
                if n >= 3:
                    it = items[n - 3]
                    pe.wait_ge(a.wt_ready, it.n + 1)
                    if it.n >= 2:
                        pe.wait_ge(a.o_done, it.n - 1)
                    for kb in range(it.nk // P):
                        mm = pe.matmul(PS[:, 6 + it.n % 2, 0:it.dv], WT[:, it.n % 2, bass.ts(kb, P)], it.v[kb],
                                       start=(kb == 0), stop=(kb == it.nk // P - 1))
                    mm.then_inc(a.pv_done, 1)
                for what in a.hooks["pe"].get(n, []):
                    what(pe)

        def act_attn(act, a, link, after):
            items = a.items
            for n in range(len(items) + 2):
                if n < len(items) and items[n].kind == "sb":
                    it = items[n]
                    if n >= 2:
                        act.wait_ge(a.comb if items[n - 2].kind == "diff" else a.logits, n - 1)
                    act.wait_ge(a.qk_done, n + 1)
                    z = LM(0, n)[:, 0:it.nk]
                    c = link(act.activation(z, PS[:, 2 * (n % 2), 0:it.nk], ACT.Abs))
                    after(c)
                    c = link(act.activation(z, z, ACT.Exp, scale=-1.0))
                    after(c)
                    act.activation(z, z, ACT.Ln, bias=1.0).then_inc(a.pre_done, 1)
                if 1 <= n < len(items) + 1:
                    it = items[n - 1]
                    if it.kind != "diff" and it.n >= 2:
                        act.wait_ge(a.turned, it.n - 1)
                    act.wait_ge(a.logits, it.n + 1)
                    if it.kind == "sb":
                        act.activation(W[:, it.n % 2, 0:it.nk], LM(1, it.n)[:, 0:it.nk], ACT.Exp).then_inc(a.exp_done, 1)
                    elif it.kind == "diff":
                        for m in range(2):
                            z = LM(m, it.n)[:, 0:it.nk]
                            x = act.activation(z, z, ACT.Exp, bias=it.st[:, 2 + m:3 + m], accum_out=it.st[:, 4 + m:5 + m])
                        x.then_inc(a.exp_done, 1)
                    else:
                        if it.sink is not None:
                            act.activation(it.st[:, 5:6], it.sink, ACT.Exp, bias=it.st[:, 2:3])
                        act.activation(W[:, it.n % 2, 0:it.nk], LM(0, it.n)[:, 0:it.nk], ACT.Exp,
                                       bias=it.st[:, 2:3], accum_out=it.st[:, 4:5]).then_inc(a.exp_done, 1)
                if n >= 2:
                    it = items[n - 2]
                    act.wait_ge(a.turned, it.n + 1)
                    if it.n >= 2:
                        act.wait_ge(a.pv_done, it.n - 1)
                    act.activation(WT[:, it.n % 2, 0:it.nk], PS[:, 4 + it.n % 2, 0:it.nk], ACT.Copy).then_inc(a.wt_ready, 1)
                for what in a.hooks["act"].get(n, []):
                    what(act)

        def dve_attn(dve, a, link, after):
            items = a.items
            for n in range(len(items) + 4):
                if n < len(items):
                    it = items[n]
                    dve.wait_ge(a.qk_done, n + 1)
                    if n >= 2:
                        dve.wait_ge(a.exp_done, n - 1)
                        dve.wait_ge(a.comb, n - 1)
                    S = PS[:, 2 * (n % 2), 0:it.nk]
                    if it.kind == "sb":
                        dve.wait_ge(a.pre_done, it.pre)
                        u, z = LM(0, n)[:, 0:it.nk], LM(1, n)[:, 0:it.nk]
                        c = link(dve.scalar_tensor_tensor(out=u, in0=S, scalar=0.0, in1=u, op0=ALU.max, op1=ALU.add))
                        after(c)
                        c = link(dve.tensor_tensor_scan(z[:, ::-1], u[:, ::-1], u[:, ::-1], 0.0, ALU.add, ALU.max))
                        after(c)
                        dve.tensor_tensor(z, S, z, ALU.subtract).then_inc(a.logits, 1)
                        dve.wait_ge(a.logits, n + 1)
                        dve.sem_inc(a.s_read, 1)
                    else:
                        for m in range(len(it.maps)):
                            c = link(dve.tensor_tensor_reduce(
                                out=LM(m, n)[:, 0:it.nk], in0=PS[:, 2 * (n % 2) + m, 0:it.nk], in1=it.bias,
                                scale=a.scale, scalar=-3e38, op0=ALU.add, op1=ALU.max, accum_out=it.st[:, m:m + 1]))
                        after(c)
                        dve.sem_inc(a.s_read, 1)
                        nm = len(it.maps)
                        if it.kind == "soft" and it.sink is not None:
                            dve.tensor_scalar(it.st[:, 2:3], it.st[:, 0:1], it.sink, -1.0, ALU.max, ALU.mult).then_inc(a.logits, 1)
                        else:
                            dve.tensor_scalar(it.st[:, 2:2 + nm], it.st[:, 0:nm], -1.0, None, ALU.mult).then_inc(a.logits, 1)
                if 1 <= n < len(items) + 1:
                    it = items[n - 1]
                    dve.wait_ge(a.exp_done, it.n + 1)
                    if it.kind == "sb":
                        dve.sem_inc(a.comb, 1)
                    elif it.kind == "diff":
                        if it.n >= 2:
                            dve.wait_ge(a.turned, it.n - 1)
                        c = link(dve.reciprocal(it.st[:, 6:8], it.st[:, 4:6]))
                        after(c)
                        c = link(dve.tensor_scalar(it.st[:, 7:8], it.st[:, 7:8], small[:, 0:1], it.st[:, 4:5],
                                                   ALU.mult, ALU.mult))
                        after(c)
                        z0, z1 = LM(0, it.n)[:, 0:it.nk], LM(1, it.n)[:, 0:it.nk]
                        dve.scalar_tensor_tensor(out=W[:, it.n % 2, 0:it.nk], in0=z1, scalar=it.st[:, 7:8], in1=z0,
                                                 op0=ALU.mult, op1=ALU.add).then_inc(a.comb, 1)
                    else:
                        if it.sink is not None:
                            after(link(dve.tensor_tensor(it.st[:, 4:5], it.st[:, 4:5], it.st[:, 5:6], ALU.add)))
                        c = link(dve.reciprocal(it.st[:, 6:7], it.st[:, 4:5]))
                        after(c)
                        if it.gate is not None:
                            c = link(dve.tensor_tensor(it.st[:, 6:7], it.st[:, 6:7], it.gate, ALU.mult))
                            after(c)
                        dve.sem_inc(a.comb, 1)
                if n >= 4:
                    it = items[n - 4]
                    dve.wait_ge(a.pv_done, it.n + 1)
                    pv = PS[:, 6 + it.n % 2, 0:it.dv]
                    if it.kind == "soft" and it.add:
                        dve.scalar_tensor_tensor(out=it.out, in0=pv, scalar=it.st[:, 6:7], in1=it.out,
                                                 op0=ALU.mult, op1=ALU.add).then_inc(a.o_done, 1)
                    elif it.kind != "sb":
                        dve.tensor_scalar(it.out, pv, it.st[:, 6:7], None, ALU.mult).then_inc(a.o_done, 1)
                    else:
                        dve.tensor_copy(it.out, pv).then_inc(a.o_done, 1)
                    dve.wait_ge(a.o_done, it.n + 1)
                for what in a.hooks["dve"].get(n, []):
                    what(dve)

        o_ready = [sem("o_ready1"), sem("o_ready2")]
        o_turned = [sem("o_turned1"), sem("o_turned2")]
        o_hi = [sem("o_hi1"), sem("o_hi2")]
        o_split = [sem("o_split1"), sem("o_split2")]

        def pe_turn(pe, b):
            for n in range(2 * TB):
                half, i = n // TB, n % TB
                pe.wait_ge(o_ready[b], 7 + half)
                if n >= 4:
                    pe.wait_ge(o_split[b], n - 3)
                for c in range(4):
                    mm = pe.transpose(PS[:, n % 4, bass.ts(c, P)], O[:, i, bass.ts(half * 4 + c, P)], ident[:, :])
                mm.then_inc(o_turned[b], 1)

        def turned_aps(n):
            half, i = n // TB, n % TB
            src = PS[:, n % 4, :].rearrange("p (c n) -> p c n", c=4)
            return src, H_hi[:, 4 * half:4 * half + 4, bass.ts(i, P)], H_lo[:, 4 * half:4 * half + 4, bass.ts(i, P)]

        def act_turn(act, b):
            for n in range(2 * TB):
                src, hi, _ = turned_aps(n)
                act.wait_ge(o_turned[b], n + 1)
                act.activation(hi, src, ACT.Copy).then_inc(o_hi[b], 1)

        def dve_turn(dve, b):
            for n in range(2 * TB):
                src, hi, lo = turned_aps(n)
                dve.wait_ge(o_hi[b], n + 1)
                dve.tensor_tensor(lo, src, hi.bitcast(F32), ALU.subtract).then_inc(o_split[b], 1)

        def pe_wo(pe, b, u0):
            for j in range(KC):
                pe.wait_ge(lo_done, u0 + j + 1)
                if j == 0:
                    pe.wait_ge(o_split[b], 2 * TB)
                pe_chunk(pe, (u0 + j) % RING, j)

        head_sq = sem("head_sq")
        head_sum = sem("head_sum")
        head_ln = sem("head_ln")
        head_root = sem("head_root")
        head_mul = sem("head_mul")
        gain_ready = sem("gain_ready")

        def head_group(p):
            c = p // 2
            heads = 1 if p % 2 == 0 else 2
            cols = O[:, :, (T if p % 2 else 0) + c * P:(T if p % 2 else 0) + (c + 1) * P]
            done = groups1[p + 1] if p < 7 else len(items1)
            return cols, heads, done

        def pool_heads(pool):
            at1.preps[3].move(pool)
            for p in range(8):
                if p + 2 < 8:
                    at1.preps[2 * (p + 2) + 1].move(pool)
                cols, heads, done = head_group(p)
                pool.wait_ge(at1.o_done, done)
                z = scratch[:, 0:T].rearrange("p (i d) -> p i d", i=TB)
                pool.tensor_tensor(z, cols, cols, ALU.mult).then_inc(head_sq, 1)
                pool.wait_ge(head_root, p + 1)
                if heads == 1:
                    x = cols
                    r = small[:, 24:24 + TB].unsqueeze(2).to_broadcast([P, TB, P])
                    g = row[:, ROW_SUB:ROW_SUB + P].unsqueeze(1).to_broadcast([P, TB, P])
                    pool.wait_ge(gain_ready, 1)
                    pool.tensor_tensor(x, x, r, ALU.mult).then_inc(head_mul, 1)
                    pool.wait_ge(head_mul, 2 * p + 1)
                    pool.tensor_tensor(x, x, g, ALU.mult).then_inc(head_mul, 1)
                    pool.wait_ge(head_mul, 2 * p + 2)
                else:
                    x = cols.rearrange("p i (h d) -> p i h d", h=2)
                    r = small[:, 24:24 + 2 * TB].rearrange("p (i h) -> p i h", h=2).unsqueeze(3).to_broadcast([P, TB, 2, HD])
                    g = row[:, ROW_SBN:ROW_SBN + HD].unsqueeze(1).unsqueeze(2).to_broadcast([P, TB, 2, HD])
                    pool.tensor_tensor(x, x, r, ALU.mult).then_inc(head_mul, 1)
                    pool.wait_ge(head_mul, 2 * p + 1)
                    pool.tensor_tensor(x, x, g, ALU.mult).then_inc(head_mul, 1)
                    pool.wait_ge(head_mul, 2 * p + 2)
                pool.sem_inc(o_ready[0], 1)

        def dve_head(p):
            def what(dve):
                _, heads, _ = head_group(p)
                dve.wait_ge(head_sq, p + 1)
                dve.tensor_reduce(small[:, 16:16 + heads * TB], scratch[:, 0:T].rearrange(
                    "p (n d) -> p n d", n=heads * TB), AX_X, ALU.add).then_inc(head_sum, 1)
            return what

        def act_head(p):
            def what(act):
                _, heads, _ = head_group(p)
                act.wait_ge(head_sum, p + 1)
                a, r = small[:, 16:16 + heads * TB], small[:, 24:24 + heads * TB]
                act.activation(r, a, ACT.Ln, bias=epsc[:, 0:1], scale=heads / P).then_inc(head_ln, 1)
                act.wait_ge(head_ln, p + 1)
                act.activation(r, r, ACT.Exp, scale=-0.5).then_inc(head_root, 1)
            return what

        for p in range(7):
            hook(at1, "dve", groups1[p + 1] + 5, dve_head(p))
            hook(at1, "act", groups1[p + 1] + 6, act_head(p))

        rcol_turned = sem("rcol_turned")
        rcol_done = sem("rcol_done")

        def pe_rcol(pe, n):
            pe.wait_ge(norm_inverse, n.at)
            for tb in range(TB):
                mm = pe.transpose(PS[:, STAT, bass.ts(tb, P)], rstd[:, bass.ts(tb, P)], ident[:, :])
            mm.then_inc(rcol_turned, 1)

        def dve_rcol(dve, b):
            dve.wait_ge(rcol_turned, b + 1)
            dve.tensor_copy(rcol[:, :], PS[:, STAT, :].rearrange("p (b c) -> p b c", b=TB)[:, :, 0]).then_inc(rcol_done, 1)

        qk_evac = [sem("qk_evac1"), sem("qk_evac2")]
        cm = {k: sem("cm_" + k) for k in (
            "raw", "kp", "kp_hi", "kp_lo", "mlp", "pre_t", "hid", "kv", "kv_sb", "z", "zz", "s", "l", "e", "p", "t", "pt", "pv", "used")}
        gate_e = sem("gate_e")
        lam_e = sem("lam_e")


        def pe_mlp(s, piece):
            def what(pe):
                t, half = piece // 2, piece % 2
                u = U_CMP + 4 * s + t
                if piece == 0:
                    pe.wait_ge(cm["kp_lo"], s + 1)
                    if s == 1:
                        pe.wait_ge(cm["mlp"], 1)
                if half == 0:
                    pe.wait_ge(lo_done, u + 1)
                for j4 in range(2 * half, 2 * half + 2):
                    j = 4 * t + j4
                    cols = slice(j4 * CMP_HID, (j4 + 1) * CMP_HID)
                    o = PS[0:2 * NCMP, 1, 0:CMP_HID]
                    pe.matmul(o, kp_hi[:, j, :], w_hi[:, u % RING, cols], start=(j == 0), stop=False)
                    pe.matmul(o, kp_hi[:, j, :], w_lo[:, u % RING, cols], start=False, stop=False)
                    mm = pe.matmul(o, kp_lo[:, j, :], w_hi[:, u % RING, cols], start=False, stop=(j == 15))
                if half == 1:
                    mm.then_inc(unit_done, 1)
            return what

        def act_unit(u):
            return lambda act: act_hi_static(act, u)

        def dve_windows(s):
            def what(dve):
                dve.wait_ge(cm["raw"], 64 * (s + 1))
                if s == 1:
                    dve.wait_ge(unit_done, U_CMP + 4)
                win = bass.AP(tensor=kpair.tensor, offset=kpair.offset,
                              ap=[kpair.ap[0], [2, 16], [T, 2], [CMP_STRIDE, NCMP]])
                pos = pc("pos_k" if s == 0 else "pos_v", 0, 16).unsqueeze(2).unsqueeze(3).to_broadcast([P, 16, 2, NCMP])
                dve.tensor_tensor(kp.rearrange("p j (g c) -> p j g c", g=2), win, pos, ALU.add).then_inc(cm["kp"], 1)
            return what

        def act_windows(s):
            def what(act):
                act.wait_ge(cm["kp"], s + 1)
                act.activation(kp_hi, kp, ACT.Copy).then_inc(cm["kp_hi"], 1)
            return what

        def dve_windows_lo(s):
            def what(dve):
                dve.wait_ge(cm["kp_hi"], s + 1)
                dve.tensor_tensor(kp_lo, kp, kp_hi.bitcast(F32), ALU.subtract).then_inc(cm["kp_lo"], 1)
            return what

        def act_hidden(s):
            def what(act):
                if s == 1:
                    act.wait_ge(cm["pre_t"], 1)
                act.wait_ge(unit_done, U_CMP + 4 * s + 4)
                act.activation(hidden, PS[0:2 * NCMP, 1, 0:CMP_HID], ACT.Copy).then_inc(cm["mlp"], 1)
            return what

        def pe_hidden(s):
            def what(pe):
                pe.wait_ge(cm["mlp"], s + 1)
                for half in range(2):
                    at = s * CMP_HID + half * P
                    mm = pe.transpose(PS[:, 3, at:at + 2 * NCMP], hidden[:, bass.ts(half, P)],
                                      ident[0:2 * NCMP, 0:2 * NCMP])
                mm.then_inc(cm["pre_t"], 1)
            return what

        def act_gelu(act):
            act.wait_ge(cm["pre_t"], 2)
            for s in range(2):
                for half in range(2):
                    at = s * CMP_HID + half * P
                    act.activation(hid[:, s, half, :], PS[:, 3, at:at + 2 * NCMP], ACT.Gelu_apprx_tanh,
                                   bias=pc("b1_k" if s == 0 else "b1_v", half)).then_inc(cm["hid"], 1)
            act.preload_act_table_set("natural_log_exp_and_others")

        def pe_second(pe):
            pe.wait_ge(cm["hid"], 4)
            for g in range(2):
                for half in range(2):
                    pe.matmul(PS[g * HD:(g + 1) * HD, 1, 0:NCMP], pc("w2_k", half * HD, HD),
                              hid[:, 0, half, g * NCMP:(g + 1) * NCMP], start=(half == 0), stop=(half == 1))
            for i in range(4):
                for g in range(2):
                    for half in range(2):
                        mm = pe.matmul(PS[32 * i:32 * i + NCMP, 3, g * HD:(g + 1) * HD],
                                       hid[:, 1, half, g * NCMP:(g + 1) * NCMP], pc("w2_v", half * HD, HD),
                                       start=(half == 0), stop=(half == 1))
            mm.then_inc(cm["kv"], 1)

        def act_second(act):
            act.wait_ge(cm["kv"], 1)
            act.activation(kcT[:, 0:NCMP], PS[:, 1, 0:NCMP], ACT.Copy).then_inc(cm["kv_sb"], 1)
            for i in range(4):
                act.activation(vc[32 * i:32 * i + NCMP, :, :], PS[32 * i:32 * i + NCMP, 3, 0:2 * HD].rearrange(
                    "p (g d) -> p g d", g=2), ACT.Copy).then_inc(cm["kv_sb"], 1)

        def pe_cmp_s(g, r):
            def what(pe):
                if g == 0 and r == 0:
                    pe.wait_ge(cm["kv_sb"], 5)
                for i in range(TB):
                    mm = pe.matmul(PS[:, 1 + 2 * g, r * P + i * 32:r * P + i * 32 + NCMP],
                                   QK[g * HD:(g + 1) * HD, r, bass.ts(i, P)], kcT[g * HD:(g + 1) * HD, 0:NCMP],
                                   start=True, stop=True)
                if r == 3:
                    mm.then_inc(cm["s"], 1)
            return what

        def cmp_logits(g):
            return cmp_L(g).rearrange("p (h c) -> p h c", c=32)[:, :, 0:NCMP]

        def dve_cmp_logits(g):
            def what(dve):
                dve.wait_ge(cm["s"], g + 1)
                dist = cdist[:, :].rearrange("p (i c) -> p i c", i=4)
                z = cmp_L(g).rearrange("p (h i c) -> p h i c", h=4, i=4)
                zs = PS[:, 1 + 2 * g, :].rearrange("p (h i c) -> p h i c", h=4, i=4)
                mx = small[:, 32:48]
                dve.memset(cmp_L(g), 0.0).then_inc(cm["z"], 1)
                dve.wait_ge(cm["z"], 7 * g + 1)
                for r in range(4):
                    f = -2.0 ** (-8.0 * (4 * g + r + 1) / N_NSA) / SCALE
                    dve.scalar_tensor_tensor(out=z[:, r, :, 0:NCMP], in0=dist[:, :, 0:NCMP], scalar=f,
                                             in1=zs[:, r, :, 0:NCMP], op0=ALU.mult, op1=ALU.add).then_inc(cm["z"], 1)
                dve.wait_ge(cm["z"], 7 * g + 5)
                dve.tensor_reduce(mx, cmp_logits(g), AX_X, ALU.max).then_inc(cm["z"], 1)
                dve.wait_ge(cm["z"], 7 * g + 6)
                dve.tensor_scalar(mx, mx, MASKED / SCALE, None, ALU.max).then_inc(cm["z"], 1)
                dve.wait_ge(cm["z"], 7 * g + 7)
                dve.tensor_tensor(cmp_logits(g), cmp_logits(g), mx.unsqueeze(2).to_broadcast([P, 16, NCMP]),
                                  ALU.subtract).then_inc(cm["l"], 1)
            return what

        def act_cmp_exp(g):
            def what(act):
                act.wait_ge(cm["l"], g + 1)
                act.activation(cmp_L(g), cmp_L(g), ACT.Exp, scale=SCALE).then_inc(cm["e"], 1)
            return what

        def dve_cmp_probs(g):
            def what(dve):
                mx = small[:, 32:48]
                dve.wait_ge(cm["e"], g + 1)
                dve.tensor_reduce(mx, cmp_logits(g), AX_X, ALU.add).then_inc(cm["zz"], 1)
                dve.wait_ge(cm["zz"], 4 * g + 1)
                dve.tensor_scalar(mx, mx, 0.5, None, ALU.max).then_inc(cm["zz"], 1)
                dve.wait_ge(cm["zz"], 4 * g + 2)
                dve.reciprocal(mx, mx).then_inc(cm["zz"], 1)
                dve.wait_ge(cm["zz"], 4 * g + 3)
                gv = gates[:, :, 12 * g:12 * g + 12].rearrange("p i (r b) -> p r i b", b=3)[:, :, :, 0]
                m4 = mx.rearrange("p (r i) -> p r i", i=4)
                dve.tensor_tensor(m4, m4, gv, ALU.mult).then_inc(cm["zz"], 1)
                dve.wait_ge(cm["zz"], 4 * g + 4)
                dve.tensor_tensor(cmp_logits(g), cmp_logits(g), mx.unsqueeze(2).to_broadcast([P, 16, NCMP]),
                                  ALU.mult).then_inc(cm["p"], 1)
            return what

        def pe_cmp_turn(g):
            def what(pe):
                pe.wait_ge(cm["p"], g + 1)
                for r in range(4):
                    mm = pe.transpose(PS[:, 1 + 2 * g, bass.ts(r, P)], cmp_L(g)[:, bass.ts(r, P)], ident[:, :])
                mm.then_inc(cm["t"], 1)
            return what

        def act_cmp_turn(g):
            def what(act):
                act.wait_ge(cm["t"], g + 1)
                act.activation(scratch[:, bass.ts(g, T)], PS[:, 1 + 2 * g, :], ACT.Copy).then_inc(cm["pt"], 1)
            return what

        def pe_cmp_pv(i, part):
            def what(pe):
                pe.wait_ge(cm["pt"], 2)
                if i >= 2:
                    pe.wait_ge(cm["used"], i - 1)
                for h in range(4 * part, 4 * part + 4):
                    mm = pe.matmul(PS[:, 1 + 2 * (i % 2), bass.ts(h, HD)], cmp_PT(h)[32 * i:32 * i + NCMP, :],
                                   vc[32 * i:32 * i + NCMP, h // 4, :], start=True, stop=True)
                if part == 1:
                    mm.then_inc(cm["pv"], 1)
            return what

        def dve_cmp_add(i):
            def what(dve):
                dve.wait_ge(cm["pv"], i + 1)
                o = O[:, i, 0:T]
                dve.tensor_tensor(o, PS[:, 1 + 2 * (i % 2), :], o, ALU.add).then_inc(cm["used"], 1)
            return what

        for s, at in ((0, 2), (1, 18)):
            hook(at2, "dve", at, dve_windows(s))
            hook(at2, "act", at + 1, act_windows(s))
            hook(at2, "dve", at + 2, dve_windows_lo(s))
            for piece in range(8):
                hook(at2, "pe", at + 4 + piece, pe_mlp(s, piece))
                if piece % 2:
                    hook(at2, "act", at + 6 + piece, act_unit(U_CMP + 4 * s + piece // 2))
            hook(at2, "act", at + 13, act_hidden(s))
            hook(at2, "pe", at + 15, pe_hidden(s))
        hook(at2, "act", 35, act_gelu)
        hook(at2, "pe", 37, pe_second)
        hook(at2, "act", 38, act_second)
        for g in range(2):
            for r in range(4):
                hook(at2, "pe", 40 + 4 * g + r, pe_cmp_s(g, r))
            hook(at2, "dve", 45 + 4 * g, dve_cmp_logits(g))
            hook(at2, "act", 46 + 4 * g, act_cmp_exp(g))
            hook(at2, "dve", 47 + 4 * g, dve_cmp_probs(g))
            hook(at2, "pe", 49 + 4 * g, pe_cmp_turn(g))
            hook(at2, "act", 50 + 4 * g, act_cmp_turn(g))
        for i, at in ((0, 58), (1, 61), (2, 72), (3, 75)):
            for part in range(2):
                hook(at2, "pe", at + part, pe_cmp_pv(i, part))
            hook(at2, "dve", (69, 70, 75, 78)[i], dve_cmp_add(i))

        @block.sync
        def _(sp):
            sp.dma_start(stage[:, 0, :], weights[0]).then_inc(loaded[0], 16)
            sp.dma_start(par[:, :], params).then_inc(par_loaded, 16)
            for half in range(2):
                sp.dma_start(X[:, 4 * half:4 * half + 4, :], x_t[:, 4 * half:4 * half + 4, :]).then_inc(x_loaded[half], 16)
                if half == 0:
                    sp.dma_start(stage[:, 1, :], weights[1]).then_inc(loaded[1], 16)
            sp.dma_start(row[:, :], rows.to_broadcast([P, N_ROW])).then_inc(row_loaded, 16)
            sp.dma_start(tab[:, :], table_t).then_inc(tab_loaded, 16)
            for u in range(2, RING):
                sp.dma_start(stage[:, u, :], weights[u]).then_inc(loaded[u], 16)
            sp.wait_ge(strips_done[0], 1)
            sp.dma_start(bias_line[:, :, 0:LINE], line[:, :].unsqueeze(1).to_broadcast([N_DIFF, P, LINE])).then_inc(line_out, 16)
            sp.wait_ge(line_out, 16)
            sp.dma_start(strip[:, 0:N_DIFF, :], bass.AP(
                tensor=bias_line.tensor, offset=P - 1,
                ap=[[LINE, P], [P * (LINE + 1), N_DIFF], [1, T]])).then_inc(strips_done[0], 16)

            def load(u0, u1):
                rounds = (u1 - u0) // RING if u1 - u0 > RING else 0
                if rounds:
                    with sp.Fori(0, rounds) as r:
                        for i in range(RING):
                            sp.wait_ge(lo_done, r * RING + (u0 + i + 1 - RING))
                            sp.dma_start(stage[:, (u0 + i) % RING, :], weights[u0 + i:u0 + rounds * RING:RING][
                                bass.ds(r, 1)].rearrange("a p n -> p (a n)")).then_inc(loaded[(u0 + i) % RING], 16)
                for u in range(u0 + rounds * RING, u1):
                    sp.wait_ge(lo_done, u + 1 - RING)
                    sp.dma_start(stage[:, u % RING, :], weights[u]).then_inc(loaded[u % RING], 16)

            load(RING, U_WO + 2 * RING - 1)
            at1.preps[0].move(sp, ("lo",))
            load(U_WO + 2 * RING - 1, U_WO + 2 * RING)
            for q in at1.preps[2::2]:
                q.move(sp)
            load(U_WO + 2 * RING, U_CMP + 2 * RING - 1)
            ks_.move(sp)
            q0.move(sp, ("lo",))
            for s in range(2):
                if s == 1:
                    sp.wait_ge(cm["kp"], 1)
                for g in range(2):
                    src = QK[g * HD:(g + 1) * HD, 6 + s, :]
                    sp.dma_start(kpair[0:HD, g, :], src).then_inc(cm["raw"], 16)
                    sp.dma_start(kpair[HD:P, g, 0:T - 1], src[:, 1:T]).then_inc(cm["raw"], 16)
            at2.preps[3].move(sp)
            load(U_CMP + 2 * RING - 1, U_CMP + 3 * RING)
            at2.preps[4].move(sp)
            load(U_CMP + 3 * RING, U_WO2 + 2 * RING)
            for q in at2.preps[5:]:
                q.move(sp)
            load(U_WO2 + 2 * RING, N_UNITS)
            for k in range(KC):
                sp.wait_ge(n_final.scaled, k + 1)
                sp.dma_start(out_t[:, k, :], Y2[:, k, :]).then_inc(out_done, 16)
            sp.wait_ge(out_done, 16 * KC)

        @block.gpsimd
        def _(pool):
            pool.memset(ones[:, :], 1.0 / D).then_inc(const_done, 1)
            pool.memset(ident[:, :], 0.0).then_inc(const_done, 1)
            pool.memset(epsc[:, :], EPS).then_inc(const_done, 1)
            pool.memset(strip[:, N_DIFF, 0:P], 0.0).then_inc(const_done, 1)
            pool.wait_ge(const_done, 4)
            pool.affine_select(out=ident[:, :], in_=ident[:, :], compare_op=ALU.not_equal, fill=1.0, base=0,
                               pattern=[[-1, P]], channel_multiplier=1).then_inc(const_done, 1)
            pool.affine_select(out=strip[:, N_DIFF, 0:P], in_=strip[:, N_DIFF, 0:P], compare_op=ALU.is_gt, fill=MASKED,
                               base=0, pattern=[[-1, P]], channel_multiplier=1).then_inc(const_done, 1)
            pool.wait_ge(const_done, 6)
            pool.tensor_copy(ident_r[:, :], ident[:, :]).then_inc(const_done, 1)
            pool.tensor_copy(mask_r[:, :], strip[:, N_DIFF, 0:P]).then_inc(const_done, 1)

            def rest(u_of, slot):
                pool.wait_ge(hi_done, u_of)
                pool.tensor_tensor(w_lo[:, slot, :], stage[:, slot, :], w_hi[:, slot, :].bitcast(F32),
                                   ALU.subtract).then_inc(lo_done, 1)

            def run(u0, u1):
                rounds = (u1 - u0) // RING
                if rounds > 1:
                    with pool.Fori(0, rounds) as r:
                        for i in range(RING):
                            rest(r * RING + (u0 + i + 1), (u0 + i) % RING)
                    u0 += rounds * RING
                for u in range(u0, u1):
                    rest(u + 1, u % RING)

            run(0, 2)
            pool_sum(pool, n_attn_pre)
            run(2, U_WO + RING - 1)
            at1.preps[1].move(pool)
            run(U_WO + RING - 1, U_WO + RING)
            pool_heads(pool)
            pool_sum(pool, n_attn_post, lambda k: rest(U_WO + RING + k + 1, (U_WO + RING + k) % RING))
            pool_post(pool, n_attn_post)
            pool_sum(pool, n_ffn_pre)
            run(U_UP1 + RING, U_UP2 + RING - 1)
            pool_post(pool, n_ffn_post)
            pool_sum(pool, n_ffn1)
            run(U_UP2 + RING - 1, U_MIX + RING - 1)
            pool_sum(pool, n_mix)
            run(U_MIX + RING - 1, U_MIX + RING)
            di, ci = L0[:, 0, :].bitcast(I32), L0[:, 1, 0:P].bitcast(I32)
            dist, cd = L1[:, 0, :], L1[:, 1, 0:P]
            pool.iota(di, pattern=[[-1, T]], base=3 * P, channel_multiplier=1).then_inc(const_done, 1)
            pool.iota(ci.rearrange("p (i c) -> p i c", i=4),
                      pattern=[[P, 4], [-CMP_STRIDE, 32]], base=-(CMP_BLOCK - 1), channel_multiplier=1).then_inc(const_done, 1)
            pool.wait_ge(const_done, 10)
            pool.tensor_copy(dist, di).then_inc(const_done, 1)
            pool.tensor_copy(cd, ci).then_inc(const_done, 1)
            pool.wait_ge(const_done, 12)
            pool.affine_select(out=WT[:, 1, 0:256], in_=dist[:, 256:512], compare_op=ALU.is_ge, fill=FAR,
                               base=P, pattern=[[-1, 256]], channel_multiplier=1).then_inc(const_done, 1)
            pool.wait_ge(const_done, 13)
            pool.affine_select(out=WT[:, 1, 0:256], in_=WT[:, 1, 0:256], compare_op=ALU.is_gt, fill=FAR,
                               base=0, pattern=[[1, 256]], channel_multiplier=-1).then_inc(const_done, 1)
            pool.affine_select(out=dist, in_=dist, compare_op=ALU.is_ge, fill=FAR,
                               base=3 * P, pattern=[[-1, T]], channel_multiplier=1).then_inc(const_done, 1)
            pool.affine_select(out=cd.rearrange("p (i c) -> p i c", i=4),
                               in_=cd.rearrange("p (i c) -> p i c", i=4), compare_op=ALU.is_ge, fill=FAR,
                               base=-(CMP_BLOCK - 1), pattern=[[P, 4], [-CMP_STRIDE, 32]], channel_multiplier=1).then_inc(const_done, 1)
            run(U_MIX + RING, U_CMP + RING - 1)
            kw_.move(pool)
            run(U_CMP + RING - 1, U_UP3 + RING)
            pool_sum(pool, n_ffn2)
            run(U_UP3 + RING, N_UNITS)
            pool_sum(pool, n_final, upto=POOL_ADDS)

        @block.scalar
        def _(act):
            count = [0]

            def link(ins):
                ins.then_inc(act_self, 1)
                count[0] += 1
                return count[0]

            def after(c):
                act.wait_ge(act_self, c)

            for u in range(2):
                act_hi(act, u, None, 16, wait_free=False)
            act.wait_ge(par_loaded, 16)

            def others():
                for u in range(2, RING):
                    act_hi(act, u, None, 16, wait_free=False)
            act_fold(act, n_attn_pre, others)
            act.wait_ge(lam_e, 2)
            act.activation(small[:, 4:6], small[:, 2:4], ACT.Exp).then_inc(lam_e, 1)
            with act.Fori(0, 4) as r:
                for i in range(4):
                    v = U_QKV + i + RING
                    act_hi(act, v % RING, r * 4 + v, r * 16 + 16 * (v // RING + 1))
            act.wait_ge(rcol_done, 1)
            for g in range(2):
                for t in range(4 - g):
                    act_hi_static(act, U_QKV + 16 + 4 * g + t)
                if g == 1:
                    act.wait_ge(unit_done, U_QKV + 24)
                    act.wait_ge(qk_evac[0], 4 + 16)
                    for q in at1.preps[0:2]:
                        q.act_split(act)
                    at1.preps[0].move(act, ("hi",))
                    act_hi_static(act, U_QKV + 23)
                for tb in range(TB):
                    act.activation(V[:, g, tb, :], PS[:, (4 if g == 0 else 0) + tb, :], ACT.Copy,
                                   scale=rcol[:, tb:tb + 1]).then_inc(v_ready[0], 1)
            act.preload_act_table_set("natural_log_exp_and_others")
            act_attn(act, at1, link, after)
            act_head(7)(act)
            act_turn(act, 0)
            for j in range(KC):
                act.wait_ge(unit_done, U_WO + j + 1)
                act.activation(QK[:, j, :], PS[:, j, :], ACT.Copy).then_inc(n_attn_post.ready, 1)
                act_square(act, n_attn_post, j)
                act_hi_static(act, U_WO + j)
            act_inverse(act, n_attn_post)
            act_fold(act, n_ffn_pre)
            act_ffn(act, 0, U_UP1, U_DN1, True)
            for k in range(KC):
                if k % 2 == 0:
                    act.wait_ge(y_done[0], k + 1)
                    act.activation(Y2[:, k, :], PS[:, k, :], ACT.Copy).then_inc(n_ffn_post.ready, 1)
                else:
                    act.wait_ge(y_odd, k // 2 + 1)
                act_square(act, n_ffn_post, k, k // 2 + 1)
            act_inverse(act, n_ffn_post)
            act_hi_static(act, U_DN1 + FC - 1)
            act_fold(act, n_ffn1)
            act_ffn(act, 1, U_UP2, U_DN2, False)
            act_fold(act, n_mix, lambda: act_hi_static(act, U_DN2 + FC - 1))
            with act.Fori(0, 3) as r:
                for i in range(4):
                    v = U_MIX + i + RING
                    act_hi(act, v % RING, r * 4 + v, r * 16 + 16 * (v // RING + 1))
            act_hi_static(act, U_MIX + 12)
            for t in range(3):
                act_hi_static(act, U_MIX + 13 + t)
            act.wait_ge(unit_done, U_MIX + 17)
            act.wait_ge(qk_evac[1], 4 + 13)
            for q in (ks_, kw_, q0):
                q.act_split(act)
            q0.move(act, ("hi",))
            act_hi_static(act, U_MIX + 16)
            act.wait_ge(rcol_done, 2)
            for tb in range(TB):
                act.activation(V[:, 0, tb, 0:NAT2], PS[:, 4 + tb, 0:NAT2], ACT.Copy,
                               scale=rcol[:, tb:tb + 1]).then_inc(v_ready[1], 1)
            act.wait_ge(v_ready[1], TB)
            act.preload_act_table_set("natural_log_exp_and_others")
            act.activation(gates[:, :, :], V[:, 0, :, 3 * P:NAT2], ACT.Exp, scale=-1.0).then_inc(gate_e, 1)
            act_attn(act, at2, link, after)
            act_turn(act, 1)
            for j in range(KC):
                act_hi_static(act, U_WO2 + j)
            act_fold(act, n_ffn2)
            act_ffn(act, 2, U_UP3, U_DN3, False)
            for k in range(KC):
                n_final.wait_ready(act, k)
                act_square(act, n_final, k)
            act_inverse(act, n_final)

        @block.tensor
        def _(pe):
            pe.sem_inc(ffn_free, 2)
            pe.sem_inc(qk_evac[0], 4)
            pe.sem_inc(qk_evac[1], 4)
            pe.wait_ge(const_done, 8)
            pe_first_pair(pe, n_attn_pre, U_QKV)
            pe_stat(pe, n_attn_pre)
            for i in range(2, 4):
                pe.wait_ge(lo_done, U_QKV + i + 1)
                pe_chunk(pe, (U_QKV + i) % RING, i)
            pe_rcol(pe, n_attn_pre)
            with pe.Fori(1, 4) as r:
                for i in range(4):
                    pe.wait_ge(lo_done, r * 4 + (U_QKV + i + 1))
                    pe.wait_ge(qk_evac[0], r * 4 + (i + 1))
                    pe_chunk(pe, (U_QKV + i) % RING, i)
            pe.wait_ge(rcol_done, 1)
            pe_by_token(pe, U_QKV + 16, 4, T)
            pe.wait_ge(qk_evac[0], 20)
            pe_by_token(pe, U_QKV + 20, 0, T)
            pe.wait_ge(v_ready[0], 2 * TB)
            pe_attn(pe, at1)
            pe.wait_ge(at1.o_done, len(items1))
            pe_turn(pe, 0)
            pe_wo(pe, 0, U_WO)
            pe_stat(pe, n_attn_post)
            pe_ffn(pe, 0, U_UP1, U_DN1, n_ffn_pre)
            pe_stat(pe, n_ffn_post)
            pe_ffn(pe, 1, U_UP2, U_DN2, n_ffn1)
            pe_first_pair(pe, n_mix, U_MIX)
            pe_stat(pe, n_mix)
            for i in range(2, 4):
                pe.wait_ge(lo_done, U_MIX + i + 1)
                pe_chunk(pe, (U_MIX + i) % RING, i)
            pe_rcol(pe, n_mix)
            with pe.Fori(1, 3) as r:
                for i in range(4):
                    pe.wait_ge(lo_done, r * 4 + (U_MIX + i + 1))
                    pe.wait_ge(qk_evac[1], r * 4 + (i + 1))
                    pe_chunk(pe, (U_MIX + i) % RING, i)
            pe.wait_ge(lo_done, U_MIX + 13)
            pe.wait_ge(qk_evac[1], 13)
            pe_chunk(pe, (U_MIX + 12) % RING, 0)
            pe.wait_ge(rcol_done, 2)
            pe_by_token(pe, U_MIX + 13, 4, NAT2)
            pe.wait_ge(v_ready[1], TB)
            pe_attn(pe, at2)
            pe.wait_ge(at2.o_done, len(items2))
            pe_turn(pe, 1)
            pe_wo(pe, 1, U_WO2)
            pe_ffn(pe, 2, U_UP3, U_DN3, n_ffn2)
            pe_stat(pe, n_final)

        @block.vector
        def _(dve):
            count = [0]

            def link(ins):
                ins.then_inc(dve_self, 1)
                count[0] += 1
                return count[0]

            def after(c):
                dve.wait_ge(dve_self, c)

            dve.wait_ge(row_loaded, 16)
            for m in range(2):
                a = row[:, ROW_LAM + 2 * m * HD:ROW_LAM + (2 * m + 1) * HD]
                b = row[:, ROW_LAM + (2 * m + 1) * HD:ROW_LAM + (2 * m + 2) * HD]
                dve.tensor_tensor_reduce(out=tmp[:, 0, m * HD:(m + 1) * HD], in0=a, in1=b, scale=1.0, scalar=0.0, op0=ALU.mult,
                                         op1=ALU.add, accum_out=small[:, 2 + m:3 + m]).then_inc(lam_e, 1)
            dve.wait_ge(tab_loaded, 16)
            for b, lo, hi in bucket_runs():
                c = link(dve.tensor_copy(line[:, T - 1 - hi:T - lo],
                                         tab[:, b:b + 1].to_broadcast([N_DIFF, hi - lo + 1])))
            c = link(dve.memset(line[:, T:LINE], MASKED))
            after(c)
            dve.sem_inc(strips_done[0], 1)
            dve.wait_ge(par_loaded, 16)
            gain = row[:, ROW_SUB:ROW_SUB + P]
            dve.tensor_scalar(gain, gain, 1.0 - LAM_INIT, None, ALU.mult).then_inc(gain_ready, 1)
            dve_fold(dve, n_attn_pre)

            def evacuate(b, bank, chunk, scale, unit_wait):
                dve.wait_ge(unit_done, unit_wait)
                if scale != 1.0:
                    x = dve.scalar_tensor_tensor(out=chunk, in0=PS[:, bank, :], scalar=scale, in1=rstd[:, :],
                                                 op0=ALU.mult, op1=ALU.mult)
                else:
                    x = dve.tensor_tensor(chunk, PS[:, bank, :], rstd[:, :], ALU.mult)
                x.then_inc(qk_evac[b], 1)

            def projections(b, u0, rounds, scale):
                for i in range(4):
                    evacuate(b, i, QK[:, i, :], scale(i), u0 + i + 1)
                dve_rcol(dve, b)
                with dve.Fori(1, rounds) as r:
                    for i in range(4):
                        evacuate(b, i, QK[:, bass.ds(r * 4 + i, 1), :].rearrange("p a n -> p (a n)"), scale(i),
                                 r * 4 + (u0 + i + 1))

            projections(0, U_QKV, 4, lambda i: SCALE if i % 2 == 0 else 1.0)
            dve.wait_ge(lam_e, 3)
            after(link(dve.tensor_tensor(small[:, 0:1], small[:, 5:6], small[:, 4:5], ALU.subtract)))
            after(link(dve.tensor_scalar(small[:, 0:1], small[:, 0:1], LAM_INIT, None, ALU.subtract)))
            dve.wait_ge(strips_done[0], 17)
            dve.wait_ge(const_done, 8)
            for q in at1.preps[0:2]:
                q.dve_split(dve)
            dve_attn(dve, at1, link, after)
            dve_head(7)(dve)
            dve_turn(dve, 0)
            dve_post(dve, n_attn_post)
            dve_fold(dve, n_ffn_pre)
            dve_ffn(dve, 0, U_UP1, True)
            n = n_ffn_post
            for k in range(KC + 1):
                if k % 2 and k < KC:
                    dve.wait_ge(y_done[0], k + 1)
                    dve.tensor_copy(Y2[:, k, :], PS[:, k, :]).then_inc(y_odd, 1)
                if k >= 2:
                    dve.wait_ge(n.squared, k)
                    if k >= 3:
                        dve.wait_ge(n.added, k - 2)
                    dve.tensor_tensor(rstd[:, :], sq[:, 0, :] if k == 2 else rstd[:, :], sq[:, (k - 1) % 2, :],
                                      ALU.add).then_inc(n.added, 1)
            dve_post(dve, n_ffn_post)
            dve_fold(dve, n_ffn1)
            dve_ffn(dve, 1, U_UP2, False)

            def residual(inst, norm):
                for k in range(KC):
                    dve.wait_ge(y_done[inst], k + 1)
                    dve.scalar_tensor_tensor(out=X[:, k, :], in0=PS[:, k, :], scalar=0.5, in1=X[:, k, :],
                                             op0=ALU.mult, op1=ALU.add).then_inc(norm.ready, 1)
            residual(1, n_mix)
            dve_fold(dve, n_mix)
            projections(1, U_MIX, 3, lambda i: 1.0)
            evacuate(1, 0, QK[:, 12, :], 1.0, U_MIX + 13)
            dve.wait_ge(const_done, 16)
            for h in range(N_NSA):
                f = -2.0 ** (-8.0 * (h + 1) / N_NSA) / SCALE
                link(dve.tensor_scalar(strip[:, h, :], L1[:, 0, :], f, None, ALU.mult))
                c = link(dve.tensor_scalar(swa_strip(h), WT[:, 1, 0:256], f, None, ALU.mult))
            c = link(dve.tensor_copy(cdist[:, :], L1[:, 1, 0:P]))
            after(c)
            for q in (ks_, kw_, q0):
                q.dve_split(dve)
            dve.wait_ge(gate_e, 1)
            after(link(dve.tensor_scalar(gates[:, :, :], gates[:, :, :], 1.0, None, ALU.add)))
            after(link(dve.reciprocal(gates[:, :, :], gates[:, :, :])))
            dve_attn(dve, at2, link, after)
            dve.sem_inc(o_ready[1], 8)
            dve_turn(dve, 1)
            for j in range(KC):
                dve.wait_ge(unit_done, U_WO2 + j + 1)
                dve.tensor_tensor(X[:, j, :], X[:, j, :], PS[:, j, :], ALU.add).then_inc(n_ffn2.ready, 1)
            dve_fold(dve, n_ffn2)
            dve_ffn(dve, 2, U_UP3, False)
            residual(2, n_final)
            for k in range(POOL_ADDS, KC):
                dve.wait_ge(n_final.squared, k + 1)
                dve.wait_ge(n_final.added, k - 1)
                dve.tensor_tensor(rstd[:, :], rstd[:, :], sq[:, k % 2, :], ALU.add).then_inc(n_final.added, 1)
            dve.wait_ge(norm_inverse, n_final.at)
            for k in range(KC):
                dve.scalar_tensor_tensor(out=Y2[:, k, :], in0=X[:, k, :], scalar=pc("final", k),
                                         in1=rstd[:, :], op0=ALU.mult, op1=ALU.mult).then_inc(n_final.scaled, 1)


def kernel(**inp):
    import concourse.bacc as bacc
    from concourse.bass_utils import run_bass_kernel_spmd

    f32 = np.float32

    def chunks(w):
        w = w.reshape(KC, P, -1, P)
        return w.transpose(2, 1, 0, 3).reshape(-1, P, UNIT)

    def by_token(w):
        wide = np.zeros((D, T), f32)
        wide[:, :w.shape[1]] = w
        return wide.reshape(4, 2, P, T).transpose(0, 2, 1, 3).reshape(4, P, UNIT)

    def up(w):
        w = w.reshape(D, 2, FC, P).transpose(0, 2, 1, 3).reshape(D, 2 * FF)
        return chunks(w)

    def pairs(w):
        return w.reshape(D, 2, 4, HD).transpose(0, 2, 1, 3).reshape(D, 8 * HD)

    def cmp1(w):
        return w.reshape(4, 4, P, CMP_HID).transpose(0, 2, 1, 3).reshape(4, P, UNIT)

    w = np.asarray(inp["w_qkv"][0])
    dq, dk, dv, sq_, sk, sv = np.split(w, 6, axis=1)
    qk = np.stack([a.reshape(D, 4, P) for a in (dq, dk, sq_, sk)], axis=2).reshape(D, 16 * P)
    m = np.asarray(inp["w_mix_in_2"][0])
    qa, kva, ga, qb, kvb = np.split(m, np.cumsum([512, 768, 24, 512]).tolist(), axis=1)
    kc, vcr, ks, vs, kw, vw = np.split(kva, 6, axis=1)
    kb, vb = np.split(kvb, 2, axis=1)
    mix_t = np.concatenate([pairs(qa), ks, kw, kc, vcr, pairs(qb), kb], axis=1)
    mix_n = np.concatenate([vs, vw, vb, ga], axis=1)
    weights = np.concatenate([
        chunks(qk), by_token(dv), by_token(sv), chunks(np.asarray(inp["w_o"][0])),
        up(np.asarray(inp["w_up"][0])), np.asarray(inp["w_down"][0]).reshape(FC, P, UNIT),
        up(np.asarray(inp["ffn1_w_in_2"][0])), np.asarray(inp["ffn1_w_out_2"][0]).reshape(FC, P, UNIT),
        chunks(mix_t), by_token(mix_n),
        cmp1(np.asarray(inp["cmp_k_w1_2"][0])), cmp1(np.asarray(inp["cmp_v_w1_2"][0])),
        chunks(np.asarray(inp["w_mix_out_2"][0])),
        up(np.asarray(inp["ffn2_w_in_2"][0])), np.asarray(inp["ffn2_w_out_2"][0]).reshape(FC, P, UNIT)], axis=0)
    assert weights.shape[0] == N_UNITS

    def cols(v):
        return np.asarray(v).reshape(-1, P).T

    params = np.concatenate(
        [cols(inp[n]) for n in ("attn_pre_norm", "attn_post_norm", "ffn_pre_norm", "ffn_post_norm",
                                "ffn1_norm_2", "mix_norm_2", "ffn2_norm_2", "final_norm_2", "conv_w", "conv_b",
                                "cmp_k_pos_2", "cmp_v_pos_2", "cmp_k_b1_2", "cmp_v_b1_2")]
        + [np.asarray(inp[n][0]).reshape(2, P, HD).transpose(1, 0, 2).reshape(P, 2 * HD)
           for n in ("cmp_k_w2_2", "cmp_v_w2_2")], axis=1)
    assert params.shape == (P, N_PARAMS)
    rows = np.concatenate([np.asarray(inp[n]).reshape(-1) for n in (
        "lambda_q1", "lambda_k1", "lambda_q2", "lambda_k2", "diff_subln", "sb_norm", "swa_sinks_2")])[None]
    x_t = np.asarray(inp["x"])[0].T.reshape(KC, P, T).transpose(1, 0, 2)
    arrays = {"weights": weights, "x_t": x_t, "params": params, "rows": rows, "table_t": np.asarray(inp["rel_bias"]).T}
    nc = bacc.Bacc("TRN2", target_bir_lowering=False, num_devices=1)
    args, given = [], {}
    for name, a in arrays.items():
        given["in_" + name] = np.ascontiguousarray(a)
        args.append(nc.dram_tensor("in_" + name, a.shape, F32, kind="ExternalInput").ap())
    args.append(nc.dram_tensor("bias_line", (N_DIFF, P, LINE + 1), F32, kind="Internal").ap())
    args.append(nc.dram_tensor("out_t", (P, KC, T), F32, kind="ExternalOutput").ap())
    build(nc, *args)
    r = run_bass_kernel_spmd(nc, [given], core_ids=[0])
    out = r.results[0]["out_t"]
    return np.ascontiguousarray(out.transpose(2, 1, 0).reshape(1, T, D))
```
